# Optimizing a Trainium2 kernel written in Bass

```python
import math
import jax
import jax.numpy as jnp
from jax import lax
import numpy as np
import jax, jax.numpy as jnp

D_MODEL = 1024
BATCH = 1
SEQ = 256
DEPTH = 2

GRID_W = 64
CTX_LEN = 256
N_MIXERS = 2
N_DN_LAYERS = (DEPTH + N_MIXERS - 1) // N_MIXERS
N_DA_LAYERS = DEPTH // N_MIXERS

DN_HEADS = 8
DN_DK = 128
DN_DV = 128
DN_CONV = 5
DN_CHUNK = 64

DA_HEADS = 8
DA_DIM = 64
DA_QBLOCK = 128
ROPE_BASE = 10000.0

FFN_HIDDEN = -(-(8 * D_MODEL) // (3 * 256)) * 256

DEEPNORM_ALPHA = (2.0 * DEPTH) ** 0.25
DEEPNORM_BETA = (8.0 * DEPTH) ** -0.25
LN_EPS = 1e-5
RMS_EPS = 1e-6


def _layernorm(x, g, b):
    xf = x.astype(jnp.float32)
    mu = jnp.mean(xf, axis=-1, keepdims=True)
    var = jnp.mean(jnp.square(xf - mu), axis=-1, keepdims=True)
    return ((xf - mu) * lax.rsqrt(var + LN_EPS)).astype(x.dtype) * g + b

def _rmsnorm(x, g):
    xf = x.astype(jnp.float32)
    y = xf * lax.rsqrt(jnp.mean(jnp.square(xf), axis=-1, keepdims=True) + RMS_EPS)
    return y.astype(x.dtype) * g

def _l2norm(x):
    xf = x.astype(jnp.float32)
    return xf * lax.rsqrt(jnp.sum(jnp.square(xf), axis=-1, keepdims=True) + RMS_EPS)

def _swiglu(h, w_gate, w_up, w_down):
    return (jax.nn.silu(h @ w_gate) * (h @ w_up)) @ w_down

def _centred_dwconv(x, w):
    pad = (DN_CONV - 1) // 2
    return lax.conv_general_dilated(
        x, w[:, None, :].astype(x.dtype), window_strides=(1,), padding=[(pad, pad)],
        dimension_numbers=('NWC', 'WIO', 'NWC'), feature_group_count=x.shape[-1])

def _axial_rope(rows, dtype):
    quarter = DA_DIM // 4
    inv_freq = ROPE_BASE ** (-jnp.arange(quarter, dtype=jnp.float32) / quarter)
    row = jnp.repeat(jnp.arange(rows, dtype=jnp.float32), GRID_W)
    col = jnp.tile(jnp.arange(GRID_W, dtype=jnp.float32), rows)
    ang_r = row[:, None] * inv_freq
    ang_c = col[:, None] * inv_freq
    ang = jnp.concatenate([ang_r, ang_r, ang_c, ang_c], axis=-1)
    return jnp.cos(ang).astype(dtype), jnp.sin(ang).astype(dtype)

def _apply_rope(x, cos, sin):
    quarter = DA_DIM // 4
    half = DA_DIM // 2

    def rot_half(u):
        return jnp.concatenate([-u[..., quarter:], u[..., :quarter]], axis=-1)

    x_rot = jnp.concatenate([rot_half(x[..., :half]), rot_half(x[..., half:])], axis=-1)
    return x * cos + x_rot * sin

def _flip_seq(t, direction):
    return jnp.flip(t, axis=2) if direction == 1 else t

def _chunked_gated_delta(q, k, v, g, beta, s0):
    bsz, nh, L, _ = q.shape
    dv = v.shape[-1]
    nc = L // DN_CHUNK

    def blocks(t):
        return t.reshape(bsz, nh, nc, DN_CHUNK, *t.shape[3:])

    q, k, v, g, beta = (blocks(t) for t in (q, k, v.astype(jnp.float32), g, beta))
    G = jnp.cumsum(g, axis=-1)
    idx = jnp.arange(DN_CHUNK)
    incl = idx[:, None] >= idx[None, :]
    strict = idx[:, None] > idx[None, :]
    gamma = jnp.exp(jnp.where(incl, G[..., :, None] - G[..., None, :], -jnp.inf))
    kb = k * beta[..., None]
    a_low = jnp.where(strict, jnp.einsum('bhnid,bhnjd->bhnij', kb, k) * gamma, 0.0)
    eye = jnp.eye(DN_CHUNK, dtype=jnp.float32)
    rhs = jnp.concatenate([v * beta[..., None], kb * jnp.exp(G)[..., None]], axis=-1)
    uw = lax.linalg.triangular_solve(eye + a_low, rhs, left_side=True, lower=True, unit_diagonal=True)
    u, w = uw[..., :dv], uw[..., dv:]
    qk = jnp.einsum('bhnid,bhnjd->bhnij', q, k) * gamma
    g_last = G[..., -1]
    q_dec = q * jnp.exp(G)[..., None]
    k_dec = k * jnp.exp(g_last[..., None] - G)[..., None]

    def step(s, inp):
        u_n, w_n, qk_n, qd_n, kd_n, gl_n = inp
        v_new = u_n - jnp.einsum('bhck,bhkv->bhcv', w_n, s)
        o_n = jnp.einsum('bhck,bhkv->bhcv', qd_n, s) + jnp.einsum('bhij,bhjv->bhiv', qk_n, v_new)
        s = s * jnp.exp(gl_n)[..., None, None] + jnp.einsum('bhck,bhcv->bhkv', kd_n, v_new)
        return s, o_n

    xs = tuple(jnp.moveaxis(t, 2, 0) for t in (u, w, qk, q_dec, k_dec, g_last))
    s_final, o = lax.scan(step, s0, xs)
    o = jnp.moveaxis(o, 0, 2).reshape(bsz, nh, L, dv)
    return o, s_final

def _gated_deltanet(h_lat, h_ctx, w_in, conv_w, a_log, dt_bias, norm_g, w_out, need_ctx):
    f32 = jnp.float32
    hk = DN_HEADS * DN_DK
    hv = DN_HEADS * DN_DV
    n_qkv = 2 * hk + hv

    def project(h):
        bsz, L, _ = h.shape
        p = h @ w_in
        qkv = jax.nn.silu(_centred_dwconv(p[..., :n_qkv], conv_w))
        q = _l2norm(qkv[..., :hk].reshape(bsz, L, DN_HEADS, DN_DK)) * (DN_DK ** -0.5)
        k = _l2norm(qkv[..., hk:2 * hk].reshape(bsz, L, DN_HEADS, DN_DK))
        v = qkv[..., 2 * hk:].reshape(bsz, L, DN_HEADS, DN_DV).astype(f32)
        z = p[..., n_qkv:n_qkv + hv]
        off = n_qkv + hv
        a = p[..., off:off + 2 * DN_HEADS].reshape(bsz, L, 2, DN_HEADS).astype(f32)
        b = p[..., off + 2 * DN_HEADS:].reshape(bsz, L, 2, DN_HEADS).astype(f32)
        g = -jnp.exp(a_log.astype(f32)) * jax.nn.softplus(a + dt_bias.astype(f32))
        beta = jax.nn.sigmoid(b)
        heads = lambda t: jnp.transpose(t, (0, 2, 1, 3))
        dirs = lambda t: jnp.transpose(t, (2, 0, 3, 1))
        return heads(q), heads(k), heads(v), z, dirs(g), dirs(beta)

    qc, kc, vc, zc, gc, bc = project(h_ctx)
    ql, kl, vl, zl, gl, bl = project(h_lat)
    bsz = h_lat.shape[0]
    outs_lat, outs_ctx = [], []
    for d in range(2):
        s0 = jnp.zeros((bsz, DN_HEADS, DN_DK, DN_DV), f32)
        oc, s_ctx = _chunked_gated_delta(_flip_seq(qc, d), _flip_seq(kc, d), _flip_seq(vc, d),
                                         _flip_seq(gc[d], d), _flip_seq(bc[d], d), s0)
        ol, _ = _chunked_gated_delta(_flip_seq(ql, d), _flip_seq(kl, d), _flip_seq(vl, d),
                                     _flip_seq(gl[d], d), _flip_seq(bl[d], d), s_ctx)
        outs_ctx.append(_flip_seq(oc, d))
        outs_lat.append(_flip_seq(ol, d))

    def out(o, z):
        bsz_, _, L, _ = o.shape
        o = _rmsnorm(jnp.transpose(o, (0, 2, 1, 3)), norm_g.astype(f32))
        o = o.astype(z.dtype) * jax.nn.silu(z.reshape(bsz_, L, DN_HEADS, DN_DV))
        return o.reshape(bsz_, L, hv) @ w_out

    y_ctx = out(outs_ctx[0] + outs_ctx[1], zc) if need_ctx else None
    return out(outs_lat[0] + outs_lat[1], zl), y_ctx

def _diff_attention(h_lat, h_ctx, w_in, lam, subln_g, w_out, lambda_init, rope, need_ctx):
    f32 = jnp.float32
    hq = DA_HEADS * 2 * DA_DIM

    def project(h, use_rope):
        bsz, L, _ = h.shape
        p = h @ w_in
        q = p[..., :hq].reshape(bsz, L, DA_HEADS, 2, DA_DIM).transpose(3, 0, 2, 1, 4)
        k = p[..., hq:2 * hq].reshape(bsz, L, DA_HEADS, 2, DA_DIM).transpose(3, 0, 2, 1, 4)
        v = p[..., 2 * hq:].reshape(bsz, L, DA_HEADS, 2 * DA_DIM).transpose(0, 2, 1, 3)
        if use_rope:
            q = _apply_rope(q, rope[0], rope[1])
            k = _apply_rope(k, rope[0], rope[1])
        return q * (DA_DIM ** -0.5), k, v

    lam_f = lam.astype(f32)
    lam_val = (jnp.exp(jnp.sum(lam_f[0] * lam_f[1])) - jnp.exp(jnp.sum(lam_f[2] * lam_f[3]))
               + lambda_init)

    def attend(q, k, v):
        s = jnp.einsum('cbhqd,cbhkd->cbhqk', q, k).astype(f32)
        p = jax.nn.softmax(s, axis=-1)
        a = p[0] - lam_val * p[1]
        return jnp.einsum('bhqk,bhkv->bhqv', a, v.astype(f32))

    def out(o):
        bsz_, _, L, _ = o.shape
        o = _rmsnorm(jnp.transpose(o, (0, 2, 1, 3)), subln_g.astype(f32)) * (1.0 - lambda_init)
        return o.reshape(bsz_, L, hq).astype(h_lat.dtype) @ w_out

    qc, kc, vc = project(h_ctx, False)
    ql, kl, vl = project(h_lat, True)
    k_all = jnp.concatenate([kl, kc], axis=3)
    v_all = jnp.concatenate([vl, vc], axis=2)
    bsz, L = h_lat.shape[:2]
    nb = L // DA_QBLOCK
    qb = jnp.moveaxis(ql.reshape(2, bsz, DA_HEADS, nb, DA_QBLOCK, DA_DIM), 3, 0)
    ob = lax.map(lambda q_blk: attend(q_blk, k_all, v_all), qb)
    o_lat = jnp.moveaxis(ob, 0, 2).reshape(bsz, DA_HEADS, L, 2 * DA_DIM)
    y_ctx = out(attend(qc, kc, vc)) if need_ctx else None
    return out(o_lat), y_ctx

def first_inputs(seed: int = 0) -> dict:
    key = jax.random.key(seed)
    ks = iter(jax.random.split(key, 32))
    f32 = jnp.float32
    D = D_MODEL
    hk = DN_HEADS * DN_DK
    hv = DN_HEADS * DN_DV
    hq = DA_HEADS * 2 * DA_DIM

    def nrm(shape, scale):
        return jax.random.normal(next(ks), shape, f32) * scale

    inputs = {}
    inputs['x'] = nrm((BATCH, SEQ, D), 1.0)
    inputs['c'] = nrm((BATCH, D), 1.0)
    inputs['ctx'] = nrm((BATCH, CTX_LEN, D), 1.0)
    inputs['c_ctx'] = nrm((D,), 1.0)
    inputs['ada_w'] = nrm((DEPTH, D, 6 * D), D ** -0.5)
    inputs['ada_b'] = nrm((DEPTH, 6 * D), 0.01)
    inputs['ln1_g'] = 1.0 + nrm((DEPTH, D), 0.02)
    inputs['ln1_b'] = nrm((DEPTH, D), 0.02)
    inputs['ln2_g'] = 1.0 + nrm((DEPTH, D), 0.02)
    inputs['ln2_b'] = nrm((DEPTH, D), 0.02)
    inputs['ffn_w_gate'] = nrm((DEPTH, D, FFN_HIDDEN), D ** -0.5)
    inputs['ffn_w_up'] = nrm((DEPTH, D, FFN_HIDDEN), D ** -0.5)
    inputs['ffn_w_down'] = nrm((DEPTH, FFN_HIDDEN, D), FFN_HIDDEN ** -0.5 * DEEPNORM_BETA)
    inputs['dn_w_in'] = jnp.concatenate([
        nrm((N_DN_LAYERS, D, 2 * hk + 2 * hv), D ** -0.5),
        nrm((N_DN_LAYERS, D, 2 * DN_HEADS), 0.1 * D ** -0.5),
        nrm((N_DN_LAYERS, D, 2 * DN_HEADS), D ** -0.5),
    ], axis=-1)
    inputs['dn_conv'] = nrm((N_DN_LAYERS, DN_CONV, 2 * hk + hv), DN_CONV ** -0.5)
    inputs['dn_a_log'] = jnp.log(jax.random.uniform(next(ks), (N_DN_LAYERS, 2, DN_HEADS), f32, 1.0, 16.0))
    dt = jnp.exp(jax.random.uniform(next(ks), (N_DN_LAYERS, 2, DN_HEADS), f32,
                                    math.log(1e-3), math.log(1e-1)))
    inputs['dn_dt_bias'] = dt + jnp.log(-jnp.expm1(-dt))
    inputs['dn_norm_g'] = 1.0 + nrm((N_DN_LAYERS, DN_DV), 0.02)
    inputs['dn_w_out'] = nrm((N_DN_LAYERS, hv, D), hv ** -0.5 * DEEPNORM_BETA)
    inputs['da_w_in'] = nrm((N_DA_LAYERS, D, 3 * hq), D ** -0.5)
    inputs['da_lambda'] = nrm((N_DA_LAYERS, 4, DA_DIM), 0.1)
    inputs['da_subln_g'] = 1.0 + nrm((N_DA_LAYERS, 2 * DA_DIM), 0.02)
    inputs['da_w_out'] = nrm((N_DA_LAYERS, hq, D), hq ** -0.5 * DEEPNORM_BETA)
    return inputs

def first_block(x, c, ctx, c_ctx, ada_w, ada_b, ln1_g, ln1_b, ln2_g, ln2_b,
              ffn_w_gate, ffn_w_up, ffn_w_down,
              dn_w_in, dn_conv, dn_a_log, dn_dt_bias, dn_norm_g, dn_w_out,
              da_w_in, da_lambda, da_subln_g, da_w_out):
    L = x.shape[1]
    rows = L // GRID_W
    rope = _axial_rope(rows, x.dtype)
    s_lat = jax.nn.silu(c)
    s_ctx = jax.nn.silu(c_ctx)
    for i in range(DEPTH):
        last = i == DEPTH - 1
        sh1, sc1, gt1, sh2, sc2, gt2 = jnp.split((s_lat @ ada_w[i] + ada_b[i])[:, None, :], 6, axis=-1)
        sh1c, sc1c, gt1c, sh2c, sc2c, gt2c = jnp.split(s_ctx @ ada_w[i] + ada_b[i], 6, axis=-1)
        h = x * (1.0 + sc1) + sh1
        hc = ctx * (1.0 + sc1c) + sh1c
        j = i // N_MIXERS
        if i % N_MIXERS == 0:
            y, yc = _gated_deltanet(h, hc, dn_w_in[j], dn_conv[j], dn_a_log[j], dn_dt_bias[j],
                                    dn_norm_g[j], dn_w_out[j], not last)
        else:
            y, yc = _diff_attention(h, hc, da_w_in[j], da_lambda[j], da_subln_g[j], da_w_out[j],
                                    0.8 - 0.6 * math.exp(-0.3 * i), rope, not last)
        x = _layernorm(DEEPNORM_ALPHA * x + gt1 * y, ln1_g[i], ln1_b[i])
        x = _layernorm(DEEPNORM_ALPHA * x
                       + gt2 * _swiglu(x * (1.0 + sc2) + sh2, ffn_w_gate[i], ffn_w_up[i], ffn_w_down[i]),
                       ln2_g[i], ln2_b[i])
        if not last:
            ctx = _layernorm(DEEPNORM_ALPHA * ctx + gt1c * yc, ln1_g[i], ln1_b[i])
            ctx = _layernorm(DEEPNORM_ALPHA * ctx
                             + gt2c * _swiglu(ctx * (1.0 + sc2c) + sh2c, ffn_w_gate[i], ffn_w_up[i], ffn_w_down[i]),
                             ln2_g[i], ln2_b[i])
    return x


HEAD_DIM = 64
GROUP_WIDTH = D_MODEL // 2
GROUP_HEADS = GROUP_WIDTH // HEAD_DIM
RW_HEADS = GROUP_HEADS
RW_DIM = GROUP_WIDTH
DECAY_LORA = 64
AAA_LORA = 64
GATE_LORA = 128
RW_GN_EPS = 64e-5
MLA_HEADS = GROUP_HEADS
MLA_NOPE = HEAD_DIM
MLA_ROPE = HEAD_DIM // 2
MLA_V = HEAD_DIM
MLA_Q_RANK = D_MODEL // 4
MLA_KV_RANK = D_MODEL // 8
FOX_HEADS = GROUP_HEADS
FOX_DIM = GROUP_WIDTH
MOBA_HEADS = GROUP_HEADS
MOBA_DIM = GROUP_WIDTH
MOBA_BLOCK = 256
MOBA_TOPK = 3
MOBA_Q_CHUNK = 32
Q_BLOCK = 128
ROPE_THETA = 10000.0
NORM_EPS = 1e-6
D_FF = 256 * ((8 * D_MODEL // 3 + 255) // 256)
N_EXPERTS = 8
TOP_K = 2
D_EXPERT = 7 * D_MODEL // 2

RW_SIZES = (RW_DIM, RW_DIM, RW_DIM, DECAY_LORA, AAA_LORA, GATE_LORA)
RW_COLS = sum(RW_SIZES)
MLA_SIZES = (MLA_Q_RANK, MLA_KV_RANK, MLA_ROPE)
IN0_COLS = RW_COLS + sum(MLA_SIZES)
FOX_SIZES = (FOX_DIM, FOX_DIM, FOX_DIM, FOX_HEADS)
FOX_COLS = sum(FOX_SIZES)
MOBA_SIZES = (MOBA_DIM, MOBA_DIM, MOBA_DIM)
IN1_COLS = FOX_COLS + sum(MOBA_SIZES)
MIX0_OUT = RW_DIM + MLA_HEADS * MLA_V
MIX1_OUT = FOX_DIM + MOBA_DIM


def split_cols(t, sizes):
    return jnp.split(t, [int(i) for i in np.cumsum(sizes)[:-1]], axis=-1)

def to_heads(t, n_heads):
    b, s, _ = t.shape
    return t.reshape(b, s, n_heads, -1)

def rmsnorm(x, g, eps=NORM_EPS):
    xf = x.astype(jnp.float32)
    xf = xf * lax.rsqrt(jnp.mean(xf * xf, axis=-1, keepdims=True) + eps)
    return (xf * g.astype(jnp.float32)).astype(x.dtype)

def rope_tables(seq_len, dim):
    inv_freq = ROPE_THETA ** (-jnp.arange(0, dim, 2, dtype=jnp.float32) / dim)
    ang = jnp.arange(seq_len, dtype=jnp.float32)[:, None] * inv_freq[None, :]
    return jnp.cos(ang), jnp.sin(ang)

def apply_rope(x, cos_r, sin_r):
    xf = x.astype(jnp.float32)
    x1, x2 = jnp.split(xf, 2, axis=-1)
    c, s = cos_r[:, None, :], sin_r[:, None, :]
    return jnp.concatenate([x1 * c - x2 * s, x2 * c + x1 * s], axis=-1).astype(x.dtype)

def swiglu(t, w_gate, w_up, w_down):
    return (jax.nn.silu(t @ w_gate) * (t @ w_up)) @ w_down

def block_causal_attention(q, k, v, scale, log_decay_cum=None):
    b, h, s, _ = q.shape
    k_pos = jnp.arange(s)

    def one_block(i):
        start = i * Q_BLOCK
        qb = lax.dynamic_slice_in_dim(q, start, Q_BLOCK, axis=2)
        logits = jnp.einsum('bhqd,bhkd->bhqk', qb, k).astype(jnp.float32) * scale
        q_pos = start + jnp.arange(Q_BLOCK)
        if log_decay_cum is not None:
            dq = lax.dynamic_slice_in_dim(log_decay_cum, start, Q_BLOCK, axis=2)
            logits = logits + dq[..., :, None] - log_decay_cum[..., None, :]
        logits = jnp.where(k_pos[None, :] <= q_pos[:, None], logits, -jnp.inf)
        p = jax.nn.softmax(logits, axis=-1).astype(v.dtype)
        return jnp.einsum('bhqk,bhkd->bhqd', p, v)

    out = lax.map(one_block, jnp.arange(s // Q_BLOCK))
    return out.transpose(1, 2, 0, 3, 4).reshape(b, h, s, -1)

def rwkv7_time_mix(r, k, v, w_down, a_down, g_down, w0, w2, a0, a2, g2,
                   k_k, k_a, r_k, lnx_g, lnx_b):
    out_dtype = r.dtype
    f32 = jnp.float32
    r, k, v, w_down, a_down, g_down = (t.astype(f32) for t in (r, k, v, w_down, a_down, g_down))
    b, s, c = r.shape
    h, n = RW_HEADS, HEAD_DIM
    log_w = -jax.nn.softplus(-(w0 + jnp.tanh(w_down) @ w2)) - 0.5
    decay = jnp.exp(-jnp.exp(log_w))
    a = jax.nn.sigmoid(a0 + a_down @ a2)
    g = jax.nn.sigmoid(g_down) @ g2
    kk = (k * k_k).reshape(b, s, h, n)
    kk = kk / jnp.maximum(jnp.linalg.norm(kk, axis=-1, keepdims=True), 1e-12)
    k = k * (1.0 + (a - 1.0) * k_a)
    r_h, w_h, k_h, v_h, a_h = (t.reshape(b, s, h, n) for t in (r, decay, k, v, a))
    b_h = kk * a_h
    xs = tuple(jnp.moveaxis(t, 1, 0) for t in (r_h, w_h, k_h, v_h, kk, b_h))

    def step(state, inp):
        r_t, w_t, k_t, v_t, kk_t, b_t = inp
        sa = jnp.einsum('bhvk,bhk->bhv', state, -kk_t)
        state = (state * w_t[:, :, None, :] + sa[..., None] * b_t[:, :, None, :]
                 + v_t[..., None] * k_t[:, :, None, :])
        return state, jnp.einsum('bhvk,bhk->bhv', state, r_t)

    state0 = jnp.zeros((b, h, n, n), f32)
    _, y = lax.scan(step, state0, xs)
    y = jnp.moveaxis(y, 0, 1)
    mu = jnp.mean(y, axis=-1, keepdims=True)
    var = jnp.mean(jnp.square(y - mu), axis=-1, keepdims=True)
    y = ((y - mu) * lax.rsqrt(var + RW_GN_EPS)).reshape(b, s, c) * lnx_g + lnx_b
    bonus = jnp.sum(r_h * k_h * r_k, axis=-1, keepdims=True) * v_h
    y = (y + bonus.reshape(b, s, c)) * g
    return y.astype(out_dtype)

def mla_attention(q_lat, kv_lat, k_rope, q_norm, w_uq, kv_norm, w_ukv, cos_r, sin_r):
    b, s, _ = q_lat.shape
    h = MLA_HEADS
    q = to_heads(rmsnorm(q_lat, q_norm) @ w_uq, h)
    q_nope, q_pe = q[..., :MLA_NOPE], apply_rope(q[..., MLA_NOPE:], cos_r, sin_r)
    kv = to_heads(rmsnorm(kv_lat, kv_norm) @ w_ukv, h)
    k_nope, v = kv[..., :MLA_NOPE], kv[..., MLA_NOPE:]
    k_pe = apply_rope(k_rope[:, :, None, :], cos_r, sin_r)
    q = jnp.concatenate([q_nope, q_pe], axis=-1)
    k = jnp.concatenate([k_nope, jnp.broadcast_to(k_pe, (b, s, h, MLA_ROPE))], axis=-1)
    out = block_causal_attention(q.transpose(0, 2, 1, 3), k.transpose(0, 2, 1, 3),
                                 v.transpose(0, 2, 1, 3), (MLA_NOPE + MLA_ROPE) ** -0.5)
    return out.transpose(0, 2, 1, 3).reshape(b, s, h * MLA_V)

def forgetting_attention(q, k, v, f_logit, b_f):
    b, s, _ = q.shape
    h = FOX_HEADS
    log_f = jax.nn.log_sigmoid(f_logit.astype(jnp.float32) + b_f.astype(jnp.float32))
    d_cum = jnp.cumsum(log_f, axis=1).transpose(0, 2, 1)
    qh, kh, vh = (to_heads(t, h).transpose(0, 2, 1, 3) for t in (q, k, v))
    out = block_causal_attention(qh, kh, vh, HEAD_DIM ** -0.5, d_cum)
    return out.transpose(0, 2, 1, 3).reshape(b, s, h * HEAD_DIM)

def moba_attention(q, k, v, cos_r, sin_r):
    b, s, _ = q.shape
    h, d = MOBA_HEADS, HEAD_DIM
    qh = apply_rope(to_heads(q, h), cos_r, sin_r).transpose(0, 2, 1, 3)
    kh = apply_rope(to_heads(k, h), cos_r, sin_r).transpose(0, 2, 1, 3)
    vh = to_heads(v, h).transpose(0, 2, 1, 3)
    nb = -(-s // MOBA_BLOCK)
    pad = nb * MOBA_BLOCK - s
    kp = jnp.pad(kh, ((0, 0), (0, 0), (0, pad), (0, 0)))
    vp = jnp.pad(vh, ((0, 0), (0, 0), (0, pad), (0, 0)))
    k_blocks = kp.reshape(b, h, nb, MOBA_BLOCK, d)
    v_blocks = vp.reshape(b, h, nb, MOBA_BLOCK, d)
    k_mean = jnp.mean(k_blocks.astype(jnp.float32), axis=3).astype(kh.dtype)
    n_sel = min(MOBA_TOPK, nb)
    n_sel_keys = n_sel * MOBA_BLOCK
    scale = d ** -0.5
    b_idx = jnp.arange(b)[:, None, None, None]
    h_idx = jnp.arange(h)[None, :, None, None]
    blk_ids = jnp.arange(nb)
    offs = jnp.arange(MOBA_BLOCK)

    def one_chunk(i):
        start = i * MOBA_Q_CHUNK
        qc = lax.dynamic_slice_in_dim(qh, start, MOBA_Q_CHUNK, axis=2)
        q_pos = start + jnp.arange(MOBA_Q_CHUNK)
        own = start // MOBA_BLOCK
        gate = jnp.einsum('bhqd,bhnd->bhqn', qc, k_mean).astype(jnp.float32)
        gate = jnp.where(blk_ids < own, gate, -jnp.inf)
        _, sel = lax.top_k(gate, n_sel)
        sel_valid = sel < own
        k_sel = k_blocks[b_idx, h_idx, sel]
        v_sel = v_blocks[b_idx, h_idx, sel]
        s_sel = jnp.einsum('bhqd,bhqjld->bhqjl', qc, k_sel).astype(jnp.float32) * scale
        s_sel = jnp.where(sel_valid[..., None], s_sel, -jnp.inf)
        k_own = lax.dynamic_slice_in_dim(kp, own * MOBA_BLOCK, MOBA_BLOCK, axis=2)
        v_own = lax.dynamic_slice_in_dim(vp, own * MOBA_BLOCK, MOBA_BLOCK, axis=2)
        s_own = jnp.einsum('bhqd,bhld->bhql', qc, k_own).astype(jnp.float32) * scale
        s_own = jnp.where((own * MOBA_BLOCK + offs)[None, :] <= q_pos[:, None], s_own, -jnp.inf)
        logits = jnp.concatenate([s_sel.reshape(b, h, MOBA_Q_CHUNK, n_sel_keys), s_own], axis=-1)
        p = jax.nn.softmax(logits, axis=-1).astype(vh.dtype)
        p_sel = p[..., :n_sel_keys].reshape(b, h, MOBA_Q_CHUNK, n_sel, MOBA_BLOCK)
        p_own = p[..., n_sel_keys:]
        return (jnp.einsum('bhqjl,bhqjld->bhqd', p_sel, v_sel)
                + jnp.einsum('bhql,bhld->bhqd', p_own, v_own))

    out = lax.map(one_chunk, jnp.arange(s // MOBA_Q_CHUNK))
    out = out.transpose(1, 2, 0, 3, 4).reshape(b, h, s, d)
    return out.transpose(0, 2, 1, 3).reshape(b, s, h * d)

def moe_swiglu(t, router, w_gate, w_up, w_down):
    logits = (t @ router).astype(jnp.float32)
    top_logits, top_idx = lax.top_k(logits, TOP_K)
    gates = jax.nn.softmax(top_logits, axis=-1)
    combine = jnp.sum(jax.nn.one_hot(top_idx, N_EXPERTS, dtype=jnp.float32) * gates[..., None], axis=1)
    out = jnp.zeros_like(t)
    for e in range(N_EXPERTS):
        out = out + combine[:, e:e + 1].astype(t.dtype) * swiglu(t, w_gate[e], w_up[e], w_down[e])
    return out

def even_layer(h, norm_mix, w_in, shift_mu, rw_w0, rw_w2, rw_a0, rw_a2, rw_g2, rw_kk, rw_ka,
               rw_rk, rw_lnx_g, rw_lnx_b, mla_qnorm, mla_wuq, mla_kvnorm, mla_wukv, w_out,
               norm_ffn, ffn_wg, ffn_wu, ffn_wd, cos_r, sin_r):
    u = rmsnorm(h, norm_mix)
    proj = u @ w_in
    rw_cols, mla_cols = proj[..., :RW_COLS], proj[..., RW_COLS:]
    rw_prev = jnp.pad(rw_cols[:, :-1], ((0, 0), (1, 0), (0, 0)))
    rw_cols = rw_cols + shift_mu * (rw_prev - rw_cols)
    y_a = rwkv7_time_mix(*split_cols(rw_cols, RW_SIZES), rw_w0, rw_w2, rw_a0, rw_a2, rw_g2,
                         rw_kk, rw_ka, rw_rk, rw_lnx_g, rw_lnx_b)
    y_b = mla_attention(*split_cols(mla_cols, MLA_SIZES), mla_qnorm, mla_wuq, mla_kvnorm,
                        mla_wukv, cos_r, sin_r)
    h = h + jnp.concatenate([y_a, y_b], axis=-1) @ w_out
    return h + swiglu(rmsnorm(h, norm_ffn), ffn_wg, ffn_wu, ffn_wd)

def odd_layer(h, norm_mix, w_in, fox_bf, w_out, norm_ffn, router, moe_wg, moe_wu, moe_wd,
              cos_r, sin_r):
    b, s, d = h.shape
    u = rmsnorm(h, norm_mix)
    proj = u @ w_in
    fox_cols, moba_cols = proj[..., :FOX_COLS], proj[..., FOX_COLS:]
    y_c = forgetting_attention(*split_cols(fox_cols, FOX_SIZES), fox_bf)
    y_d = moba_attention(*split_cols(moba_cols, MOBA_SIZES), cos_r, sin_r)
    h = h + jnp.concatenate([y_c, y_d], axis=-1) @ w_out
    t = rmsnorm(h, norm_ffn).reshape(b * s, d)
    return h + moe_swiglu(t, router, moe_wg, moe_wu, moe_wd).reshape(b, s, d)

def second_inputs(seed: int = 0) -> dict:
    key = jax.random.key(seed)
    ks = iter(jax.random.split(key, 40))
    D = D_MODEL

    def nrm(shape, scale):
        return scale * jax.random.normal(next(ks), shape, jnp.float32)

    def gain(n):
        return 1.0 + nrm((n,), 0.05)

    return {
        'x': nrm((BATCH, SEQ, D), 1.0),
        'norm_mix_0': gain(D),
        'w_in_0': nrm((D, IN0_COLS), D ** -0.5),
        'shift_mu_0': jax.random.uniform(next(ks), (RW_COLS,), jnp.float32, 0.2, 0.8),
        'rw_w0_0': jax.random.uniform(next(ks), (RW_DIM,), jnp.float32, -6.0, -1.0),
        'rw_w2_0': nrm((DECAY_LORA, RW_DIM), DECAY_LORA ** -0.5),
        'rw_a0_0': nrm((RW_DIM,), 0.1),
        'rw_a2_0': nrm((AAA_LORA, RW_DIM), AAA_LORA ** -0.5),
        'rw_g2_0': nrm((GATE_LORA, RW_DIM), GATE_LORA ** -0.5),
        'rw_kk_0': 0.85 + nrm((RW_DIM,), 0.05),
        'rw_ka_0': 1.0 + nrm((RW_DIM,), 0.05),
        'rw_rk_0': nrm((RW_HEADS, HEAD_DIM), 0.1),
        'rw_lnx_g_0': gain(RW_DIM),
        'rw_lnx_b_0': nrm((RW_DIM,), 0.02),
        'mla_qnorm_0': gain(MLA_Q_RANK),
        'mla_wuq_0': nrm((MLA_Q_RANK, MLA_HEADS * (MLA_NOPE + MLA_ROPE)), MLA_Q_RANK ** -0.5),
        'mla_kvnorm_0': gain(MLA_KV_RANK),
        'mla_wukv_0': nrm((MLA_KV_RANK, MLA_HEADS * (MLA_NOPE + MLA_V)), MLA_KV_RANK ** -0.5),
        'w_out_0': nrm((MIX0_OUT, D), MIX0_OUT ** -0.5),
        'norm_ffn_0': gain(D),
        'ffn_wg_0': nrm((D, D_FF), D ** -0.5),
        'ffn_wu_0': nrm((D, D_FF), D ** -0.5),
        'ffn_wd_0': nrm((D_FF, D), D_FF ** -0.5),
        'norm_mix_1': gain(D),
        'w_in_1': nrm((D, IN1_COLS), D ** -0.5),
        'fox_bf_1': 3.0 + nrm((FOX_HEADS,), 0.5),
        'w_out_1': nrm((MIX1_OUT, D), MIX1_OUT ** -0.5),
        'norm_ffn_1': gain(D),
        'router_1': nrm((D, N_EXPERTS), D ** -0.5),
        'moe_wg_1': nrm((N_EXPERTS, D, D_EXPERT), D ** -0.5),
        'moe_wu_1': nrm((N_EXPERTS, D, D_EXPERT), D ** -0.5),
        'moe_wd_1': nrm((N_EXPERTS, D_EXPERT, D), D_EXPERT ** -0.5),
        'final_norm': gain(D),
    }

def second_block(x, norm_mix_0, w_in_0, shift_mu_0, rw_w0_0, rw_w2_0, rw_a0_0, rw_a2_0, rw_g2_0,
              rw_kk_0, rw_ka_0, rw_rk_0, rw_lnx_g_0, rw_lnx_b_0, mla_qnorm_0, mla_wuq_0,
              mla_kvnorm_0, mla_wukv_0, w_out_0, norm_ffn_0, ffn_wg_0, ffn_wu_0, ffn_wd_0,
              norm_mix_1, w_in_1, fox_bf_1, w_out_1, norm_ffn_1, router_1, moe_wg_1, moe_wu_1,
              moe_wd_1, final_norm):
    seq_len = x.shape[1]
    rope_mla = rope_tables(seq_len, MLA_ROPE)
    rope_full = rope_tables(seq_len, HEAD_DIM)
    layer_params = (
        (norm_mix_0, w_in_0, shift_mu_0, rw_w0_0, rw_w2_0, rw_a0_0, rw_a2_0, rw_g2_0, rw_kk_0,
         rw_ka_0, rw_rk_0, rw_lnx_g_0, rw_lnx_b_0, mla_qnorm_0, mla_wuq_0, mla_kvnorm_0,
         mla_wukv_0, w_out_0, norm_ffn_0, ffn_wg_0, ffn_wu_0, ffn_wd_0),
        (norm_mix_1, w_in_1, fox_bf_1, w_out_1, norm_ffn_1, router_1, moe_wg_1, moe_wu_1,
         moe_wd_1),
    )
    h = x
    for layer in range(DEPTH):
        if layer % 2 == 0:
            h = even_layer(h, *layer_params[layer], *rope_mla)
        else:
            h = odd_layer(h, *layer_params[layer], *rope_full)
    return rmsnorm(h, final_norm)


def setup_inputs(seed=0):
    out = dict(first_inputs(seed))
    for name, value in second_inputs(seed + 1).items():
        if name != "x":
            out[name + "_2"] = value
    return out


def reference(
    x, c, ctx, c_ctx, ada_w, ada_b, ln1_g, ln1_b, ln2_g, ln2_b, ffn_w_gate, ffn_w_up,
    ffn_w_down, dn_w_in, dn_conv, dn_a_log, dn_dt_bias, dn_norm_g, dn_w_out, da_w_in, da_lambda,
    da_subln_g, da_w_out, norm_mix_0_2, w_in_0_2, shift_mu_0_2, rw_w0_0_2, rw_w2_0_2, rw_a0_0_2,
    rw_a2_0_2, rw_g2_0_2, rw_kk_0_2, rw_ka_0_2, rw_rk_0_2, rw_lnx_g_0_2, rw_lnx_b_0_2,
    mla_qnorm_0_2, mla_wuq_0_2, mla_kvnorm_0_2, mla_wukv_0_2, w_out_0_2, norm_ffn_0_2,
    ffn_wg_0_2, ffn_wu_0_2, ffn_wd_0_2, norm_mix_1_2, w_in_1_2, fox_bf_1_2, w_out_1_2,
    norm_ffn_1_2, router_1_2, moe_wg_1_2, moe_wu_1_2, moe_wd_1_2, final_norm_2,
):
    x = first_block(
        x, c, ctx, c_ctx, ada_w, ada_b, ln1_g, ln1_b, ln2_g, ln2_b, ffn_w_gate, ffn_w_up,
        ffn_w_down, dn_w_in, dn_conv, dn_a_log, dn_dt_bias, dn_norm_g, dn_w_out, da_w_in,
        da_lambda, da_subln_g, da_w_out,
    )
    return second_block(
        x, norm_mix_0_2, w_in_0_2, shift_mu_0_2, rw_w0_0_2, rw_w2_0_2, rw_a0_0_2, rw_a2_0_2,
        rw_g2_0_2, rw_kk_0_2, rw_ka_0_2, rw_rk_0_2, rw_lnx_g_0_2, rw_lnx_b_0_2, mla_qnorm_0_2,
        mla_wuq_0_2, mla_kvnorm_0_2, mla_wukv_0_2, w_out_0_2, norm_ffn_0_2, ffn_wg_0_2,
        ffn_wu_0_2, ffn_wd_0_2, norm_mix_1_2, w_in_1_2, fox_bf_1_2, w_out_1_2, norm_ffn_1_2,
        router_1_2, moe_wg_1_2, moe_wu_1_2, moe_wd_1_2, final_norm_2,
    )


_drawn_inputs = setup_inputs


def setup_inputs(seed=0):
    import zlib

    import numpy as np

    out = dict(_drawn_inputs(seed))
    spreads = {}
    factors = {'da_lambda': 8.0, 'da_subln_g': 4.101, 'mla_qnorm_0_2': 2.949}
    for name, (base, spread) in spreads.items():
        noise = np.random.default_rng([zlib.crc32(name.encode()), seed]).standard_normal(out[name].shape)
        drawn = base * np.exp(spread * noise) if base else spread * noise
        out[name] = jnp.asarray(drawn.astype(out[name].dtype))
    for name, factor in factors.items():
        out[name] = (out[name] * factor).astype(out[name].dtype)
    return out
```

```python
import math
from contextlib import ExitStack

import numpy as np
import concourse.bass as bass
from concourse import mybir

P = 128
D = 1024
KB = D // P
L = 256
F32 = mybir.dt.float32
BF16 = mybir.dt.bfloat16
U32 = mybir.dt.uint32
ALU = mybir.AluOpType
ACT = mybir.ActivationFunctionType
AX = mybir.AxisListType.X
ds = bass.ds

DEPTH = 2
ALPHA = (2.0 * DEPTH) ** 0.25
FFN = 2816
EXPERTS, D_EXPERT = 8, 3584
HEADS = 8
PAIRS = HEADS // 2
RW_COLS = 1792
MLA_QK = 96
LAMBDA_INIT = 0.8 - 0.6 * math.exp(-0.3 * 1)
LEVELS = 7
NEG = -1e30

C_ID, C_UP, C_LO, C_SUP, C_ONES, C_ONES64, C_RDA, C_RMLA, C_RMOBA, C_LV = range(10)
N_MATS = C_LV + 2 * LEVELS
E_RMS, E_LN, E_GN, E_SHIFT = range(4)
T_DA, T_MLA, T_MOBA = range(3)
GUARD_LOG2 = 20


def constants():
    f = np.float32
    r, c = np.arange(P)[:, None], np.arange(P)[None, :]
    m = np.zeros((P, N_MATS, P), f)
    m[:, C_ID] = r == c
    m[:, C_UP] = r <= c
    m[:, C_LO] = r >= c
    m[:, C_SUP] = r < c
    m[:, C_ONES] = 1
    m[:, C_ONES64] = r // 64 == c // 64

    def rotation(start, width):
        h = width // 2
        for j in range(h):
            yield start + h + j, start + j, -1.0
            yield start + j, start + h + j, 1.0

    for b in range(4):
        for i, o, v in rotation(32 * b, 32):
            m[i, C_RDA, o] = v
    for i, o, v in rotation(64, 32):
        m[i, C_RMLA, o] = v
    for b in range(2):
        for i, o, v in rotation(64 * b, 64):
            m[i, C_RMOBA, o] = v
    for l in range(LEVELS):
        b = 1 << l
        lower = (r // (2 * b) == c // (2 * b)) & (r // b % 2 == 1) & (c // b % 2 == 0)
        m[:, C_LV + l] = lower
        m[:, C_LV + LEVELS + l] = lower.T

    def tables(ang):
        return np.cos(ang), np.sin(ang)

    pos = np.arange(L, dtype=f)
    t = np.zeros((P, 3, 2, L), f)
    inv = f(10000.0) ** (-np.arange(16, dtype=f) / f(16))
    row, col = np.floor(pos / 64).astype(f), (pos % 64).astype(f)
    ang = np.concatenate([inv[:, None] * row, inv[:, None] * row, inv[:, None] * col, inv[:, None] * col])
    t[:, T_DA, 0], t[:, T_DA, 1] = (np.concatenate([x, x]) for x in tables(ang.astype(f)))
    inv = f(10000.0) ** (-np.arange(0, 32, 2, dtype=f) / f(32))
    ang = np.concatenate([inv[:, None] * pos] * 2).astype(f)
    t[:, T_MLA, 0] = 1
    t[64:96, T_MLA, 0], t[64:96, T_MLA, 1] = tables(ang)
    inv = f(10000.0) ** (-np.arange(0, 64, 2, dtype=f) / f(64))
    ang = np.concatenate([inv[:, None] * pos] * 4).astype(f)
    t[:, T_MOBA, 0], t[:, T_MOBA, 1] = tables(ang)

    mask = np.zeros((P, 3, P), f)
    mask[:, 0] = mask[:, 2] = np.where(c > r, f(NEG), f(0))
    eps = np.zeros((P, 4), f)
    eps[:, E_RMS], eps[:, E_LN], eps[:, E_GN], eps[:, E_SHIFT] = 1e-6, 1e-5, 64e-5, GUARD_LOG2 / 2 * math.log(2)
    return {
        "const_mats": m.reshape(P, -1), "const_rope": t.reshape(P, -1),
        "const_mask": mask.reshape(P, -1), "const_eps": eps, "const_iota": np.arange(EXPERTS, dtype=f),
    }


class Steps:

    def __init__(self, k, name, steps):
        self.sem, self.sem_name, self.names, self.built = k.sem(name), name, steps.split(), 0
        self.n = len(self.names)
        k.steps.append(self)

    def credit(self, eng):
        eng.sem_inc(self.sem, self.n)

    def at(self, name, rnd=0):
        return self.sem, rnd * self.n + (self.n + self.names.index(name) + 1)

    def done(self, name):
        assert self.names[self.built % self.n] == name, (name, self.names[self.built % self.n])
        self.built += 1
        return self.sem, 1


class Kern:
    pass


def setup(k, nc, ctx, t, out):
    k.nc, k.t, k.out, k.steps = nc, t, out, []

    def sb(name, shape, dt=F32):
        return ctx.enter_context(nc.sbuf_tensor(name, shape, dt))

    k.sem = lambda name: ctx.enter_context(nc.semaphore(name))
    k.X = sb("X", [P, 4, D])
    k.XT = sb("XT", [P, KB, 2 * L])
    k.OT = sb("OT", [P, KB, 2 * L])
    k.WO = sb("WO", [P, KB, D])
    k.WH = sb("WH", [P, 4, D])
    k.WF = sb("WF", [P, 2, 3, D])
    k.mats = sb("mats", [P, N_MATS, P])
    k.rope = sb("rope", [P, 3, 2, L])
    k.mask = sb("mask", [P, 3, P])
    k.eps = sb("eps", [P, 4])
    k.vecs = sb("vecs", [P, 3, P])

    k.S = sb("scratch", [P, 16384])
    k.vrow = view(k, 13312, 3, P)
    k.small = sb("small", [P, 512])
    k.zero = sb("zero", [P, 640], BF16)
    k.PS = ctx.enter_context(nc.psum_tensor("PS", [P, 8, 512], F32))
    k.ada = nc.dram_tensor("ada_rows", (2, 2, 6 * D), F32, kind="Internal").ap()
    k.grow = nc.dram_tensor("gate_rows", (HEADS, 4, 2 * L), F32, kind="Internal").ap()
    k.frow = nc.dram_tensor("forget_rows", (HEADS, L), F32, kind="Internal").ap()

    k.d = {name: k.sem("dma_" + name) for name in (
        "consts vecs x ada_b ada_w0 ada_w1 ada_store ada_vecs head_w gate_w gate_in gate_store gate_rows "
        "out_w norm_rows ffn_w0 ffn_w1 lam_in lora_w lat_w forget_in forget_store forget_rows router_in "
        "out_store").split()}


def view(k, at, *shape):
    n = int(np.prod(shape))
    v = k.S[:, at:at + n]
    if len(shape) == 1:
        return v
    if len(shape) == 2:
        return v.rearrange("p (a b) -> p a b", a=shape[0])
    if len(shape) == 3:
        return v.rearrange("p (a b c) -> p a b c", a=shape[0], b=shape[1])
    return v.rearrange("p (a b c d) -> p a b c d", a=shape[0], b=shape[1], c=shape[2])


def mat(k, c):
    return k.mats[:, c, :]


def bcast(ap, n):
    return ap.unsqueeze(1).to_broadcast([ap.shape[0], n, ap.shape[-1]])


def feature_rows(ap):
    return ap.rearrange("(kb p) n -> p kb n", p=P)


def rsqrt(k, act, buf, src, scale, eps):
    act.activation(buf, src, ACT.Ln, scale=scale, bias=eps)
    act.drain()
    return act.activation(buf, buf, ACT.Exp, scale=-0.5)



V_DN_G, V_DA_G, V_QN, V_KVN, V_MUW = 120, 121, 122, 124, 125
V_MIX0, V_FFN0, V_MIX1, V_FFN1, V_C = 40, 48, 56, 64, 72
ROWS0, ROWS1 = 127, 88
N_VEC_LOADS = 20
N_ADA_VEC_LOADS = 8


def mod_col(k, layer, who, part, what, kb):
    c = ((layer * 2 + who) * 2 + part) * 16 + what * 8 + kb
    return k.vecs[:, 2, c:c + 1]


def vec_col(k, tile, c):
    return k.vecs[:, tile, c:c + 1]


def declare_pre(k):
    k.pre_pe = Steps(k, "pre_pe", "vecs")
    k.pre_act = Steps(k, "pre_act", "vecs silu")
    k.pre_dve = Steps(k, "pre_dve", "zeros")
    k.ada_pe = Steps(k, "ada_pe", "half0 half1")
    k.ada_dve = Steps(k, "ada_dve", "half0 half1")
    k.adv_pe = Steps(k, "adv_pe", "cols")
    k.adv_act = Steps(k, "adv_act", "cols")
    k.adv_dve = Steps(k, "adv_dve", "scales")
    k.ada_acc = k.S[0:2, 0:12 * D]
    k.cond = k.small[:, 496:512]


def pre_sync(k, sp):
    t, d = k.t, k.d
    sp.dma_start(k.mats[:, :, :].rearrange("p a b -> p (a b)"), t["const_mats"]).then_inc(d["consts"], 16)
    sp.dma_start(k.eps[:, :], t["const_eps"]).then_inc(d["consts"], 16)

    def rows(tile, at, ap, n):
        sp.dma_start(k.vrow[at:at + n, tile, :], ap.rearrange("(r c) -> r c", c=P)).then_inc(d["vecs"], 16)

    rows(1, V_C, t["c"][0], 8)
    rows(1, V_C + 8, t["c_ctx"], 8)
    rows(0, 0, t["dn_conv"][0].rearrange("a n -> (a n)"), 120)
    rows(0, V_DN_G, t["dn_norm_g"][0], 1)
    rows(0, V_DA_G, t["da_subln_g"][0], 1)
    rows(0, V_QN, t["mla_qnorm_0_2"], 2)
    rows(0, V_KVN, t["mla_kvnorm_0_2"], 1)
    rows(0, V_MUW, t["shift_mu_0_2"][1536:RW_COLS], 2)
    rows(1, 0, t["shift_mu_0_2"][0:1536], 12)
    for n, name in enumerate(("rw_w0_0_2", "rw_a0_0_2", "rw_kk_0_2", "rw_ka_0_2")):
        rows(1, 12 + 4 * n, t[name], 4)
    rows(1, 28, t["rw_rk_0_2"].rearrange("h d -> (h d)"), 4)
    rows(1, 32, t["rw_lnx_g_0_2"], 4)
    rows(1, 36, t["rw_lnx_b_0_2"], 4)
    for at, name in ((V_MIX0, "norm_mix_0_2"), (V_FFN0, "norm_ffn_0_2"), (V_MIX1, "norm_mix_1_2"),
                     (V_FFN1, "norm_ffn_1_2")):
        rows(1, at, t[name], 8)
    sp.dma_start(k.ada_acc, t["ada_b"].rearrange("l n -> (l n)").partition_broadcast(2)).then_inc(d["ada_b"], 16)
    for layer in range(DEPTH):
        with sp.Fori(0, 6) as j:
            for half in range(2):
                sp.wait_ge(*k.ada_pe.at(f"half{half}", j + (layer * 6 - 1)))
                sp.dma_start(k.WO[:, :, half * 512:(half + 1) * 512],
                             feature_rows(t["ada_w"][layer])[:, :, ds(j * D + half * 512, 512)]
                             ).then_inc(d[f"ada_w{half}"], 16)
    sp.dma_start(k.X[:, 0:2, :], t["x"][0].rearrange("(t p) n -> p t n", p=P)).then_inc(d["x"], 16)
    sp.dma_start(k.X[:, 2:4, :], t["ctx"][0].rearrange("(t p) n -> p t n", p=P)).then_inc(d["x"], 16)
    sp.dma_start(k.rope[:, :, :, :].rearrange("p a b c -> p (a b c)"), t["const_rope"]).then_inc(d["x"], 16)
    sp.dma_start(k.mask[:, :, :].rearrange("p a b -> p (a b)"), t["const_mask"]).then_inc(d["x"], 16)


def pre_gpsimd(k, pool):
    d = k.d
    for layer in range(DEPTH):
        pool.wait_ge(*k.ada_dve.at("half1", layer * 6 + 5))
        pool.dma_start(k.ada[layer], k.ada_acc[:, layer * 6 * D:(layer + 1) * 6 * D]).then_inc(d["ada_store"], 16)
    pool.wait_ge(d["ada_store"], 32)
    for layer in range(DEPTH):
        for who in range(2):
            for part in range(2):
                at = ((layer * 2 + who) * 2 + part) * 16
                src = k.ada[layer, who, part * 3 * D:part * 3 * D + 2 * D]
                pool.dma_start(k.vrow[at:at + 16, 2, :], src.rearrange("(r c) -> r c", c=P)
                               ).then_inc(d["ada_vecs"], 16)


def pre_tensor(k, pe):
    nc, d = k.nc, k.d
    pe.wait_ge(d["consts"], 32)
    pe.wait_ge(d["vecs"], 16 * N_VEC_LOADS)
    ident = mat(k, C_ID)
    nc.tensor.transpose(k.PS[:, 2, 0:ROWS0], k.vrow[0:ROWS0, 0, :], ident[0:ROWS0, 0:ROWS0])
    nc.tensor.transpose(k.PS[:, 3, 0:ROWS1], k.vrow[0:ROWS1, 1, :], ident[0:ROWS1, 0:ROWS1]
                        ).then_inc(*k.pre_pe.done("vecs"))
    pe.wait_ge(*k.pre_act.at("silu"))
    cond = k.cond.rearrange("p (w kb) -> p kb w", w=2)
    for layer in range(DEPTH):
        with pe.Fori(0, 6) as j:
            for half in range(2):
                pe.wait_ge(d[f"ada_w{half}"], j * 16 + (layer * 6 + 1) * 16)
                pe.wait_ge(*k.ada_dve.at(f"half{half}", j + (layer * 6 - 1)))
                for kb in range(KB):
                    mm = nc.tensor.matmul(k.PS[0:2, half, :], cond[:, kb, :],
                                          k.WO[:, kb, half * 512:(half + 1) * 512],
                                          start=kb == 0, stop=kb == KB - 1)
                mm.then_inc(*k.ada_pe.done(f"half{half}"))
    pe.wait_ge(d["ada_vecs"], 16 * N_ADA_VEC_LOADS)
    nc.tensor.transpose(k.PS[:, 2, 0:P], k.vrow[:, 2, :], ident).then_inc(*k.adv_pe.done("cols"))


def pre_scalar(k, act):
    act.wait_ge(*k.pre_pe.at("vecs"))
    act.activation(k.vecs[:, 0, 0:ROWS0], k.PS[:, 2, 0:ROWS0], ACT.Copy)
    act.activation(k.vecs[:, 1, 0:ROWS1], k.PS[:, 3, 0:ROWS1], ACT.Copy).then_inc(*k.pre_act.done("vecs"))
    act.activation(k.cond, k.PS[:, 3, V_C:V_C + 16], ACT.Silu).then_inc(*k.pre_act.done("silu"))
    act.wait_ge(*k.adv_pe.at("cols"))
    act.activation(k.vecs[:, 2, :], k.PS[:, 2, 0:P], ACT.Copy).then_inc(*k.adv_act.done("cols"))


def pre_vector(k, dve):
    nc, d = k.nc, k.d
    nc.vector.memset(k.zero[:, :], 0.0).then_inc(*k.pre_dve.done("zeros"))
    dve.wait_ge(d["ada_b"], 16)
    for layer in range(DEPTH):
        with dve.Fori(0, 6) as j:
            for half in range(2):
                dve.wait_ge(*k.ada_pe.at(f"half{half}", j + layer * 6))
                acc = k.ada_acc[:, ds(j * D + (layer * 6 * D + half * 512), 512)]
                nc.vector.tensor_tensor(acc, acc, k.PS[0:2, half, :], ALU.add
                                        ).then_inc(*k.ada_dve.done(f"half{half}"))
    dve.wait_ge(*k.adv_act.at("cols"))
    scales = k.vecs[:, 2, :].rearrange("p (a s kb) -> p a s kb", s=2, kb=8)[:, :, 1, :]
    nc.vector.tensor_scalar(scales, scales, 1.0, None, ALU.add).then_inc(*k.adv_dve.done("scales"))



def declare_xt(k):
    k.xt_pe = Steps(k, "xt_pe", " ".join(f"t{kb}" for kb in range(KB)))
    k.xt_act = Steps(k, "xt_act", " ".join(f"x{kb}" for kb in range(KB)))


def xt_tensor(k, pe, rnd, src, tiles):
    nc = k.nc
    for kb in range(KB):
        if kb >= 4:
            pe.wait_ge(*k.xt_act.at(f"x{kb - 4}", rnd))
        for n, tile in enumerate(tiles):
            mm = nc.tensor.transpose(k.PS[:, kb % 4, n * P:(n + 1) * P], src(tile, kb), mat(k, C_ID))
        mm.then_inc(*k.xt_pe.done(f"t{kb}"))


def xt_scalar(k, act, rnd, parts):
    for kb in range(KB):
        act.wait_ge(*k.xt_pe.at(f"t{kb}", rnd))
        for n, (to, scale, shift) in enumerate(parts):
            a = act.activation(k.XT[:, kb, to:to + L], k.PS[:, kb % 4, n * L:(n + 1) * L], ACT.Identity,
                               scale=scale(kb), bias=shift(kb) if shift else 0.0)
        a.then_inc(*k.xt_act.done(f"x{kb}"))



def declare_norms(k):
    k.out_pe = Steps(k, "out_pe", "y0 y1 y2 y3")
    k.ln_dve = Steps(k, "ln_dve", "var out")
    k.ln_act = Steps(k, "ln_act", "rstd")
    k.res_dve = Steps(k, "res_dve", "h out")
    k.res_act = Steps(k, "res_act", "rstd")


def out_tensor(k, pe, rnd, tiles, ready):
    nc = k.nc
    pe.wait_ge(k.d["out_w"], 16 * (rnd + 1))
    for w in ready:
        pe.wait_ge(*w)
    for tile in range(4):
        if tile in tiles:
            for half in range(2):
                for kb in range(KB):
                    mm = nc.tensor.matmul(k.PS[:, tile * 2 + half, :], k.OT[:, kb, tile * P:(tile + 1) * P],
                                          k.WO[:, kb, half * 512:(half + 1) * 512],
                                          start=kb == 0, stop=kb == KB - 1)
            mm.then_inc(*k.out_pe.done(f"y{tile}"))
        else:
            pe.drain().then_inc(*k.out_pe.done(f"y{tile}"))


def bank_rows(k, bank):
    return k.PS[:, bank:bank + 2, :].rearrange("p a b -> p (a b)")


def ln_vector(k, dve, rnd, tile, bank, gate):
    nc = k.nc
    r = view(k, 0, D)
    stats, mv, var = k.small[:, 400:412], k.small[:, 412:414], k.small[:, 413:414]
    nc.vector.tensor_tensor(r, bank_rows(k, bank), k.WH[:, gate, :], ALU.mult)
    dve.drain()
    nc.vector.scalar_tensor_tensor(r, k.X[:, tile, :], ALPHA, r, ALU.mult, ALU.add)
    dve.drain()
    for h in range(2):
        nc.vector.bn_stats(stats[:, 6 * h:6 * h + 6], r[:, h * 512:(h + 1) * 512])
    dve.drain()
    nc.vector.bn_aggr(mv, stats).then_inc(*k.ln_dve.done("var"))
    dve.wait_ge(*k.ln_act.at("rstd", rnd))
    dve.drain()
    nc.vector.tensor_scalar(r, r, mv[:, 0:1], k.small[:, 414:415], ALU.subtract, ALU.mult)
    dve.drain()
    nc.vector.tensor_tensor(r, r, k.WH[:, 1, :], ALU.mult)
    dve.drain()
    nc.vector.tensor_tensor(k.X[:, tile, :], r, k.WH[:, 2, :], ALU.add).then_inc(*k.ln_dve.done("out"))
    dve.drain()


def ln_scalar(k, act, rnd):
    act.wait_ge(*k.ln_dve.at("var", rnd))
    rsqrt(k, act, k.small[:, 414:415], k.small[:, 413:414], 1.0, k.eps[:, E_LN:E_LN + 1]
          ).then_inc(*k.ln_act.done("rstd"))


def res_vector(k, dve, rnd, tile, bank, gain=None):
    nc = k.nc
    if bank is None:
        dve.drain().then_inc(*k.res_dve.done("h"))
    else:
        nc.vector.tensor_tensor(k.X[:, tile, :], k.X[:, tile, :], bank_rows(k, bank), ALU.add
                                ).then_inc(*k.res_dve.done("h"))
    dve.wait_ge(*k.res_act.at("rstd", rnd))
    out = view(k, D * (1 + tile), D)
    if gain is None:
        nc.vector.tensor_scalar(out, k.X[:, tile, :], k.small[:, 416 + tile:417 + tile], None, ALU.mult
                                ).then_inc(*k.res_dve.done("out"))
    else:
        nc.vector.scalar_tensor_tensor(out, k.X[:, tile, :], k.small[:, 416 + tile:417 + tile], gain,
                                       ALU.mult, ALU.mult).then_inc(*k.res_dve.done("out"))


def res_scalar(k, act, rnd, tile):
    act.wait_ge(*k.res_dve.at("h", rnd))
    ms = k.small[:, 416 + tile:417 + tile]
    act.activation(view(k, 0, D), k.X[:, tile, :], ACT.Square, accum_out=ms)
    act.drain()
    rsqrt(k, act, ms, ms, 1.0 / D, k.eps[:, E_RMS:E_RMS + 1]).then_inc(*k.res_act.done("rstd"))
    act.drain()



def declare_ffn(k):
    k.ffn_pe = Steps(k, "ffn_pe", "up0 up1 down0 down1")
    k.ffn_act = Steps(k, "ffn_act", "silu0 silu1")
    k.ffn_dve = Steps(k, "ffn_dve", "h0 h1")
    k.acc_pe = Steps(k, "acc_pe", "sum")
    k.sg = view(k, 4096, 2, L)
    k.hid = view(k, 4096 + 2 * L, 2, L)


def ffn_sync(k, sp, wg, wu, wd, rounds, base, off=0):
    wg, wu = feature_rows(wg), feature_rows(wu)
    with sp.Fori(0, rounds) as j:
        for s in range(2):
            sp.wait_ge(*k.ffn_pe.at(f"down{s}", j + (off + (base - 1))))
            cols = ds(j * 256 + s * P, P)
            for n, w in ((0, wg), (1, wu)):
                sp.dma_start(k.WF[:, s, n, :].rearrange("p (kb n) -> p kb n", kb=KB), w[:, :, cols]
                             ).then_inc(k.d[f"ffn_w{s}"], 16)
            sp.dma_start(k.WF[:, s, 2, :], wd[cols, :]).then_inc(k.d[f"ffn_w{s}"], 16)


def zero_sum(k, start):
    for bank in range(4):
        mm = k.nc.tensor.matmul(k.PS[:, bank, :], k.zero[:, 0:P], k.zero[:, P:P + 512],
                                start=start, stop=not start)
    return mm


def ffn_tensor(k, pe, col, rounds, base, off=0):
    nc = k.nc
    zero_sum(k, True)
    with pe.Fori(0, rounds) as j:
        rnd = j + (off + base)
        for s in range(2):
            pe.wait_ge(k.d[f"ffn_w{s}"], (rnd + 1) * 48)
            for n in range(2):
                w = k.WF[:, s, n, :].rearrange("p (kb n) -> p kb n", kb=KB)
                for kb in range(KB):
                    mm = nc.tensor.matmul(k.PS[:, 4 + s, n * L:(n + 1) * L], w[:, kb, :],
                                          k.XT[:, kb, col:col + L], start=kb == 0, stop=kb == KB - 1)
            mm.then_inc(*k.ffn_pe.done(f"up{s}"))
        for s in range(2):
            pe.wait_ge(*k.ffn_dve.at(f"h{s}", rnd))
            for tile in range(2):
                for half in range(2):
                    mm = nc.tensor.matmul(k.PS[:, tile * 2 + half, :], k.hid[:, s, tile * P:(tile + 1) * P],
                                          k.WF[:, s, 2, half * 512:(half + 1) * 512],
                                          start=False, stop=False)
            mm.then_inc(*k.ffn_pe.done(f"down{s}"))
    zero_sum(k, False).then_inc(*k.acc_pe.done("sum"))


def ffn_scalar(k, act, rounds, base, off=0):
    with act.Fori(0, rounds) as j:
        rnd = j + (off + base)
        for s in range(2):
            act.wait_ge(*k.ffn_pe.at(f"up{s}", rnd))
            act.activation(k.sg[:, s, :], k.PS[:, 4 + s, 0:L], ACT.Silu).then_inc(*k.ffn_act.done(f"silu{s}"))


def ffn_vector(k, dve, rounds, base, off=0):
    nc = k.nc
    with dve.Fori(0, rounds) as j:
        rnd = j + (off + base)
        for s in range(2):
            dve.wait_ge(*k.ffn_act.at(f"silu{s}", rnd))
            dve.wait_ge(*k.ffn_pe.at(f"down{s}", rnd - 1))
            nc.vector.tensor_tensor(k.hid[:, s, :], k.sg[:, s, :], k.PS[:, 4 + s, L:2 * L], ALU.mult
                                    ).then_inc(*k.ffn_dve.done(f"h{s}"))



def inverse_steps(groups):
    return (" ".join(" ".join([f"ax{l}{g}" for g in range(groups)] + [f"xax{l}{g}" for g in range(groups)])
                     for l in range(LEVELS)),
            " ".join(" ".join([f"ax{l}{g}" for g in range(groups)] + [f"x{l}{g}" for g in range(groups)])
                     for l in range(LEVELS)))


def inverse_tensor(k, pe, rnd, groups, s_pe, s_dve, at, x, xt, p, banks_p, banks_x, banks_t):
    nc = k.nc
    for l in range(LEVELS):
        for g in range(groups):
            if l:
                pe.wait_ge(*s_dve.at(f"x{l - 1}{g}", rnd))
            for n in range(4):
                mm = nc.tensor.matmul(k.PS[:, banks_p[g], n * P:(n + 1) * P], at(g, n),
                                      x[:, g, n, :] if l else mat(k, C_ID), start=True, stop=True)
            mm.then_inc(*s_pe.done(f"ax{l}{g}"))
        for g in range(groups):
            pe.wait_ge(*s_dve.at(f"ax{l}{g}", rnd))
            for n in range(4):
                if l < LEVELS - 1:
                    nc.tensor.matmul(k.PS[:, banks_x[g], n * P:(n + 1) * P],
                                     xt[:, g, n, :] if l else mat(k, C_ID), p[:, g, n, :],
                                     start=True, stop=True)
                mm = nc.tensor.matmul(k.PS[:, banks_t[g], n * P:(n + 1) * P], p[:, g, n, :],
                                      xt[:, g, n, :] if l else mat(k, C_ID), start=True, stop=True)
            mm.then_inc(*s_pe.done(f"xax{l}{g}"))


def tiles_of(k, bank):
    return k.PS[:, bank, :].rearrange("p (n c) -> p n c", n=4)


def inverse_vector(k, dve, rnd, groups, s_pe, s_dve, x, xt, p, banks_p, banks_x, banks_t, reverse):
    nc = k.nc
    for l in range(LEVELS):
        for g in range(groups):
            dve.wait_ge(*s_pe.at(f"ax{l}{g}", rnd))
            lv = bcast(mat(k, C_LV + l + (LEVELS if reverse[g] else 0)), 4)
            nc.vector.tensor_tensor(p[:, g, :, :], tiles_of(k, banks_p[g]), lv, ALU.mult
                                    ).then_inc(*s_dve.done(f"ax{l}{g}"))
        for g in range(groups):
            dve.wait_ge(*s_pe.at(f"xax{l}{g}", rnd))
            if l < LEVELS - 1:
                nc.vector.tensor_tensor(x[:, g, :, :], x[:, g, :, :] if l else bcast(mat(k, C_ID), 4),
                                        tiles_of(k, banks_x[g]), ALU.subtract)
            nc.vector.tensor_tensor(xt[:, g, :, :], xt[:, g, :, :] if l else bcast(mat(k, C_ID), 4),
                                    tiles_of(k, banks_t[g]), ALU.subtract).then_inc(*s_dve.done(f"x{l}{g}"))



G_CUM, G_NBE, G_BETA, G_KDEC, G_TOT = range(5)


def declare_gates(k):
    k.gate_pe = Steps(k, "gate_pe", "ab sums rows")
    k.gate_act = Steps(k, "gate_act", "beta soft rows decays")
    k.gate_dve = Steps(k, "gate_dve", "nabs g diff nbe")
    k.gw = view(k, 15896, KB, 32)
    k.dtb, k.alog = view(k, 16152, 32)[:, 0:16], view(k, 16152, 32)[:, 16:32]
    k.gx = view(k, 16184, 4, 16)
    k.ge = view(k, 16248, 4, 16)
    k.gg = view(k, 16312, 4, 16)
    k.grows = k.S[0:8, 0:4 * 512]
    k.gall = k.small[:, 0:320].rearrange("p (q t c) -> p q t c", q=5, t=4)


def gates_gpsimd(k, pool):
    t, d = k.t, k.d
    pool.dma_start(k.gw, feature_rows(t["dn_w_in"][0])[:, :, 4 * D:4 * D + 32]).then_inc(d["gate_w"], 16)
    for to, name in ((k.dtb, "dn_dt_bias"), (k.alog, "dn_a_log")):
        pool.dma_start(to, t[name][0].rearrange("d h -> (d h)").partition_broadcast(P)).then_inc(d["gate_in"], 16)
    pool.wait_ge(*k.gate_act.at("rows"))
    pool.dma_start(k.grow.rearrange("h a n -> h (a n)"), k.grows).then_inc(d["gate_store"], 16)
    pool.wait_ge(d["gate_store"], 16)


def gates_tensor(k, pe):
    nc, ps = k.nc, k.PS
    pe.wait_ge(k.d["gate_w"], 16)
    pe.wait_ge(*k.xt_act.at("x7", 0))
    for tile in range(4):
        for kb in range(KB):
            mm = nc.tensor.matmul(ps[:, 4, tile * 32:tile * 32 + 32], k.XT[:, kb, tile * P:(tile + 1) * P],
                                  k.gw[:, kb, :], start=kb == 0, stop=kb == KB - 1)
    mm.then_inc(*k.gate_pe.done("ab"))
    pe.wait_ge(*k.gate_dve.at("g"))
    for tile in range(4):
        for d, tri in ((0, C_UP), (1, C_LO)):
            nc.tensor.matmul(ps[:, 5, tile * 16 + 8 * d:tile * 16 + 8 * d + 8], mat(k, tri),
                             k.gg[:, tile, 8 * d:8 * d + 8], start=True, stop=True)
        mm = nc.tensor.matmul(ps[:, 6, tile * 16:tile * 16 + 16], mat(k, C_ONES), k.gg[:, tile, :],
                              start=True, stop=True)
    mm.then_inc(*k.gate_pe.done("sums"))
    for tile in range(4):
        c = slice(tile * P, (tile + 1) * P)
        for d, tri in ((0, C_UP), (1, C_LO)):
            nc.tensor.matmul(ps[0:8, d, c], k.gg[:, tile, 8 * d:8 * d + 8], mat(k, tri), start=True, stop=True)
            mm = nc.tensor.matmul(ps[0:8, 2 + d, c], k.gall[:, G_BETA, tile, 8 * d:8 * d + 8], mat(k, C_ID),
                                  start=True, stop=True)
    mm.then_inc(*k.gate_pe.done("rows"))


def gates_scalar(k, act):
    ps = k.PS
    act.wait_ge(*k.gate_pe.at("ab"))
    ab = ps[:, 4, 0:128].rearrange("p (t c) -> p t c", t=4)
    act.activation(k.gall[:, G_BETA, :, :], ab[:, :, 16:32], ACT.Sigmoid).then_inc(*k.gate_act.done("beta"))
    act.wait_ge(*k.gate_dve.at("nabs"))
    act.wait_ge(k.d["gate_in"], 32)
    act.activation(k.alog, k.alog, ACT.Exp)
    act.activation(k.ge, k.ge, ACT.Exp)
    act.drain()
    act.activation(k.ge, k.ge, ACT.Ln, bias=1.0).then_inc(*k.gate_act.done("soft"))
    act.wait_ge(*k.gate_pe.at("rows"))
    act.activation(k.grows, ps[0:8, 0:4, :].rearrange("p a b -> p (a b)"), ACT.Copy
                   ).then_inc(*k.gate_act.done("rows"))
    act.wait_ge(*k.gate_dve.at("diff"))
    act.activation(k.gall[:, G_NBE, :, :], k.gall[:, G_CUM, :, :], ACT.Exp)
    act.activation(k.gall[:, G_KDEC, :, :], k.gall[:, G_KDEC, :, :], ACT.Exp)
    act.activation(k.gall[:, G_TOT, :, :], ps[:, 6, 0:64].rearrange("p (t c) -> p t c", t=4), ACT.Exp)
    act.drain().then_inc(*k.gate_act.done("decays"))


def gates_vector(k, dve):
    nc, ps = k.nc, k.PS
    dve.wait_ge(*k.gate_act.at("beta"))
    dve.wait_ge(k.d["gate_in"], 32)
    ab = ps[:, 4, 0:128].rearrange("p (t c) -> p t c", t=4)
    nc.vector.tensor_tensor(k.gx, ab[:, :, 0:16], bcast(k.dtb, 4), ALU.add)
    dve.drain()
    nc.vector.scalar_tensor_tensor(k.ge, k.gx, -1.0, k.gx, ALU.mult, ALU.min).then_inc(*k.gate_dve.done("nabs"))
    dve.wait_ge(*k.gate_act.at("soft"))
    nc.vector.scalar_tensor_tensor(k.gx, k.gx, 0.0, k.ge, ALU.max, ALU.add)
    dve.wait_ge(*k.gate_act.at("soft"))
    dve.drain()
    nc.vector.scalar_tensor_tensor(k.gg, k.gx, -1.0, bcast(k.alog, 4), ALU.mult, ALU.mult
                                   ).then_inc(*k.gate_dve.done("g"))
    dve.wait_ge(*k.gate_pe.at("sums"))
    nc.vector.tensor_copy(k.gall[:, G_CUM, :, :], ps[:, 5, 0:64].rearrange("p (t c) -> p t c", t=4))
    dve.drain()
    nc.vector.tensor_tensor(k.gall[:, G_KDEC, :, :], ps[:, 6, 0:64].rearrange("p (t c) -> p t c", t=4),
                            k.gall[:, G_CUM, :, :], ALU.subtract).then_inc(*k.gate_dve.done("diff"))
    dve.wait_ge(*k.gate_act.at("decays"))
    nc.vector.scalar_tensor_tensor(k.gall[:, G_NBE, :, :], k.gall[:, G_NBE, :, :], -1.0,
                                   k.gall[:, G_BETA, :, :], ALU.mult, ALU.mult).then_inc(*k.gate_dve.done("nbe"))
    dve.drain()



SCAN = ((2, 3, 0, 1), (3, 2, 1, 0))
DN_SCALE = P ** -0.5


def declare_gdn(k):
    ip, iv = inverse_steps(2)
    scan_pe = " ".join(" ".join(f"ks{t}{d}" for d in range(2) if t) + " " + " ".join(f"vn{t}{d}" for d in range(2))
                       + " " + " ".join(f"os{t}{d}" for d in range(2)) for t in range(4))
    scan_dve = " ".join(" ".join(f"r{t}{d}" for d in range(2) if t) + " " + " ".join(f"vn{t}{d}" for d in range(2))
                        + " " + " ".join(f"s{t}{d}" for d in range(2) if t < 3) for t in range(4))
    k.gdn_pe = Steps(k, "gdn_pe", f"pq pk pv pz ssq kk qk tk tv {ip} {scan_pe} oss")
    k.gdn_act = Steps(k, "gdn_act", "gam eg raw z silu norm ktok vb o0 onorm")
    k.gdn_dve = Steps(k, "gdn_dve", f"head gam conv sq unit at att qt {iv} {scan_dve} osq out")
    k.raw = view(k, 0, 3, 2, 260)
    k.cv = view(k, 1560, 4, 512)
    k.rows = view(k, 3608, 4, 512)
    k.gm = view(k, 5656, 2, 4, P)
    k.eg = view(k, 6680, 2, 512)
    k.at_ = view(k, 7704, 2, 4, P)
    k.att = view(k, 8728, 2, 4, P)
    k.pm = view(k, 9752, 2, 4, P)
    k.xi = view(k, 10776, 2, 4, P)
    k.xit = view(k, 11800, 2, 4, P)
    k.ktok = view(k, 12824, 4, P)
    k.vb = view(k, 13336, 2, 4, P)
    k.st = view(k, 14360, 2, P)
    k.rr = view(k, 14616, 2, P)
    k.vn = view(k, 14872, 2, P)
    k.vd = view(k, 15128, 2, P)
    k.os = view(k, 15384, 512)
    k.sq = view(k, 9752, 2, 512)
    k.rn = view(k, 10776, 2, 512)
    k.gh = k.small[:, 320:360].rearrange("p (q t d) -> p q t d", q=5, t=4)
    k.cw = k.small[:, 360:375].rearrange("p (a n) -> p a n", a=5)


def gdn_sync(k, sp):
    w = feature_rows(k.t["dn_w_in"][0])
    with sp.Fori(0, HEADS) as h:
        sp.wait_ge(*k.gdn_pe.at("pz", h - 1))
        for n in range(4):
            sp.dma_start(k.WH[:, n, :].rearrange("p (kb c) -> p kb c", kb=KB), w[:, :, ds(h * P + n * D, P)]
                         ).then_inc(k.d["head_w"], 16)


def gdn_gpsimd(k, pool):
    with pool.Fori(0, HEADS) as h:
        pool.wait_ge(*k.gdn_dve.at("at", h - 1))
        pool.wait_ge(*k.gdn_act.at("eg", h - 1))
        pool.dma_start(k.rows.rearrange("p a n -> p (a n)"),
                       k.grow.rearrange("h a n -> h (a n)")[ds(h, 1), :].rearrange("h n -> (h n)").partition_broadcast(P)
                       ).then_inc(k.d["gate_rows"], 16)


def gdn_tensor(k, pe):
    nc, ps, S, A, V = k.nc, k.PS, k.gdn_pe, k.gdn_act, k.gdn_dve
    q, kt = k.cv[:, 0, :], k.cv[:, 1, :]
    pe.wait_ge(*k.gate_act.at("rows"))
    with pe.Fori(0, HEADS) as h:
        pe.wait_ge(k.d["head_w"], h * 64 + 64)
        for n, name in enumerate(("pq", "pk", "pv", "pz")):
            w = k.WH[:, n, :].rearrange("p (kb c) -> p kb c", kb=KB)
            for kb in range(KB):
                mm = nc.tensor.matmul(ps[:, n, :], w[:, kb, :], k.XT[:, kb, :], start=kb == 0, stop=kb == KB - 1)
            mm.then_inc(*S.done(name))
        pe.wait_ge(*V.at("sq", h))
        for n in range(2):
            mm = nc.tensor.matmul(ps[:, n, :], mat(k, C_ONES), k.sq[:, n, :], start=True, stop=True)
        mm.then_inc(*S.done("ssq"))
        pe.wait_ge(*V.at("unit", h))
        for name, bank, rhs in (("kk", 0, kt), ("qk", 1, q)):
            for n in range(4):
                c = slice(n * P, (n + 1) * P)
                mm = nc.tensor.matmul(ps[:, bank, c], kt[:, c], rhs[:, c], start=True, stop=True)
            mm.then_inc(*S.done(name))
        for name, bank, src in (("tk", 2, kt), ("tv", 3, k.cv[:, 2, :])):
            for n in range(4):
                c = slice(n * P, (n + 1) * P)
                mm = nc.tensor.transpose(ps[:, bank, c], src[:, c], mat(k, C_ID))
            mm.then_inc(*S.done(name))
        pe.wait_ge(*V.at("at", h))
        pe.wait_ge(*V.at("att", h))
        inverse_tensor(k, pe, h, 2, S, V, lambda g, n: k.at_[:, g, n, :], k.xi, k.xit, k.pm, (4, 5), (6, 7), (0, 1))
        for t in range(4):
            for d in range(2):
                tile = SCAN[d][t]
                if t == 0:
                    pe.wait_ge(*A.at("vb", h))
                    pe.wait_ge(*V.at("qt", h))
                    continue
                pe.wait_ge(*V.at(f"s{t - 1}{d}", h))
                nc.tensor.matmul(ps[:, 2 + d, 0:P], kt[:, tile * P:(tile + 1) * P], k.st[:, d, :],
                                 start=True, stop=True).then_inc(*S.done(f"ks{t}{d}"))
            for d in range(2):
                tile = SCAN[d][t]
                if t:
                    pe.wait_ge(*V.at(f"r{t}{d}", h))
                pe.wait_ge(*V.at(f"x{LEVELS - 1}{d}", h))
                rhs = k.rr[:, d, :] if t else k.vb[:, d, tile, :]
                nc.tensor.matmul(ps[:, 2 + d, P:2 * P], k.xit[:, d, tile, :], rhs, start=True, stop=True
                                 ).then_inc(*S.done(f"vn{t}{d}"))
            for d in range(2):
                tile = SCAN[d][t]
                c = slice(tile * P, (tile + 1) * P)
                pe.wait_ge(*V.at(f"vn{t}{d}", h))
                if t:
                    nc.tensor.matmul(ps[:, 4 + d, c], k.st[:, d, :], k.eg[:, d, c], start=True, stop=False)
                nc.tensor.matmul(ps[:, 4 + d, c], k.vn[:, d, :], k.att[:, d, tile, :], start=t == 0, stop=True)
                nc.tensor.matmul(ps[:, 2 + d, 2 * P:3 * P], k.ktok[:, tile, :], k.vd[:, d, :],
                                 start=True, stop=True).then_inc(*S.done(f"os{t}{d}"))
        pe.wait_ge(*V.at("osq", h))
        nc.tensor.matmul(ps[:, 6, :], mat(k, C_ONES), k.pm[:, 0, :, :].rearrange("p a b -> p (a b)"),
                         start=True, stop=True).then_inc(*S.done("oss"))


def gdn_scalar(k, act):
    ps, S, T, V = k.PS, k.gdn_act, k.gdn_pe, k.gdn_dve
    with act.Fori(0, HEADS) as h:
        act.wait_ge(*V.at("out", h - 1))
        act.wait_ge(*V.at("gam", h))
        act.activation(k.gm[:, :, :, :].rearrange("p a b c -> p (a b c)"),
                       k.gm[:, :, :, :].rearrange("p a b c -> p (a b c)"), ACT.Exp).then_inc(*S.done("gam"))
        act.activation(k.eg[:, :, :], k.rows[:, 0:2, :], ACT.Exp).then_inc(*S.done("eg"))
        for n, name in enumerate(("pq", "pk", "pv")):
            act.wait_ge(*T.at(name, h))
            a = act.activation(k.raw[:, n, :, 2:258], ps[:, n, :].rearrange("p (s c) -> p s c", s=2), ACT.Copy)
        a.then_inc(*S.done("raw"))
        act.wait_ge(*T.at("pz", h))
        act.activation(k.cv[:, 3, :], ps[:, 3, :], ACT.Silu).then_inc(*S.done("z"))
        act.wait_ge(*V.at("conv", h))
        act.activation(k.cv[:, 0:3, :], k.cv[:, 0:3, :], ACT.Silu).then_inc(*S.done("silu"))
        act.wait_ge(*T.at("ssq", h))
        rsqrt(k, act, k.rn[:, :, :], ps[:, 0:2, :], 1.0, k.eps[:, E_RMS:E_RMS + 1]).then_inc(*S.done("norm"))
        act.wait_ge(*T.at("tk", h))
        act.activation(k.ktok[:, :, :], tiles_of(k, 2), ACT.Copy).then_inc(*S.done("ktok"))
        act.wait_ge(*T.at("tv", h))
        for d in range(2):
            for n in range(4):
                a = act.activation(k.vb[:, d, n, :], ps[:, 3, n * P:(n + 1) * P], ACT.Copy,
                                   scale=k.gh[:, G_BETA, n, d:d + 1])
        a.then_inc(*S.done("vb"))
        act.wait_ge(*T.at("os31", h))
        act.activation(k.os, ps[:, 4, :], ACT.Copy).then_inc(*S.done("o0"))
        act.wait_ge(*T.at("oss", h))
        rsqrt(k, act, k.rn[:, 0, :], ps[:, 6, :], 1.0 / P, k.eps[:, E_RMS:E_RMS + 1]).then_inc(*S.done("onorm"))


def gdn_vector(k, dve):
    nc, ps, S, T, A = k.nc, k.PS, k.gdn_dve, k.gdn_pe, k.gdn_act
    conv = k.vecs[:, 0, 0:120].rearrange("p (a n h) -> p a n h", a=5, n=3)
    gall = k.gall.rearrange("p q t (d h) -> p (q t d) h", d=2)
    dve.wait_ge(k.d["gate_store"], 16)
    nc.vector.memset(k.raw[:, :, :, 0:2], 0.0)
    nc.vector.memset(k.raw[:, :, :, 258:260], 0.0)
    dve.drain()
    with dve.Fori(0, HEADS) as h:
        nc.vector.tensor_copy(k.gh.rearrange("p q t d -> p (q t d)").unsqueeze(2), gall[:, :, ds(h, 1)])
        for a in range(5):
            nc.vector.tensor_copy(k.cw[:, a, :].unsqueeze(2), conv[:, a, :, ds(h, 1)])
        dve.drain().then_inc(*S.done("head"))
        dve.wait_ge(k.d["gate_rows"], h * 16 + 16)
        for d in range(2):
            for n in range(4):
                nc.vector.tensor_scalar(k.gm[:, d, n, :], k.rows[:, d, n * P:(n + 1) * P],
                                        k.gh[:, G_CUM, n, d:d + 1], 0.0, ALU.subtract, ALU.min)
        dve.drain().then_inc(*S.done("gam"))
        dve.wait_ge(*A.at("raw", h))
        for n in range(3):
            cv = k.cv[:, n, :].rearrange("p (s c) -> p s c", s=2)
            nc.vector.tensor_scalar(cv, k.raw[:, n, :, 0:L], k.cw[:, 0, n:n + 1], None, ALU.mult)
        for a in range(1, 5):
            dve.drain()
            for n in range(3):
                cv = k.cv[:, n, :].rearrange("p (s c) -> p s c", s=2)
                i = nc.vector.scalar_tensor_tensor(cv, k.raw[:, n, :, a:a + L], k.cw[:, a, n:n + 1], cv,
                                                   ALU.mult, ALU.add)
        i.then_inc(*S.done("conv"))
        dve.wait_ge(*A.at("silu", h))
        nc.vector.tensor_tensor(k.sq[:, :, :], k.cv[:, 0:2, :], k.cv[:, 0:2, :], ALU.mult).then_inc(*S.done("sq"))
        dve.wait_ge(*A.at("gam", h))
        for d, tri in ((0, C_UP), (1, C_LO)):
            nc.vector.tensor_tensor(k.gm[:, d, :, :], k.gm[:, d, :, :], bcast(mat(k, tri), 4), ALU.mult)
        dve.wait_ge(*A.at("norm", h))
        nc.vector.scalar_tensor_tensor(k.cv[:, 0, :], k.cv[:, 0, :], DN_SCALE, k.rn[:, 0, :], ALU.mult, ALU.mult)
        nc.vector.tensor_tensor(k.cv[:, 1, :], k.cv[:, 1, :], k.rn[:, 1, :], ALU.mult).then_inc(*S.done("unit"))
        dve.wait_ge(*T.at("kk", h))
        for d in range(2):
            nc.vector.tensor_tensor(k.at_[:, d, :, :], tiles_of(k, 0), k.gm[:, d, :, :], ALU.mult)
        dve.drain()
        i = nc.vector.tensor_tensor(k.at_.rearrange("p d n c -> p (d n c)"), k.at_.rearrange("p d n c -> p (d n c)"),
                                    k.rows[:, 2:4, :].rearrange("p d c -> p (d c)"), ALU.mult)
        i.then_inc(*S.done("at"))
        dve.wait_ge(*T.at("qk", h))
        for d in range(2):
            i = nc.vector.tensor_tensor(k.att[:, d, :, :], tiles_of(k, 1), k.gm[:, d, :, :], ALU.mult)
        i.then_inc(*S.done("att"))
        dve.wait_ge(*A.at("eg", h))
        for d in range(2):
            i = nc.vector.tensor_tensor(k.eg[:, d, :], k.eg[:, d, :], k.cv[:, 0, :], ALU.mult)
        i.then_inc(*S.done("qt"))
        inverse_vector(k, dve, h, 2, T, S, k.xi, k.xit, k.pm, (4, 5), (6, 7), (0, 1), (False, True))
        for t in range(4):
            for d in range(2):
                tile = SCAN[d][t]
                if t == 0:
                    continue
                dve.wait_ge(*T.at(f"ks{t}{d}", h))
                nc.vector.scalar_tensor_tensor(k.rr[:, d, :], ps[:, 2 + d, 0:P], k.gh[:, G_NBE, tile, d:d + 1],
                                               k.vb[:, d, tile, :], ALU.mult, ALU.add
                                               ).then_inc(*S.done(f"r{t}{d}"))
            for d in range(2):
                tile = SCAN[d][t]
                dve.wait_ge(*T.at(f"vn{t}{d}", h))
                nc.vector.tensor_copy(k.vn[:, d, :], ps[:, 2 + d, P:2 * P])
                nc.vector.tensor_scalar(k.vd[:, d, :], ps[:, 2 + d, P:2 * P], k.gh[:, G_KDEC, tile, d:d + 1],
                                        None, ALU.mult).then_inc(*S.done(f"vn{t}{d}"))
            for d in range(2 if t < 3 else 0):
                tile = SCAN[d][t]
                dve.wait_ge(*T.at(f"os{t}{d}", h))
                if t == 0:
                    i = nc.vector.tensor_copy(k.st[:, d, :], ps[:, 2 + d, 2 * P:3 * P])
                else:
                    i = nc.vector.scalar_tensor_tensor(k.st[:, d, :], k.st[:, d, :], k.gh[:, G_TOT, tile, d:d + 1],
                                                       ps[:, 2 + d, 2 * P:3 * P], ALU.mult, ALU.add)
                i.then_inc(*S.done(f"s{t}{d}"))
        dve.wait_ge(*A.at("o0", h))
        nc.vector.tensor_tensor(k.os, k.os, ps[:, 5, :], ALU.add)
        dve.drain()
        nc.vector.tensor_tensor(k.pm[:, 0, :, :].rearrange("p a b -> p (a b)"), k.os, k.os, ALU.mult
                                ).then_inc(*S.done("osq"))
        dve.wait_ge(*A.at("onorm", h))
        nc.vector.scalar_tensor_tensor(k.os, k.os, vec_col(k, 0, V_DN_G), k.rn[:, 0, :], ALU.mult, ALU.mult)
        dve.drain()
        nc.vector.tensor_tensor(k.OT[:, ds(h, 1), :].rearrange("p a n -> p (a n)"), k.os, k.cv[:, 3, :], ALU.mult
                                ).then_inc(*S.done("out"))



DA_SCALE = 64 ** -0.5


def declare_da(k):
    k.lam_dve = Steps(k, "lam_dve", "dots lam")
    k.lam_act = Steps(k, "lam_act", "exps")
    k.da_pe = Steps(k, "da_pe", "pq pk pv rot s00 s01 s10 s11 tr0 tr1 o oss")
    k.da_act = Steps(k, "da_act", "qk v p00 p01 p10 p11 pt0 pt1 o onorm")
    k.da_dve = Steps(k, "da_dve", "rope max rs a osq out")
    k.dq = view(k, 0, 256)
    k.dk = view(k, 256, 512)
    k.dv = view(k, 768, 4, P)
    k.dt1 = view(k, 1280, 512)
    k.dp = view(k, 1792, 2, 2, 512)
    k.da = view(k, 3840, 2, 512)
    k.dpt = view(k, 4864, 4, 256)
    k.do = view(k, 5888, 256)
    k.dsq = view(k, 6144, 256)
    k.drn = view(k, 6400, 256)
    k.lamr = view(k, 6656, 256)
    k.lamp = view(k, 6912, 2, 64)
    k.lam = k.small[:, 424:428]
    k.dag = k.small[:, 428:429]
    k.dmx, k.dnm, k.dsum, k.drs = (k.small[:, 432 + 4 * n:436 + 4 * n] for n in range(4))


def da_sync(k, sp):
    w = feature_rows(k.t["da_w_in"][0])
    with sp.Fori(0, HEADS) as h:
        sp.wait_ge(*k.da_pe.at("pv", h - 1))
        for n in range(3):
            sp.dma_start(k.WH[:, n, :].rearrange("p (kb c) -> p kb c", kb=KB), w[:, :, ds(h * P + n * D, P)]
                         ).then_inc(k.d["head_w"], 16)


def lam_gpsimd(k, pool):
    pool.dma_start(k.lamr, k.t["da_lambda"][0].rearrange("a n -> (a n)").partition_broadcast(P)
                   ).then_inc(k.d["lam_in"], 16)


def lam_vector(k, dve):
    nc = k.nc
    dve.wait_ge(k.d["lam_in"], 16)
    l = k.lamr.rearrange("p (a b n) -> p a b n", a=2, b=2)
    nc.vector.tensor_tensor(k.lamp, l[:, :, 0, :], l[:, :, 1, :], ALU.mult)
    dve.drain()
    nc.vector.tensor_reduce(k.lam[:, 0:2], k.lamp, AX, ALU.add).then_inc(*k.lam_dve.done("dots"))
    dve.wait_ge(*k.lam_act.at("exps"))
    nc.vector.tensor_tensor(k.lam[:, 2:3], k.lam[:, 0:1], k.lam[:, 1:2], ALU.subtract)
    dve.drain()
    nc.vector.tensor_scalar(k.lam[:, 3:4], k.lam[:, 2:3], LAMBDA_INIT, -1.0, ALU.add, ALU.mult)
    nc.vector.tensor_scalar(k.dag, vec_col(k, 0, V_DA_G), 1.0 - LAMBDA_INIT, None, ALU.mult
                            ).then_inc(*k.lam_dve.done("lam"))
    dve.drain()


def lam_scalar(k, act):
    act.wait_ge(*k.lam_dve.at("dots"))
    act.activation(k.lam[:, 0:2], k.lam[:, 0:2], ACT.Exp).then_inc(*k.lam_act.done("exps"))


def da_tensor(k, pe, loads):
    nc, ps, S, A, V = k.nc, k.PS, k.da_pe, k.da_act, k.da_dve
    w = [k.WH[:, n, :].rearrange("p (kb c) -> p kb c", kb=KB) for n in range(3)]
    with pe.Fori(0, HEADS) as h:
        pe.wait_ge(k.d["head_w"], h * 48 + (16 * loads + 48))
        pe.wait_ge(*V.at("out", h - 1))
        for kb in range(KB):
            mm = nc.tensor.matmul(ps[:, 0, 0:L], w[0][:, kb, :], k.XT[:, kb, 0:L], start=kb == 0, stop=kb == KB - 1)
        mm.then_inc(*S.done("pq"))
        for kb in range(KB):
            mm = nc.tensor.matmul(ps[:, 1, :], w[1][:, kb, :], k.XT[:, kb, :], start=kb == 0, stop=kb == KB - 1)
        mm.then_inc(*S.done("pk"))
        for n in range(4):
            for kb in range(KB):
                mm = nc.tensor.matmul(ps[:, 2, n * P:(n + 1) * P], k.XT[:, kb, n * P:(n + 1) * P], w[2][:, kb, :],
                                      start=kb == 0, stop=kb == KB - 1)
        mm.then_inc(*S.done("pv"))
        pe.wait_ge(*A.at("qk", h))
        nc.tensor.matmul(ps[:, 3, 0:L], mat(k, C_RDA), k.dq, start=True, stop=True)
        nc.tensor.matmul(ps[:, 3, L:2 * L], mat(k, C_RDA), k.dk[:, 0:L], start=True, stop=True
                         ).then_inc(*S.done("rot"))
        pe.wait_ge(*V.at("rope", h))
        for c in range(2):
            r = slice(64 * c, 64 * c + 64)
            for q in range(2):
                nc.tensor.matmul(ps[:, 4 + 2 * c + q, :], k.dq[r, q * P:(q + 1) * P], k.dk[r, :],
                                 start=True, stop=True).then_inc(*S.done(f"s{c}{q}"))
        pe.wait_ge(*V.at("a", h))
        pe.wait_ge(*A.at("v", h))
        for half in range(2):
            for n in range(2):
                for q in range(2):
                    at = (2 * half + n) * P
                    mm = nc.tensor.transpose(ps[:, half, n * L + q * P:n * L + (q + 1) * P],
                                             k.da[:, q, at:at + P], mat(k, C_ID))
            mm.then_inc(*S.done(f"tr{half}"))
        pe.wait_ge(*A.at("pt1", h))
        for n in range(4):
            mm = nc.tensor.matmul(ps[:, 2, 0:L], k.dv[:, n, :], k.dpt[:, n, :], start=n == 0, stop=n == 3)
        mm.then_inc(*S.done("o"))
        pe.wait_ge(*V.at("osq", h))
        nc.tensor.matmul(ps[:, 3, 0:L], mat(k, C_ONES), k.dsq, start=True, stop=True).then_inc(*S.done("oss"))


def da_scalar(k, act):
    ps, S, T, V = k.PS, k.da_act, k.da_pe, k.da_dve
    with act.Fori(0, HEADS) as h:
        act.wait_ge(*T.at("pq", h))
        act.activation(k.dq, ps[:, 0, 0:L], ACT.Copy)
        act.wait_ge(*T.at("pk", h))
        act.activation(k.dk, ps[:, 1, :], ACT.Copy)
        act.drain().then_inc(*S.done("qk"))
        act.wait_ge(*T.at("pv", h))
        act.activation(k.dv, tiles_of(k, 2), ACT.Copy).then_inc(*S.done("v"))
        act.wait_ge(*V.at("max", h))
        for c in range(2):
            for q in range(2):
                i = 2 * c + q
                act.activation(k.dp[:, c, q, :], ps[:, 4 + i, :], ACT.Exp, scale=DA_SCALE,
                               bias=k.dnm[:, i:i + 1], accum_out=k.dsum[:, i:i + 1])
                act.drain().then_inc(*S.done(f"p{c}{q}"))
        for half in range(2):
            act.wait_ge(*T.at(f"tr{half}", h))
            act.activation(k.dpt[:, 2 * half:2 * half + 2, :], ps[:, half, :].rearrange("p (n c) -> p n c", n=2),
                           ACT.Copy).then_inc(*S.done(f"pt{half}"))
        act.wait_ge(*T.at("o", h))
        act.activation(k.do, ps[:, 2, 0:L], ACT.Copy).then_inc(*S.done("o"))
        act.wait_ge(*T.at("oss", h))
        rsqrt(k, act, k.drn, ps[:, 3, 0:L], 1.0 / P, k.eps[:, E_RMS:E_RMS + 1]).then_inc(*S.done("onorm"))


def rope_vector(k, dve, x, rot, table, tmp):
    nc = k.nc
    n = x.shape[0]
    nc.vector.tensor_tensor(tmp, rot, k.rope[0:n, table, 1, :], ALU.mult)
    nc.vector.tensor_tensor(x, x, k.rope[0:n, table, 0, :], ALU.mult)
    dve.drain()
    return nc.vector.tensor_tensor(x, x, tmp, ALU.add)


def da_vector(k, dve):
    nc, ps, S, T, A = k.nc, k.PS, k.da_dve, k.da_pe, k.da_act
    with dve.Fori(0, HEADS) as h:
        dve.wait_ge(*T.at("rot", h))
        dve.wait_ge(*A.at("qk", h))
        rope_vector(k, dve, k.dq, ps[:, 3, 0:L], T_DA, k.dt1[:, 0:L])
        rope_vector(k, dve, k.dk[:, 0:L], ps[:, 3, L:2 * L], T_DA, k.dt1[:, L:2 * L])
        dve.drain().then_inc(*S.done("rope"))
        for c in range(2):
            for q in range(2):
                dve.wait_ge(*T.at(f"s{c}{q}", h))
                nc.vector.reduce_max(k.dmx[:, 2 * c + q:2 * c + q + 1], ps[:, 4 + 2 * c + q, :], AX)
        dve.drain()
        nc.vector.tensor_scalar(k.dnm, k.dmx, -DA_SCALE, None, ALU.mult).then_inc(*S.done("max"))
        dve.wait_ge(*A.at("p11", h))
        nc.vector.reciprocal(k.drs, k.dsum)
        dve.drain()
        nc.vector.tensor_scalar(k.drs[:, 2:4], k.drs[:, 2:4], k.lam[:, 3:4], None, ALU.mult).then_inc(*S.done("rs"))
        dve.drain()
        for q in range(2):
            nc.vector.tensor_scalar(k.da[:, q, :], k.dp[:, 0, q, :], k.drs[:, q:q + 1], None, ALU.mult)
        dve.drain()
        for q in range(2):
            i = nc.vector.scalar_tensor_tensor(k.da[:, q, :], k.dp[:, 1, q, :], k.drs[:, 2 + q:3 + q], k.da[:, q, :],
                                               ALU.mult, ALU.add)
        i.then_inc(*S.done("a"))
        dve.wait_ge(*A.at("o", h))
        nc.vector.tensor_tensor(k.dsq, k.do, k.do, ALU.mult).then_inc(*S.done("osq"))
        dve.wait_ge(*A.at("onorm", h))
        nc.vector.scalar_tensor_tensor(k.OT[:, ds(h, 1), 0:L].rearrange("p a n -> p (a n)"), k.do, k.dag, k.drn,
                                       ALU.mult, ALU.mult).then_inc(*S.done("out"))



def attn_steps():
    return ("s0 s1 tr0 tr1 o0 o1", "p0 p1 pt0 pt1 o", "m0 m1 w0 w1")


def declare_attn(k):
    k.aq = view(k, 8192, 2, 256)
    k.ak = view(k, 8704, 2, 256)
    k.av = view(k, 9216, 2, P)
    k.asc = view(k, 9472, 2, 384)
    k.apt = view(k, 10240, 2, 384)
    k.atm = view(k, 11008, 512)
    k.amx, k.asum = k.small[:, 448:452], k.small[:, 452:456]
    k.ars = k.small[:, 456:460]


QCOLS = (slice(0, P), slice(P, 3 * P))


def attn_tensor(k, pe, rnd, S, A, V, q, kk, v):
    nc, ps = k.nc, k.PS
    for hh in range(2):
        nc.tensor.matmul(ps[:, 4 + hh, QCOLS[0]], q(hh)[:, 0:P], kk(hh)[:, 0:P], start=True, stop=True)
        nc.tensor.matmul(ps[:, 4 + hh, QCOLS[1]], q(hh)[:, P:L], kk(hh)[:, 0:L], start=True, stop=True
                         ).then_inc(*S.done(f"s{hh}"))
    for hh in range(2):
        pe.wait_ge(*V.at(f"w{hh}", rnd))
        for n in range(3):
            mm = nc.tensor.transpose(ps[:, 6 + hh, n * P:(n + 1) * P], k.asc[:, hh, n * P:(n + 1) * P], mat(k, C_ID))
        mm.then_inc(*S.done(f"tr{hh}"))
    for hh in range(2):
        pe.wait_ge(*A.at(f"pt{hh}", rnd))
        o = ps[64 * hh:64 * hh + 64, 3, :]
        nc.tensor.matmul(o[:, 0:P], v(hh, 0), k.apt[:, hh, 0:P], start=True, stop=True)
        nc.tensor.matmul(o[:, P:L], v(hh, 0), k.apt[:, hh, P:2 * P], start=True, stop=False)
        nc.tensor.matmul(o[:, P:L], v(hh, 1), k.apt[:, hh, 2 * P:3 * P], start=False, stop=True
                         ).then_inc(*S.done(f"o{hh}"))


def attn_scalar(k, act, rnd, S, T, V, block):
    ps = k.PS
    for hh in range(2):
        act.wait_ge(*V.at(f"m{hh}", rnd))
        for q in range(2):
            i = 2 * hh + q
            act.activation(k.asc[:, hh, QCOLS[q]], k.asc[:, hh, QCOLS[q]], ACT.Exp, bias=k.amx[:, i:i + 1],
                           accum_out=k.asum[:, i:i + 1])
        act.drain().then_inc(*S.done(f"p{hh}"))
    for hh in range(2):
        act.wait_ge(*T.at(f"tr{hh}", rnd))
        act.activation(k.apt[:, hh, :], ps[:, 6 + hh, 0:384], ACT.Copy).then_inc(*S.done(f"pt{hh}"))
    act.wait_ge(*T.at("o0", rnd))
    act.wait_ge(*T.at("o1", rnd))
    act.activation(block, ps[:, 3, 0:L], ACT.Copy).then_inc(*S.done("o"))


def attn_vector(k, dve, rnd, S, T, A, scale, decay=None):
    nc, ps = k.nc, k.PS
    mask = k.mask.rearrange("p a b -> p (a b)")
    for hh in range(2):
        dve.wait_ge(*T.at(f"s{hh}", rnd))
        nc.vector.scalar_tensor_tensor(k.asc[:, hh, :], ps[:, 4 + hh, 0:384], scale, mask, ALU.mult, ALU.add)
        if decay:
            col, row = decay(hh)
            dve.drain()
            for q in range(2):
                sc = k.asc[:, hh, QCOLS[q]]
                nc.vector.scalar_tensor_tensor(sc, sc, col(q), row[:, 0:(q + 1) * P], ALU.add, ALU.subtract)
        dve.drain()
        for q in range(2):
            i = 2 * hh + q
            nc.vector.reduce_max(k.amx[:, i:i + 1], k.asc[:, hh, QCOLS[q]], AX)
        dve.drain()
        nc.vector.tensor_scalar(k.amx[:, 2 * hh:2 * hh + 2], k.amx[:, 2 * hh:2 * hh + 2], -1.0, None, ALU.mult
                                ).then_inc(*S.done(f"m{hh}"))
    for hh in range(2):
        dve.wait_ge(*A.at(f"p{hh}", rnd))
        nc.vector.reciprocal(k.ars[:, 2 * hh:2 * hh + 2], k.asum[:, 2 * hh:2 * hh + 2])
        dve.drain()
        for q in range(2):
            sc, i = k.asc[:, hh, QCOLS[q]], 2 * hh + q
            nc.vector.tensor_scalar(sc, sc, k.ars[:, i:i + 1], None, ALU.mult)
        dve.drain().then_inc(*S.done(f"w{hh}"))



RW_DECAY = -math.exp(-0.5)


def declare_rw(k):
    k.rwl_pe = Steps(k, "rwl_pe", "p")
    k.rwl_act = Steps(k, "rwl_act", "raw funcs")
    k.rwl_dve = Steps(k, "rwl_dve", "mix")
    ip, iv = inverse_steps(1)
    k.rw_pe = Steps(k, "rw_pe", f"rk vw ag ssk bo m0 m1 tr {ip} rn00 rn01 u00 u01 z rn10 rn11 u10 u11 y mean var")
    k.rw_act = Steps(k, "rw_act", "raw w a g knorm ws tok y gnorm")
    k.rw_dve = Steps(k, "rw_dve", f"head mix ksq kmax cum bo til ab {iv} rn00 rn01 u00 u01 z rn10 rn11 u10 u11 "
                                  "ysq out")
    k.raw3 = view(k, 0, 3, 257)
    k.rkv = view(k, 800, 3, 256)
    k.lw = view(k, 1568, 2, 256)
    k.l2 = view(k, 2080, 2, P)
    k.ld, k.ra, k.kk, k.k2, k.rb, k.cum = (view(k, 2336 + 256 * n, 256) for n in range(6))
    k.wt, k.wi, k.wp, k.rt, k.kt, k.bt, k.kap, k.rsq, k.rtm = (view(k, 3872 + 256 * n, 256) for n in range(9))
    k.ab = view(k, 6176, 2, 4, P)
    k.rbk = view(k, 7200, 2, 4, P)
    k.rxi, k.rxit, k.rp = (view(k, 8224 + 512 * n, 1, 4, P) for n in range(3))
    k.tok = view(k, 9760, 3, 2, P)
    k.rrn, k.ru = view(k, 10528, 2, 64), view(k, 10656, 2, 64)
    k.z = view(k, 10784, 64)
    k.y, k.rg, k.bon = (view(k, 10848 + 256 * n, 256) for n in range(3))
    k.lraw = view(k, 11616, 2, 257)
    k.lorw = view(k, 12288, KB, 256)
    k.rv = k.small[:, 376:386]
    k.oka, k.nmid, k.fz = k.small[:, 386:387], k.small[:, 388:390], k.small[:, 390:391]


R_MU, R_W0, R_A0, R_KK, R_KA, R_RK, R_G, R_B = 0, 3, 4, 5, 6, 7, 8, 9


def rwl_gpsimd(k, pool, ready):
    for w in ready:
        pool.wait_ge(*w)
    pool.dma_start(k.lorw, feature_rows(k.t["w_in_0_2"])[:, :, 1536:RW_COLS]).then_inc(k.d["lat_w"], 16)


def rwl_tensor(k, pe):
    nc = k.nc
    pe.wait_ge(k.d["lat_w"], 16)
    for n in range(2):
        for kb in range(KB):
            mm = nc.tensor.matmul(k.PS[:, n, 0:L], k.lorw[:, kb, n * P:(n + 1) * P], k.XT[:, kb, 0:L],
                                  start=kb == 0, stop=kb == KB - 1)
    mm.then_inc(*k.rwl_pe.done("p"))


def rwl_scalar(k, act):
    act.wait_ge(*k.rwl_pe.at("p"))
    act.activation(k.lraw[:, :, 1:257], k.PS[:, 0:2, 0:L], ACT.Copy).then_inc(*k.rwl_act.done("raw"))
    act.wait_ge(*k.rwl_dve.at("mix"))
    act.activation(k.lw[0:64, 0, :], k.lw[0:64, 0, :], ACT.Tanh)
    act.activation(k.lw[:, 1, :], k.lw[:, 1, :], ACT.Sigmoid)
    act.drain().then_inc(*k.rwl_act.done("funcs"))


def rwl_vector(k, dve):
    nc = k.nc
    nc.vector.memset(k.lraw[:, :, 0:1], 0.0)
    nc.vector.memset(k.raw3[:, :, 0:1], 0.0)
    dve.wait_ge(*k.rwl_act.at("raw"))
    dve.drain()
    nc.vector.tensor_tensor(k.lw, k.lraw[:, :, 0:L], k.lraw[:, :, 1:257], ALU.subtract)
    dve.drain()
    for n in range(2):
        nc.vector.scalar_tensor_tensor(k.lw[:, n, :], k.lw[:, n, :], vec_col(k, 0, V_MUW + n),
                                       k.lraw[:, n, 1:257], ALU.mult, ALU.add)
    dve.drain().then_inc(*k.rwl_dve.done("mix"))



def rw_sync(k, sp):
    t = k.t
    w = feature_rows(t["w_in_0_2"])
    with sp.Fori(0, PAIRS) as p:
        sp.wait_ge(*k.rw_pe.at("ag", p - 1))
        for n in range(3):
            sp.dma_start(k.WH[:, n, :].rearrange("p (kb c) -> p kb c", kb=KB), w[:, :, ds(p * P + n * 512, P)]
                         ).then_inc(k.d["head_w"], 16)
        for to, name in ((k.l2[0:64, 0, :], "rw_w2_0_2"), (k.l2[64:128, 0, :], "rw_a2_0_2"),
                         (k.l2[:, 1, :], "rw_g2_0_2")):
            sp.dma_start(to, t[name][:, ds(p * P, P)]).then_inc(k.d["lora_w"], 16)


def rw_tensor(k, pe, loads):
    nc, ps, S, A, V = k.nc, k.PS, k.rw_pe, k.rw_act, k.rw_dve
    w = [k.WH[:, n, :].rearrange("p (kb c) -> p kb c", kb=KB) for n in range(3)]
    rows = [slice(0, 64), slice(64, 128)]
    tcol = [slice(0, P), slice(P, 2 * P)]

    def unit(buf, hh, m, tile):
        return buf[:, hh, 2 * m + tile, :]

    pe.wait_ge(*k.rwl_act.at("funcs"))
    with pe.Fori(0, PAIRS) as p:
        pe.wait_ge(k.d["head_w"], p * 48 + (16 * loads + 48))
        pe.wait_ge(k.d["lora_w"], p * 48 + 48)
        pe.wait_ge(*V.at("out", p - 1))
        for n, bank, c in ((0, 0, 0), (1, 0, L), (2, 1, 0)):
            for kb in range(KB):
                mm = nc.tensor.matmul(ps[:, bank, c:c + L], w[n][:, kb, :], k.XT[:, kb, 0:L],
                                      start=kb == 0, stop=kb == KB - 1)
            if n == 1:
                mm.then_inc(*S.done("rk"))
        nc.tensor.matmul(ps[:, 1, L:2 * L], k.l2[0:64, 0, :], k.lw[0:64, 0, :], start=True, stop=True
                         ).then_inc(*S.done("vw"))
        nc.tensor.matmul(ps[:, 2, 0:L], k.l2[64:128, 0, :], k.lw[64:128, 0, :], start=True, stop=True)
        nc.tensor.matmul(ps[:, 2, L:2 * L], k.l2[:, 1, :], k.lw[:, 1, :], start=True, stop=True
                         ).then_inc(*S.done("ag"))
        pe.wait_ge(*V.at("ksq", p))
        nc.tensor.matmul(ps[:, 3, 0:L], mat(k, C_ONES64), k.rsq, start=True, stop=True).then_inc(*S.done("ssk"))
        pe.wait_ge(*V.at("bo", p))
        nc.tensor.matmul(ps[:, 3, L:2 * L], mat(k, C_ONES64), k.bon, start=True, stop=True).then_inc(*S.done("bo"))
        pe.wait_ge(*V.at("til", p))
        for hh in range(2):
            r = rows[hh]
            for rhs, bank in ((k.kap, 4 + 2 * hh), (k.rt, 5 + 2 * hh)):
                for m, lhs in ((0, k.bt), (1, k.kt)):
                    for tile in range(2):
                        c = (2 * m + tile) * P
                        mm = nc.tensor.matmul(ps[:, bank, c:c + P], lhs[r, tcol[tile]], rhs[r, tcol[tile]],
                                              start=True, stop=True)
            mm.then_inc(*S.done(f"m{hh}"))
        for n, src in enumerate((k.rkv[:, 2, :], k.bt, k.kt)):
            for tile in range(2):
                c = (2 * n + tile) % 4 * P
                mm = nc.tensor.transpose(ps[:, n // 2, c:c + P], src[:, tcol[tile]], mat(k, C_ID))
        mm.then_inc(*S.done("tr"))
        pe.wait_ge(*V.at("ab", p))
        inverse_tensor(k, pe, p, 1, S, V, lambda g, n: unit(k.ab, n // 2, 0, n % 2), k.rxi, k.rxit, k.rp,
                       (4,), (5,), (6,))
        pe.wait_ge(*A.at("tok", p))
        for tile in range(2):
            for hh in range(2):
                r = rows[hh]
                if tile:
                    pe.wait_ge(*V.at("z", p))
                    nc.tensor.matmul(ps[:, hh, 0:64], k.kap[r, tcol[tile]], k.z[r, :], start=True, stop=False)
                nc.tensor.matmul(ps[:, hh, 0:64], unit(k.ab, hh, 1, tile), k.tok[:, 0, tile, r],
                                 start=tile == 0, stop=True).then_inc(*S.done(f"rn{tile}{hh}"))
            for hh in range(2):
                pe.wait_ge(*V.at(f"rn{tile}{hh}", p))
                pe.wait_ge(*V.at(f"x{LEVELS - 1}0", p))
                nc.tensor.matmul(ps[:, hh, 64:128], k.rxit[:, 0, 2 * hh + tile, :], k.rrn[:, hh, :],
                                 start=True, stop=True).then_inc(*S.done(f"u{tile}{hh}"))
            for hh in range(2):
                r = rows[hh]
                pe.wait_ge(*V.at(f"u{tile}{hh}", p))
                nc.tensor.matmul(ps[r, 2, tcol[tile]], k.ru[:, hh, :], unit(k.rbk, hh, 0, tile),
                                 start=True, stop=False)
                if tile:
                    nc.tensor.matmul(ps[r, 2, tcol[tile]], k.z[r, :], k.rt[r, tcol[tile]], start=False, stop=False)
                mm = nc.tensor.matmul(ps[r, 2, tcol[tile]], k.tok[:, 0, tile, r], unit(k.rbk, hh, 1, tile),
                                      start=False, stop=True)
                if tile == 0:
                    nc.tensor.matmul(ps[r, 7, 0:64], k.tok[:, 1, tile, r], k.ru[:, hh, :], start=True, stop=False)
                    mm = nc.tensor.matmul(ps[r, 7, 0:64], k.tok[:, 2, tile, r], k.tok[:, 0, tile, r],
                                          start=False, stop=True)
            mm.then_inc(*S.done("y" if tile else "z"))
        pe.wait_ge(*A.at("y", p))
        nc.tensor.matmul(ps[:, 0, 0:L], mat(k, C_ONES64), k.y, start=True, stop=True).then_inc(*S.done("mean"))
        pe.wait_ge(*V.at("ysq", p))
        nc.tensor.matmul(ps[:, 1, 0:L], mat(k, C_ONES64), k.rsq, start=True, stop=True).then_inc(*S.done("var"))


def rw_scalar(k, act):
    ps, S, T, V = k.PS, k.rw_act, k.rw_pe, k.rw_dve
    with act.Fori(0, PAIRS) as p:
        act.wait_ge(*T.at("rk", p))
        act.activation(k.raw3[:, 0:2, 1:257], ps[:, 0, :].rearrange("p (n c) -> p n c", n=2), ACT.Copy)
        act.wait_ge(*T.at("vw", p))
        act.activation(k.raw3[:, 2, 1:257], ps[:, 1, 0:L], ACT.Copy)
        act.drain().then_inc(*S.done("raw"))
        act.wait_ge(*V.at("head", p))
        act.activation(k.ld, ps[:, 1, L:2 * L], ACT.Sigmoid, bias=k.rv[:, R_W0:R_W0 + 1]).then_inc(*S.done("w"))
        act.wait_ge(*T.at("ag", p))
        act.activation(k.ra, ps[:, 2, 0:L], ACT.Sigmoid, bias=k.rv[:, R_A0:R_A0 + 1]).then_inc(*S.done("a"))
        act.activation(k.rg, ps[:, 2, L:2 * L], ACT.Copy).then_inc(*S.done("g"))
        act.wait_ge(*V.at("kmax", p))
        act.activation(k.rtm, k.rtm, ACT.Ln, scale=float(2 ** GUARD_LOG2))
        act.drain()
        act.activation(k.rtm, k.rtm, ACT.Exp, scale=-0.5, bias=k.eps[:, E_SHIFT:E_SHIFT + 1]
                       ).then_inc(*S.done("knorm"))
        act.wait_ge(*V.at("cum", p))
        for tile in range(2):
            c = slice(tile * P, (tile + 1) * P)
            mid = k.cum[:, tile * P + 63:tile * P + 64]
            act.activation(k.wt[:, c], k.cum[:, c], ACT.Exp, bias=k.nmid[:, tile:tile + 1])
            act.activation(k.wi[:, c], k.cum[:, c], ACT.Exp, scale=-1.0, bias=mid)
            act.activation(k.wp[:, c], k.wp[:, c], ACT.Exp, bias=k.nmid[:, tile:tile + 1])
        act.activation(k.fz, k.fz, ACT.Exp)
        act.drain().then_inc(*S.done("ws"))
        act.wait_ge(*T.at("tr", p))
        act.activation(k.tok[:, 0:2, :, :].rearrange("p a b c -> p (a b c)"), ps[:, 0, :], ACT.Copy)
        act.activation(k.tok[:, 2, :, :].rearrange("p b c -> p (b c)"), ps[:, 1, 0:L], ACT.Copy)
        act.drain().then_inc(*S.done("tok"))
        act.wait_ge(*T.at("y", p))
        act.activation(k.y, ps[:, 2, 0:L], ACT.Copy).then_inc(*S.done("y"))
        act.wait_ge(*T.at("var", p))
        rsqrt(k, act, k.rtm, ps[:, 1, 0:L], 1.0 / 64, k.eps[:, E_GN:E_GN + 1]).then_inc(*S.done("gnorm"))


def rw_vector(k, dve):
    nc, ps, S, T, A = k.nc, k.PS, k.rw_dve, k.rw_pe, k.rw_act
    tt, ts, stt = nc.vector.tensor_tensor, nc.vector.tensor_scalar, nc.vector.scalar_tensor_tensor
    vecs = k.vecs[:, 1, 0:40].rearrange("p (a n) -> p a n", n=4)
    rv = lambda c: k.rv[:, c:c + 1]
    r, kk_, v = (k.rkv[:, n, :] for n in range(3))
    with dve.Fori(0, PAIRS) as p:
        nc.vector.tensor_copy(k.rv.unsqueeze(2), vecs[:, :, ds(p, 1)])
        dve.drain()
        ts(k.oka, rv(R_KA), -1.0, 1.0, ALU.mult, ALU.add)
        dve.drain().then_inc(*S.done("head"))
        dve.wait_ge(*A.at("raw", p))
        tt(k.rkv, k.raw3[:, :, 0:L], k.raw3[:, :, 1:257], ALU.subtract)
        dve.drain()
        for n in range(3):
            stt(k.rkv[:, n, :], k.rkv[:, n, :], rv(R_MU + n), k.raw3[:, n, 1:257], ALU.mult, ALU.add)
        dve.drain().then_inc(*S.done("mix"))
        ts(k.kk, kk_, rv(R_KK), None, ALU.mult)
        dve.drain()
        tt(k.rsq, k.kk, k.kk, ALU.mult).then_inc(*S.done("ksq"))
        dve.wait_ge(*T.at("ssk", p))
        ts(k.rtm, ps[:, 3, 0:L], 1e-24, None, ALU.max).then_inc(*S.done("kmax"))
        dve.wait_ge(*A.at("a", p))
        ts(k.ld, k.ld, RW_DECAY, None, ALU.mult)
        ts(k.k2, k.ra, rv(R_KA), k.oka, ALU.mult, ALU.add)
        dve.drain()
        for tile in range(2):
            c = slice(tile * P, (tile + 1) * P)
            nc.vector.tensor_tensor_scan(k.cum[:, c], mat(k, C_ONES), k.ld[:, c], 0.0, ALU.mult, ALU.add)
        tt(k.k2, k.k2, kk_, ALU.mult)
        dve.drain()
        tt(k.wp, k.cum, k.ld, ALU.subtract)
        for tile in range(2):
            ts(k.nmid[:, tile:tile + 1], k.cum[:, tile * P + 63:tile * P + 64], -1.0, None, ALU.mult)
        ts(k.fz, k.cum[:, 127:128], k.cum[:, 63:64], k.cum[:, P + 63:P + 64], ALU.subtract, ALU.add)
        dve.drain().then_inc(*S.done("cum"))
        stt(k.bon, r, rv(R_RK), k.k2, ALU.mult, ALU.mult).then_inc(*S.done("bo"))
        dve.wait_ge(*A.at("knorm", p))
        tt(k.kk, k.kk, k.rtm, ALU.mult)
        dve.drain()
        tt(k.rb, k.kk, k.ra, ALU.mult)
        dve.drain()
        dve.wait_ge(*A.at("ws", p))
        tt(k.rt, r, k.wt, ALU.mult)
        tt(k.kap, k.kk, k.wp, ALU.mult)
        tt(k.bt, k.rb, k.wi, ALU.mult)
        tt(k.kt, k.k2, k.wi, ALU.mult)
        dve.drain().then_inc(*S.done("til"))
        dve.wait_ge(*T.at("bo", p))
        tt(k.bon, v, ps[:, 3, L:2 * L], ALU.mult)
        for hh in range(2):
            dve.wait_ge(*T.at(f"m{hh}", p))
            tt(k.ab[:, hh, :, :], tiles_of(k, 4 + 2 * hh), bcast(mat(k, C_SUP), 4), ALU.mult)
            i = tt(k.rbk[:, hh, :, :], tiles_of(k, 5 + 2 * hh), bcast(mat(k, C_UP), 4), ALU.mult)
        i.then_inc(*S.done("ab"))
        inverse_vector(k, dve, p, 1, T, S, k.rxi, k.rxit, k.rp, (4,), (5,), (6,), (False,))
        for tile in range(2):
            for hh in range(2):
                dve.wait_ge(*T.at(f"rn{tile}{hh}", p))
                ts(k.rrn[:, hh, :], ps[:, hh, 0:64], -1.0, None, ALU.mult).then_inc(*S.done(f"rn{tile}{hh}"))
            for hh in range(2):
                dve.wait_ge(*T.at(f"u{tile}{hh}", p))
                nc.vector.tensor_copy(k.ru[:, hh, :], ps[:, hh, 64:128]).then_inc(*S.done(f"u{tile}{hh}"))
            if tile == 0:
                dve.wait_ge(*T.at("z", p))
                ts(k.z, ps[:, 7, 0:64], k.fz, None, ALU.mult).then_inc(*S.done("z"))
        dve.wait_ge(*T.at("mean", p))
        stt(k.y, ps[:, 0, 0:L], -1.0 / 64, k.y, ALU.mult, ALU.add)
        dve.drain()
        tt(k.rsq, k.y, k.y, ALU.mult).then_inc(*S.done("ysq"))
        dve.wait_ge(*A.at("gnorm", p))
        tt(k.y, k.y, k.rtm, ALU.mult)
        dve.drain()
        ts(k.y, k.y, rv(R_G), rv(R_B), ALU.mult, ALU.add)
        dve.drain()
        tt(k.y, k.y, k.bon, ALU.add)
        dve.drain()
        tt(k.OT[:, ds(p, 1), 0:L].rearrange("p a n -> p (a n)"), k.y, k.rg, ALU.mult).then_inc(*S.done("out"))



QN = 2
MLA_SCALE = MLA_QK ** -0.5


def declare_mla(k):
    k.lat_pe = Steps(k, "lat_pe", "p ss rot")
    k.lat_act = Steps(k, "lat_act", "copy norm")
    k.lat_dve = Steps(k, "lat_dve", "sq out")
    a_pe, a_act, a_dve = attn_steps()
    k.mla_pe = Steps(k, "mla_pe", f"p rot {a_pe}")
    k.mla_act = Steps(k, "mla_act", f"copy {a_act}")
    k.mla_dve = Steps(k, "mla_dve", f"rope {a_dve}")
    k.latw = view(k, 12288, KB, 416)
    k.ql = view(k, 0, 3, 256)
    k.qsq = view(k, 768, 3, 256)
    k.qrn = view(k, 1536, 2, 256)
    k.wq = view(k, 2048, QN, 192)
    k.wkv = view(k, 2432, 256)
    k.kpe, k.kpt = view(k, 2688, 256), view(k, 2944, 256)


def lat_gpsimd(k, pool, ready):
    for w in ready:
        pool.wait_ge(*w)
    pool.dma_start(k.latw, feature_rows(k.t["w_in_0_2"])[:, :, RW_COLS:RW_COLS + 416]).then_inc(k.d["lat_w"], 16)


def lat_tensor(k, pe):
    nc, ps = k.nc, k.PS
    pe.wait_ge(k.d["lat_w"], 32)
    for out, c, n in ((ps[:, 0, 0:L], 0, P), (ps[:, 0, L:2 * L], P, P), (ps[:, 1, 0:L], 2 * P, P),
                      (ps[64:96, 1, L:2 * L], 3 * P, 32)):
        for kb in range(KB):
            mm = nc.tensor.matmul(out, k.latw[:, kb, c:c + n], k.XT[:, kb, 0:L], start=kb == 0, stop=kb == KB - 1)
    mm.then_inc(*k.lat_pe.done("p"))
    pe.wait_ge(*k.lat_dve.at("sq"))
    for n in range(QN):
        nc.tensor.matmul(ps[:, 2, 0:L], mat(k, C_ONES), k.qsq[:, n, :], start=n == 0, stop=n == QN - 1)
    nc.tensor.matmul(ps[:, 2, L:2 * L], mat(k, C_ONES), k.qsq[:, 2, :], start=True, stop=True
                     ).then_inc(*k.lat_pe.done("ss"))
    nc.tensor.matmul(ps[64:96, 3, 0:L], k.mats[64:96, C_RMLA, 64:96], k.kpe[64:96, :], start=True, stop=True
                     ).then_inc(*k.lat_pe.done("rot"))


def lat_scalar(k, act):
    ps = k.PS
    act.wait_ge(*k.lat_pe.at("p"))
    act.activation(k.ql[:, 0:2, :].rearrange("p a b -> p (a b)"), ps[:, 0, :], ACT.Copy)
    act.activation(k.ql[:, 2, :], ps[:, 1, 0:L], ACT.Copy)
    act.activation(k.kpe[64:96, :], ps[64:96, 1, L:2 * L], ACT.Copy)
    act.drain().then_inc(*k.lat_act.done("copy"))
    act.wait_ge(*k.lat_pe.at("ss"))
    rsqrt(k, act, k.qrn[:, 0, :], ps[:, 2, 0:L], 1.0 / (QN * P), k.eps[:, E_RMS:E_RMS + 1])
    rsqrt(k, act, k.qrn[:, 1, :], ps[:, 2, L:2 * L], 1.0 / P, k.eps[:, E_RMS:E_RMS + 1])
    act.drain().then_inc(*k.lat_act.done("norm"))


def lat_vector(k, dve):
    nc, ps = k.nc, k.PS
    dve.wait_ge(*k.lat_act.at("copy"))
    nc.vector.tensor_tensor(k.qsq, k.ql, k.ql, ALU.mult).then_inc(*k.lat_dve.done("sq"))
    dve.wait_ge(*k.lat_pe.at("rot"))
    s = slice(64, 96)
    nc.vector.tensor_tensor(k.kpt[s, :], ps[s, 3, 0:L], k.rope[s, T_MLA, 1, :], ALU.mult)
    nc.vector.tensor_tensor(k.kpe[s, :], k.kpe[s, :], k.rope[s, T_MLA, 0, :], ALU.mult)
    dve.drain()
    for hh in range(2):
        nc.vector.tensor_tensor(k.ak[s, hh, :], k.kpe[s, :], k.kpt[s, :], ALU.add)
    dve.wait_ge(*k.lat_act.at("norm"))
    for n, (g, rn) in enumerate(((V_QN, 0), (V_QN + 1, 0), (V_KVN, 1))):
        nc.vector.scalar_tensor_tensor(k.ql[:, n, :], k.ql[:, n, :], vec_col(k, 0, g), k.qrn[:, rn, :],
                                       ALU.mult, ALU.mult)
    dve.drain().then_inc(*k.lat_dve.done("out"))



def mla_sync(k, sp, ready):
    t = k.t
    for w in ready:
        sp.wait_ge(*w)
    with sp.Fori(0, PAIRS) as p:
        sp.wait_ge(*k.mla_pe.at("p", p - 1))
        sp.dma_start(k.wq, t["mla_wuq_0_2"].rearrange("(a p) n -> p a n", p=P)[:, :, ds(p * 192, 192)]
                     ).then_inc(k.d["lora_w"], 16)
        sp.dma_start(k.wkv, t["mla_wukv_0_2"][:, ds(p * 256, 256)]).then_inc(k.d["lora_w"], 16)


def mla_tensor(k, pe, loads):
    nc, ps, S, A, V = k.nc, k.PS, k.mla_pe, k.mla_act, k.mla_dve
    pe.wait_ge(*k.lat_dve.at("out"))
    with pe.Fori(0, PAIRS) as p:
        pe.wait_ge(k.d["lora_w"], p * 32 + (16 * loads + 32))
        pe.wait_ge(*V.at("w1", p - 1))
        for hh in range(2):
            for n in range(QN):
                nc.tensor.matmul(ps[0:96, 0, hh * L:(hh + 1) * L], k.wq[:, n, hh * 96:(hh + 1) * 96], k.ql[:, n, :],
                                 start=n == 0, stop=n == QN - 1)
            nc.tensor.matmul(ps[0:64, 1, hh * L:(hh + 1) * L], k.wkv[:, hh * P:hh * P + 64], k.ql[:, 2, :],
                             start=True, stop=True)
        for tile in range(2):
            for hh in range(2):
                c = (2 * tile + hh) * 64
                mm = nc.tensor.matmul(ps[:, 2, c:c + 64], k.ql[:, 2, tile * P:(tile + 1) * P],
                                      k.wkv[:, hh * P + 64:hh * P + 128], start=True, stop=True)
        mm.then_inc(*S.done("p"))
        pe.wait_ge(*A.at("copy", p))
        nc.tensor.matmul(ps[0:96, 3, :], k.mats[0:96, C_RMLA, 0:96], k.aq[0:96, :, :].rearrange("p a b -> p (a b)"),
                         start=True, stop=True).then_inc(*S.done("rot"))
        pe.wait_ge(*V.at("rope", p))
        attn_tensor(k, pe, p, S, A, V, lambda hh: k.aq[0:96, hh, :], lambda hh: k.ak[0:96, hh, :],
                    lambda hh, tile: k.av[:, tile, 64 * hh:64 * hh + 64])


def mla_scalar(k, act):
    ps, S, T, V = k.PS, k.mla_act, k.mla_pe, k.mla_dve
    with act.Fori(0, PAIRS) as p:
        act.wait_ge(*T.at("p", p))
        act.activation(k.aq[0:96, :, :].rearrange("p a b -> p (a b)"), ps[0:96, 0, :], ACT.Copy)
        act.activation(k.ak[0:64, :, :].rearrange("p a b -> p (a b)"), ps[0:64, 1, :], ACT.Copy)
        act.activation(k.av.rearrange("p a b -> p (a b)"), ps[:, 2, 0:L], ACT.Copy)
        act.drain().then_inc(*S.done("copy"))
        attn_scalar(k, act, p, S, T, V, k.OT[:, ds(p + 4, 1), 0:L].rearrange("p a n -> p (a n)"))


def mla_vector(k, dve):
    nc, ps, S, T, A = k.nc, k.PS, k.mla_dve, k.mla_pe, k.mla_act
    with dve.Fori(0, PAIRS) as p:
        dve.wait_ge(*T.at("rot", p))
        cos, sin = (bcast(k.rope[0:96, T_MLA, n, :], 2) for n in range(2))
        q, tmp = k.aq[0:96, :, :], k.atm[0:96, :].rearrange("p (a b) -> p a b", a=2)
        nc.vector.tensor_tensor(tmp, ps[0:96, 3, :].rearrange("p (a b) -> p a b", a=2), sin, ALU.mult)
        nc.vector.tensor_tensor(q, q, cos, ALU.mult)
        dve.drain()
        nc.vector.tensor_tensor(q, q, tmp, ALU.add).then_inc(*S.done("rope"))
        attn_vector(k, dve, p, S, T, A, MLA_SCALE)



SCALE64 = 64 ** -0.5
FOX_F, MOBA_0 = 1536, 1544


def declare_fox(k):
    k.fg_pe = Steps(k, "fg_pe", "f d")
    k.fg_act = Steps(k, "fg_act", "soft rows")
    k.fg_dve = Steps(k, "fg_dve", "nabs g col")
    a_pe, a_act, a_dve = attn_steps()
    k.fox_pe = Steps(k, "fox_pe", f"qk v {a_pe}")
    k.fox_act = Steps(k, "fox_act", f"copy {a_act}")
    k.fox_dve = Steps(k, "fox_dve", f"head {a_dve}")
    k.moba_pe = Steps(k, "moba_pe", f"qk v rot {a_pe}")
    k.moba_act = Steps(k, "moba_act", f"copy {a_act}")
    k.moba_dve = Steps(k, "moba_dve", f"rope {a_dve}")
    k.fw = view(k, 12288, KB, 8)
    k.fbf = view(k, 12352, 8)
    k.fx, k.fe, k.fgg = view(k, 12360, 2, 8), view(k, 12376, 2, 8), view(k, 12392, 2, 8)
    k.fcol = k.small[:, 460:476].rearrange("p (t h) -> p t h", t=2)
    k.fcp = k.small[:, 476:480].rearrange("p (t h) -> p t h", t=2)
    k.frw = k.S[0:8, 12416:12672]
    k.fr = view(k, 12672, 2, 256)


def fg_gpsimd(k, pool, ready):
    t, d = k.t, k.d
    for w in ready:
        pool.wait_ge(*w)
    pool.dma_start(k.fw, feature_rows(t["w_in_1_2"])[:, :, FOX_F:FOX_F + 8]).then_inc(d["forget_in"], 16)
    pool.dma_start(k.fbf, t["fox_bf_1_2"].partition_broadcast(P)).then_inc(d["forget_in"], 16)
    pool.wait_ge(*k.fg_act.at("rows"))
    pool.dma_start(k.frow, k.frw).then_inc(d["forget_store"], 16)
    pool.wait_ge(d["forget_store"], 16)
    with pool.Fori(0, PAIRS) as p:
        pool.wait_ge(*k.fox_dve.at("m1", p - 1))
        pool.dma_start(k.fr.rearrange("p a n -> p (a n)"),
                       k.frow.rearrange("(p a) n -> p (a n)", a=2)[ds(p, 1), :].rearrange("h n -> (h n)").partition_broadcast(P)
                       ).then_inc(d["forget_rows"], 16)


def fg_tensor(k, pe):
    nc, ps = k.nc, k.PS
    pe.wait_ge(k.d["forget_in"], 32)
    for tile in range(2):
        for kb in range(KB):
            mm = nc.tensor.matmul(ps[:, 4, tile * 8:tile * 8 + 8], k.XT[:, kb, tile * P:(tile + 1) * P], k.fw[:, kb, :],
                                  start=kb == 0, stop=kb == KB - 1)
    mm.then_inc(*k.fg_pe.done("f"))
    pe.wait_ge(*k.fg_dve.at("g"))
    nc.tensor.matmul(ps[:, 5, 0:8], mat(k, C_UP), k.fgg[:, 0, :], start=True, stop=True)
    nc.tensor.matmul(ps[:, 5, 8:16], mat(k, C_UP), k.fgg[:, 1, :], start=True, stop=False)
    nc.tensor.matmul(ps[:, 5, 8:16], mat(k, C_ONES), k.fgg[:, 0, :], start=False, stop=True)
    nc.tensor.matmul(ps[0:8, 6, 0:P], k.fgg[:, 0, :], mat(k, C_UP), start=True, stop=True)
    nc.tensor.matmul(ps[0:8, 6, P:L], k.fgg[:, 1, :], mat(k, C_UP), start=True, stop=False)
    nc.tensor.matmul(ps[0:8, 6, P:L], k.fgg[:, 0, :], mat(k, C_ONES), start=False, stop=True
                     ).then_inc(*k.fg_pe.done("d"))


def fg_scalar(k, act):
    act.wait_ge(*k.fg_dve.at("nabs"))
    act.activation(k.fe, k.fe, ACT.Exp)
    act.drain()
    act.activation(k.fe, k.fe, ACT.Ln, bias=1.0).then_inc(*k.fg_act.done("soft"))
    act.wait_ge(*k.fg_pe.at("d"))
    act.activation(k.frw, k.PS[0:8, 6, 0:L], ACT.Copy).then_inc(*k.fg_act.done("rows"))


def fg_vector(k, dve):
    nc, ps = k.nc, k.PS
    dve.wait_ge(k.d["forget_in"], 32)
    dve.wait_ge(*k.fg_pe.at("f"))
    nc.vector.tensor_tensor(k.fx, ps[:, 4, 0:16].rearrange("p (t h) -> p t h", t=2), bcast(k.fbf, 2), ALU.add)
    dve.drain()
    nc.vector.scalar_tensor_tensor(k.fe, k.fx, -1.0, k.fx, ALU.mult, ALU.min).then_inc(*k.fg_dve.done("nabs"))
    dve.wait_ge(*k.fg_act.at("soft"))
    nc.vector.scalar_tensor_tensor(k.fgg, k.fx, 0.0, k.fe, ALU.min, ALU.subtract).then_inc(*k.fg_dve.done("g"))
    dve.wait_ge(*k.fg_pe.at("d"))
    nc.vector.tensor_copy(k.fcol, ps[:, 5, 0:16].rearrange("p (t h) -> p t h", t=2)).then_inc(*k.fg_dve.done("col"))
    dve.drain()


def pair_sync(k, sp, steps, last, col, base_cols=512):
    w = feature_rows(k.t["w_in_1_2"])
    with sp.Fori(0, PAIRS) as p:
        sp.wait_ge(*steps.at(last, p - 1))
        for n in range(3):
            sp.dma_start(k.WH[:, n, :].rearrange("p (kb c) -> p kb c", kb=KB),
                         w[:, :, ds(p * P + (col + n * base_cols), P)]).then_inc(k.d["head_w"], 16)


def pair_project(k, pe, S):
    nc, ps = k.nc, k.PS
    w = [k.WH[:, n, :].rearrange("p (kb c) -> p kb c", kb=KB) for n in range(3)]
    for n in range(2):
        for kb in range(KB):
            mm = nc.tensor.matmul(ps[:, 0, n * L:(n + 1) * L], w[n][:, kb, :], k.XT[:, kb, 0:L],
                                  start=kb == 0, stop=kb == KB - 1)
    mm.then_inc(*S.done("qk"))
    for tile in range(2):
        for kb in range(KB):
            mm = nc.tensor.matmul(ps[:, 1, tile * P:(tile + 1) * P], k.XT[:, kb, tile * P:(tile + 1) * P],
                                  w[2][:, kb, :], start=kb == 0, stop=kb == KB - 1)
    mm.then_inc(*S.done("v"))


def pair_copy(k, act, p, S, T):
    act.wait_ge(*T.at("qk", p))
    act.activation(k.aq.rearrange("p a b -> p (a b)"), k.PS[:, 0, :], ACT.Copy)
    act.wait_ge(*T.at("v", p))
    act.activation(k.av.rearrange("p a b -> p (a b)"), k.PS[:, 1, 0:L], ACT.Copy)
    act.drain().then_inc(*S.done("copy"))


def pair_attention(k, pe, p, S, A, V):
    attn_tensor(k, pe, p, S, A, V, lambda hh: k.aq[64 * hh:64 * hh + 64, 0, :],
                lambda hh: k.aq[64 * hh:64 * hh + 64, 1, :], lambda hh, tile: k.av[:, tile, 64 * hh:64 * hh + 64])


def fox_tensor(k, pe, loads):
    S, A, V = k.fox_pe, k.fox_act, k.fox_dve
    pe.wait_ge(*k.fg_dve.at("col"))
    pe.wait_ge(*k.fg_act.at("rows"))
    with pe.Fori(0, PAIRS) as p:
        pe.wait_ge(k.d["head_w"], p * 48 + (16 * loads + 48))
        pair_project(k, pe, S)
        pe.wait_ge(*A.at("copy", p))
        pair_attention(k, pe, p, S, A, V)


def fox_scalar(k, act):
    S, T, V = k.fox_act, k.fox_pe, k.fox_dve
    with act.Fori(0, PAIRS) as p:
        pair_copy(k, act, p, S, T)
        attn_scalar(k, act, p, S, T, V, k.OT[:, ds(p, 1), 0:L].rearrange("p a n -> p (a n)"))


def fox_vector(k, dve):
    nc, S, T, A = k.nc, k.fox_dve, k.fox_pe, k.fox_act
    with dve.Fori(0, PAIRS) as p:
        for tile in range(2):
            i = nc.vector.tensor_copy(k.fcp[:, tile, :].unsqueeze(1),
                                      k.fcol[:, tile, :].rearrange("p (a b) -> p a b", b=2)[:, ds(p, 1), :])
        dve.drain().then_inc(*S.done("head"))
        dve.wait_ge(k.d["forget_rows"], p * 16 + 16)
        attn_vector(k, dve, p, S, T, A, SCALE64,
                    lambda hh: (lambda q: k.fcp[:, q, hh:hh + 1], k.fr[:, hh, :]))


def moba_tensor(k, pe, loads):
    nc, S, A, V = k.nc, k.moba_pe, k.moba_act, k.moba_dve
    with pe.Fori(0, PAIRS) as p:
        pe.wait_ge(k.d["head_w"], p * 48 + (16 * loads + 48))
        pair_project(k, pe, S)
        pe.wait_ge(*A.at("copy", p))
        nc.tensor.matmul(k.PS[:, 2, :], mat(k, C_RMOBA), k.aq.rearrange("p a b -> p (a b)"), start=True, stop=True
                         ).then_inc(*S.done("rot"))
        pe.wait_ge(*V.at("rope", p))
        pair_attention(k, pe, p, S, A, V)


def moba_scalar(k, act):
    S, T, V = k.moba_act, k.moba_pe, k.moba_dve
    with act.Fori(0, PAIRS) as p:
        pair_copy(k, act, p, S, T)
        attn_scalar(k, act, p, S, T, V, k.OT[:, ds(p + 4, 1), 0:L].rearrange("p a n -> p (a n)"))


def moba_vector(k, dve):
    nc, ps, S, T, A = k.nc, k.PS, k.moba_dve, k.moba_pe, k.moba_act
    with dve.Fori(0, PAIRS) as p:
        dve.wait_ge(*T.at("rot", p))
        cos, sin = (bcast(k.rope[:, T_MOBA, n, :], 2) for n in range(2))
        tmp = k.atm.rearrange("p (a b) -> p a b", a=2)
        nc.vector.tensor_tensor(tmp, ps[:, 2, :].rearrange("p (a b) -> p a b", a=2), sin, ALU.mult)
        nc.vector.tensor_tensor(k.aq, k.aq, cos, ALU.mult)
        dve.drain()
        nc.vector.tensor_tensor(k.aq, k.aq, tmp, ALU.add).then_inc(*S.done("rope"))
        attn_vector(k, dve, p, S, T, A, SCALE64)



def declare_moe(k):
    k.rt_pe = Steps(k, "rt_pe", "logits")
    k.rt_act = Steps(k, "rt_act", "gates")
    k.rt_dve = Steps(k, "rt_dve", "top comb")
    k.moe_dve = Steps(k, "moe_dve", "sum")
    k.rw_ = view(k, 6144, KB, 8)
    k.rio = view(k, 6208, 8)
    k.lg = view(k, 6216, 2, 8)
    k.top = view(k, 6232, 2, 8)
    k.tix = view(k, 6248, 2, 8)
    k.tif = view(k, 6264, 2, 8)
    k.gt = view(k, 6280, 2, 2)
    k.eq = view(k, 6284, 2, 8)
    k.comb = view(k, 6304, 2, 8)
    k.ce = view(k, 6320, 2)


def router_gpsimd(k, pool, ready):
    for w in ready:
        pool.wait_ge(*w)
    pool.dma_start(k.rw_, feature_rows(k.t["router_1_2"])).then_inc(k.d["router_in"], 16)
    pool.dma_start(k.rio, k.t["const_iota"].partition_broadcast(P)).then_inc(k.d["router_in"], 16)


def router_tensor(k, pe):
    pe.wait_ge(k.d["router_in"], 32)
    for tile in range(2):
        for kb in range(KB):
            mm = k.nc.tensor.matmul(k.PS[:, 7, tile * 8:tile * 8 + 8], k.XT[:, kb, tile * P:(tile + 1) * P],
                                    k.rw_[:, kb, :], start=kb == 0, stop=kb == KB - 1)
    mm.then_inc(*k.rt_pe.done("logits"))


def router_scalar(k, act):
    act.wait_ge(*k.rt_dve.at("top"))
    act.activation(k.gt[:, :, 1:2], k.gt[:, :, 1:2], ACT.Exp).then_inc(*k.rt_act.done("gates"))


def router_vector(k, dve):
    nc = k.nc
    tt, ts, stt = nc.vector.tensor_tensor, nc.vector.tensor_scalar, nc.vector.scalar_tensor_tensor
    dve.wait_ge(k.d["router_in"], 32)
    dve.wait_ge(*k.rt_pe.at("logits"))
    nc.vector.tensor_copy(k.lg, k.PS[:, 7, 0:16].rearrange("p (t e) -> p t e", t=2))
    dve.drain()
    for tile in range(2):
        nc.vector.max(k.top[:, tile, :], k.lg[:, tile, :])
    dve.drain()
    for tile in range(2):
        nc.vector.max_index(k.tix[:, tile, :].bitcast(U32), k.top[:, tile, :], k.lg[:, tile, :])
    tt(k.gt[:, :, 1:2], k.top[:, :, 1:2], k.top[:, :, 0:1], ALU.subtract)
    dve.drain()
    nc.vector.tensor_copy(k.tif, k.tix.bitcast(U32)).then_inc(*k.rt_dve.done("top"))
    dve.wait_ge(*k.rt_act.at("gates"))
    ts(k.gt[:, :, 0:1], k.gt[:, :, 1:2], 1.0, None, ALU.add)
    dve.drain()
    nc.vector.reciprocal(k.gt[:, :, 0:1], k.gt[:, :, 0:1])
    dve.drain()
    tt(k.gt[:, :, 1:2], k.gt[:, :, 1:2], k.gt[:, :, 0:1], ALU.mult)
    dve.drain()
    for tile in range(2):
        ts(k.eq[:, tile, :], k.rio, k.tif[:, tile, 0:1], k.gt[:, tile, 0:1], ALU.is_equal, ALU.mult)
        ts(k.comb[:, tile, :], k.rio, k.tif[:, tile, 1:2], k.gt[:, tile, 1:2], ALU.is_equal, ALU.mult)
    dve.drain()
    tt(k.comb, k.comb, k.eq, ALU.add).then_inc(*k.rt_dve.done("comb"))
    dve.drain()


def moe_sync(k, sp, base):
    t = k.t
    with sp.Fori(0, EXPERTS) as e:
        wg, wu = (t[name].rearrange("e (kb p) n -> p e kb n", p=P) for name in ("moe_wg_1_2", "moe_wu_1_2"))
        wd = t["moe_wd_1_2"].rearrange("e (b p) n -> p (e b) n", p=P)
        rounds = D_EXPERT // 256
        with sp.Fori(0, rounds) as j:
            for s in range(2):
                sp.wait_ge(*k.ffn_pe.at(f"down{s}", e * rounds + j + (base - 1)))
                for n, w in ((0, wg), (1, wu)):
                    sp.dma_start(k.WF[:, s, n, :].rearrange("p (kb n) -> p kb n", kb=KB),
                                 w[:, ds(e, 1), :, ds(j * 256 + s * P, P)].rearrange("p e kb n -> p (e kb) n")
                                 ).then_inc(k.d[f"ffn_w{s}"], 16)
                sp.dma_start(k.WF[:, s, 2, :], wd[:, ds(e * (2 * rounds) + j * 2 + s, 1), :].rearrange("p a n -> p (a n)")
                             ).then_inc(k.d[f"ffn_w{s}"], 16)


def moe_tensor(k, pe, base, acc_base):
    with pe.Fori(0, EXPERTS) as e:
        pe.wait_ge(*k.moe_dve.at("sum", e - 1))
        ffn_tensor(k, pe, 0, D_EXPERT // 256, base, e * (D_EXPERT // 256))


def moe_scalar(k, act, base):
    with act.Fori(0, EXPERTS) as e:
        ffn_scalar(k, act, D_EXPERT // 256, base, e * (D_EXPERT // 256))


def moe_vector(k, dve, base, acc_base):
    nc = k.nc
    with dve.Fori(0, EXPERTS) as e:
        dve.drain()
        nc.vector.tensor_copy(k.ce.unsqueeze(2), k.comb[:, :, ds(e, 1)])
        ffn_vector(k, dve, D_EXPERT // 256, base, e * (D_EXPERT // 256))
        dve.wait_ge(*k.acc_pe.at("sum", e + acc_base))
        for tile in range(2):
            i = nc.vector.scalar_tensor_tensor(k.X[:, tile, :], bank_rows(k, 2 * tile), k.ce[:, tile:tile + 1],
                                               k.X[:, tile, :], ALU.mult, ALU.add)
        i.then_inc(*k.moe_dve.done("sum"))



DECLARE = (declare_pre, declare_xt, declare_norms, declare_ffn, declare_gates, declare_gdn, declare_da,
           declare_attn, declare_rw, declare_mla, declare_fox, declare_moe)
FR = FFN // 256
DA_LOADS, RW_LOADS, FOX_LOADS, MOBA_LOADS = 32, 56, 68, 80


def out_w_sync(k, sp, rnd, w):
    sp.wait_ge(*(k.out_pe.at("y3", rnd - 1) if rnd else k.ada_pe.at("half1", 11)))
    sp.dma_start(k.WO[:, :, :], feature_rows(w)).then_inc(k.d["out_w"], 16)


def sync_program(k, sp):
    t = k.t

    def dense(layer, base):
        ffn_sync(k, sp, t["ffn_w_gate"][layer], t["ffn_w_up"][layer], t["ffn_w_down"][layer], FR, base)

    pre_sync(k, sp)
    out_w_sync(k, sp, 0, t["dn_w_out"][0])
    gdn_sync(k, sp)
    dense(0, 0)
    dense(0, FR)
    out_w_sync(k, sp, 1, t["da_w_out"][0])
    sp.wait_ge(*k.ln_dve.at("out", 7))
    da_sync(k, sp)
    dense(1, 2 * FR)
    out_w_sync(k, sp, 2, t["w_out_0_2"])
    sp.wait_ge(*k.ln_dve.at("out", 11))
    sp.wait_ge(*k.xt_pe.at("t7", 4))
    rw_sync(k, sp)
    mla_sync(k, sp, [k.rw_dve.at("out", PAIRS - 1), k.rw_pe.at("var", PAIRS - 1)])
    ffn_sync(k, sp, t["ffn_wg_0_2"], t["ffn_wu_0_2"], t["ffn_wd_0_2"], FR, 3 * FR)
    out_w_sync(k, sp, 3, t["w_out_1_2"])
    pair_sync(k, sp, k.fox_pe, "v", 0)
    sp.wait_ge(*k.fox_pe.at("v", PAIRS - 1))
    pair_sync(k, sp, k.moba_pe, "v", MOBA_0)
    moe_sync(k, sp, 4 * FR)
    sp.wait_ge(*k.res_dve.at("out", 9))
    sp.dma_start(k.out[0].rearrange("(t p) n -> p t n", p=P), view(k, D, 2, D)).then_inc(k.d["out_store"], 16)
    sp.wait_ge(k.d["out_store"], 16)


def gpsimd_program(k, pool):
    t = k.t

    def norm_rows(waits, layer, part, ctx):
        for w in waits:
            pool.wait_ge(*w)
        g = (2 + 3 * part) * D
        gain, bias = (("ln1_g", "ln1_b"), ("ln2_g", "ln2_b"))[part]
        rows = [k.ada[layer, 0, g:g + D], t[gain][layer], t[bias][layer]]
        for n, ap in enumerate(rows + ([k.ada[layer, 1, g:g + D]] if ctx else [])):
            pool.dma_start(k.WH[:, n, :], ap.partition_broadcast(P)).then_inc(k.d["norm_rows"], 16)

    pre_gpsimd(k, pool)
    gates_gpsimd(k, pool)
    gdn_gpsimd(k, pool)
    norm_rows([k.gdn_pe.at("pz", HEADS - 1)], 0, 0, True)
    norm_rows([k.ln_dve.at("out", 3)], 0, 1, True)
    lam_gpsimd(k, pool)
    norm_rows([k.da_pe.at("pv", HEADS - 1)], 1, 0, False)
    norm_rows([k.ln_dve.at("out", 9)], 1, 1, False)
    rwl_gpsimd(k, pool, [k.ln_dve.at("out", 11)])
    lat_gpsimd(k, pool, [k.rwl_pe.at("p")])
    fg_gpsimd(k, pool, [k.res_dve.at("out", 5)])
    router_gpsimd(k, pool, [k.res_dve.at("out", 7)])
    pool.wait_ge(*k.moba_pe.at("v", PAIRS - 1))
    pool.dma_start(k.WH[:, 0, :], t["final_norm_2"].partition_broadcast(P)).then_inc(k.d["norm_rows"], 16)


def from_x(k):
    return lambda tile, kb: k.X[:, tile, kb * P:(kb + 1) * P]


def from_scratch(k):
    return lambda tile, kb: view(k, D * (1 + tile) + kb * P, P)


def tensor_program(k, pe):
    def transposes(rnd, src, tiles, *ready):
        for w in ready:
            pe.wait_ge(*w)
        xt_tensor(k, pe, rnd, src, tiles)

    def ready(rnd):
        pe.wait_ge(*k.xt_act.at("x7", rnd))

    pre_tensor(k, pe)
    pe.wait_ge(k.d["x"], 64)
    transposes(0, from_x(k), range(4), k.adv_act.at("cols"))
    gates_tensor(k, pe)
    gdn_tensor(k, pe)
    out_tensor(k, pe, 0, range(4), [k.gdn_dve.at("out", HEADS - 1)])
    transposes(1, from_x(k), range(4), k.ln_dve.at("out", 3))
    ready(1)
    ffn_tensor(k, pe, 0, FR, 0)
    pe.wait_ge(*k.ln_dve.at("out", 5))
    ffn_tensor(k, pe, L, FR, FR)
    transposes(2, from_x(k), range(4), k.ln_dve.at("out", 7))
    ready(2)
    da_tensor(k, pe, DA_LOADS)
    out_tensor(k, pe, 1, range(2), [k.da_dve.at("out", HEADS - 1)])
    transposes(3, from_x(k), range(2), k.ln_dve.at("out", 9))
    ready(3)
    ffn_tensor(k, pe, 0, FR, 2 * FR)
    transposes(4, from_scratch(k), range(2), k.res_dve.at("out", 1))
    ready(4)
    rwl_tensor(k, pe)
    rw_tensor(k, pe, RW_LOADS)
    pe.wait_ge(*k.rw_dve.at("out", PAIRS - 1))
    lat_tensor(k, pe)
    mla_tensor(k, pe, 12)
    out_tensor(k, pe, 2, range(2), [k.mla_act.at("o", PAIRS - 1)])
    transposes(5, from_scratch(k), range(2), k.res_dve.at("out", 3))
    ready(5)
    ffn_tensor(k, pe, 0, FR, 3 * FR)
    transposes(6, from_scratch(k), range(2), k.res_dve.at("out", 5))
    ready(6)
    fg_tensor(k, pe)
    fox_tensor(k, pe, FOX_LOADS)
    moba_tensor(k, pe, MOBA_LOADS)
    out_tensor(k, pe, 3, range(2), [k.moba_act.at("o", PAIRS - 1)])
    transposes(7, from_scratch(k), range(2), k.res_dve.at("out", 7))
    ready(7)
    router_tensor(k, pe)
    moe_tensor(k, pe, 4 * FR, 4)


def scalar_program(k, act):
    def modulated(rnd, layer, part, who):
        xt_scalar(k, act, rnd, [(w * L, lambda kb, w=w: mod_col(k, layer, w, part, 1, kb),
                                 lambda kb, w=w: mod_col(k, layer, w, part, 0, kb)) for w in who])

    def gained(rnd, col):
        xt_scalar(k, act, rnd, [(0, lambda kb: vec_col(k, 1, col + kb), None)])

    pre_scalar(k, act)
    act.wait_ge(*k.adv_dve.at("scales"))
    modulated(0, 0, 0, (0, 1))
    gates_scalar(k, act)
    gdn_scalar(k, act)
    for rnd in range(4):
        ln_scalar(k, act, rnd)
    modulated(1, 0, 1, (0, 1))
    for who in range(2):
        ffn_scalar(k, act, FR, who * FR)
        for rnd in (4 + 2 * who, 5 + 2 * who):
            ln_scalar(k, act, rnd)
    modulated(2, 1, 0, (0, 1))
    lam_scalar(k, act)
    da_scalar(k, act)
    for rnd in (8, 9):
        ln_scalar(k, act, rnd)
    modulated(3, 1, 1, (0,))
    ffn_scalar(k, act, FR, 2 * FR)
    for rnd in (10, 11):
        ln_scalar(k, act, rnd)
    for tile in range(2):
        res_scalar(k, act, tile, tile)
    gained(4, V_MIX0)
    rwl_scalar(k, act)
    rw_scalar(k, act)
    act.wait_ge(*k.rw_dve.at("out", PAIRS - 1))
    lat_scalar(k, act)
    mla_scalar(k, act)
    for tile in range(2):
        res_scalar(k, act, 2 + tile, tile)
    gained(5, V_FFN0)
    ffn_scalar(k, act, FR, 3 * FR)
    for tile in range(2):
        res_scalar(k, act, 4 + tile, tile)
    gained(6, V_MIX1)
    fg_scalar(k, act)
    fox_scalar(k, act)
    moba_scalar(k, act)
    for tile in range(2):
        res_scalar(k, act, 6 + tile, tile)
    gained(7, V_FFN1)
    router_scalar(k, act)
    moe_scalar(k, act, 4 * FR)
    for tile in range(2):
        res_scalar(k, act, 8 + tile, tile)


def vector_program(k, dve):
    pre_vector(k, dve)
    gates_vector(k, dve)
    gdn_vector(k, dve)
    dve.wait_ge(k.d["norm_rows"], 64)
    for tile in range(4):
        dve.wait_ge(*k.out_pe.at(f"y{tile}", 0))
        ln_vector(k, dve, tile, tile, 2 * tile, 3 if tile >= 2 else 0)
    for who in range(2):
        ffn_vector(k, dve, FR, who * FR)
        dve.wait_ge(k.d["norm_rows"], 128)
        dve.wait_ge(*k.acc_pe.at("sum", who))
        for tile in range(2):
            ln_vector(k, dve, 4 + 2 * who + tile, 2 * who + tile, 2 * tile, 3 * who)
    lam_vector(k, dve)
    da_vector(k, dve)
    dve.wait_ge(k.d["norm_rows"], 176)
    for tile in range(2):
        dve.wait_ge(*k.out_pe.at(f"y{tile}", 1))
        ln_vector(k, dve, 8 + tile, tile, 2 * tile, 0)
    ffn_vector(k, dve, FR, 2 * FR)
    dve.wait_ge(k.d["norm_rows"], 224)
    dve.wait_ge(*k.acc_pe.at("sum", 2))
    for tile in range(2):
        ln_vector(k, dve, 10 + tile, tile, 2 * tile, 0)
    for tile in range(2):
        res_vector(k, dve, tile, tile, None)
    dve.wait_ge(*k.xt_pe.at("t7", 4))
    rwl_vector(k, dve)
    rw_vector(k, dve)
    lat_vector(k, dve)
    mla_vector(k, dve)
    for tile in range(2):
        dve.wait_ge(*k.out_pe.at(f"y{tile}", 2))
        res_vector(k, dve, 2 + tile, tile, 2 * tile)
    ffn_vector(k, dve, FR, 3 * FR)
    dve.wait_ge(*k.acc_pe.at("sum", 3))
    for tile in range(2):
        res_vector(k, dve, 4 + tile, tile, 2 * tile)
    fg_vector(k, dve)
    fox_vector(k, dve)
    moba_vector(k, dve)
    for tile in range(2):
        dve.wait_ge(*k.out_pe.at(f"y{tile}", 3))
        res_vector(k, dve, 6 + tile, tile, 2 * tile)
    router_vector(k, dve)
    moe_vector(k, dve, 4 * FR, 4)
    dve.wait_ge(k.d["norm_rows"], 240)
    dve.drain()
    for tile in range(2):
        res_vector(k, dve, 8 + tile, tile, None, k.WH[:, 0, :])



def program(nc, t, out):
    with ExitStack() as ctx:
        k = Kern()
        setup(k, nc, ctx, t, out)
        for declare in DECLARE:
            declare(k)
        credits = {name: [s for s in k.steps if s.sem_name.endswith(name)] for name in ("_pe", "_act", "_dve")}
        block = ctx.enter_context(nc.Block())

        @block.sync
        def _(sp):
            sync_program(k, sp)

        @block.gpsimd
        def _(pool):
            gpsimd_program(k, pool)

        @block.scalar
        def _(act):
            for s in credits["_act"]:
                s.credit(act)
            scalar_program(k, act)

        @block.vector
        def _(dve):
            for s in credits["_dve"]:
                s.credit(dve)
            vector_program(k, dve)

        @block.tensor
        def _(pe):
            for s in credits["_pe"]:
                s.credit(pe)
            tensor_program(k, pe)



def kernel(**inputs):
    import concourse.bacc as bacc
    from concourse.bass_utils import run_bass_kernel_spmd

    nc = bacc.Bacc("TRN2", target_bir_lowering=False, num_devices=1)
    arrays = {name: np.ascontiguousarray(a) for name, a in inputs.items()}
    arrays.update(constants())
    t = {name: nc.dram_tensor("in_" + name, a.shape, mybir.dt.from_np(a.dtype), kind="ExternalInput").ap()
         for name, a in arrays.items()}
    out = nc.dram_tensor("out", (1, L, D), F32, kind="ExternalOutput").ap()
    program(nc, t, out)
    r = run_bass_kernel_spmd(nc, [{"in_" + name: a for name, a in arrays.items()}], core_ids=[0])
    return r.results[0]["out"]
```

```python
import math
from contextlib import ExitStack

import numpy as np
import concourse.bass as bass
from concourse import mybir

P = 128
D = 1024
KB = D // P
L = 256
F32 = mybir.dt.float32
BF16 = mybir.dt.bfloat16
U32 = mybir.dt.uint32
I32 = mybir.dt.int32
ALU = mybir.AluOpType
ACT = mybir.ActivationFunctionType
AX = mybir.AxisListType.X
ds = bass.ds

DEPTH = 2
ALPHA = (2.0 * DEPTH) ** 0.25
FFN = 2816
TURNS = FFN // 512
EXPERTS, D_EXPERT = 8, 3584
HEADS = 8
PAIRS = HEADS // 2
RW_COLS = 1792
MLA_QK = 96
LAMBDA_INIT = 0.8 - 0.6 * math.exp(-0.3 * 1)
LEVELS = 7
NEG = -1e30

C_ID, C_UP, C_LO, C_SUP, C_ONES, C_ONES64, C_RDA, C_RMLA, C_RMOBA, C_LV = range(10)
N_MATS = C_LV + 2 * LEVELS
E_RMS, E_LN, E_GN, E_SHIFT = range(4)
T_DA, T_MLA, T_MOBA = range(3)
GUARD_LOG2 = 20


def constants():
    f = np.float32
    r, c = np.arange(P)[:, None], np.arange(P)[None, :]
    m = np.zeros((P, N_MATS, P), f)
    m[:, C_ID] = r == c
    m[:, C_UP] = r <= c
    m[:, C_LO] = r >= c
    m[:, C_SUP] = r < c
    m[:, C_ONES] = 1
    m[:, C_ONES64] = r // 64 == c // 64

    def rotation(start, width):
        h = width // 2
        for j in range(h):
            yield start + h + j, start + j, -1.0
            yield start + j, start + h + j, 1.0

    for b in range(4):
        for i, o, v in rotation(32 * b, 32):
            m[i, C_RDA, o] = v
    for i, o, v in rotation(64, 32):
        m[i, C_RMLA, o] = v
    for b in range(2):
        for i, o, v in rotation(64 * b, 64):
            m[i, C_RMOBA, o] = v
    for l in range(LEVELS):
        b = 1 << l
        lower = (r // (2 * b) == c // (2 * b)) & (r // b % 2 == 1) & (c // b % 2 == 0)
        m[:, C_LV + l] = lower
        m[:, C_LV + LEVELS + l] = lower.T

    def tables(ang):
        return np.cos(ang), np.sin(ang)

    pos = np.arange(L, dtype=f)
    t = np.zeros((P, 3, 2, L), f)
    inv = f(10000.0) ** (-np.arange(16, dtype=f) / f(16))
    row, col = np.floor(pos / 64).astype(f), (pos % 64).astype(f)
    ang = np.concatenate([inv[:, None] * row, inv[:, None] * row, inv[:, None] * col, inv[:, None] * col])
    t[:, T_DA, 0], t[:, T_DA, 1] = (np.concatenate([x, x]) for x in tables(ang.astype(f)))
    inv = f(10000.0) ** (-np.arange(0, 32, 2, dtype=f) / f(32))
    ang = np.concatenate([inv[:, None] * pos] * 2).astype(f)
    t[:, T_MLA, 0] = 1
    t[64:96, T_MLA, 0], t[64:96, T_MLA, 1] = tables(ang)
    inv = f(10000.0) ** (-np.arange(0, 64, 2, dtype=f) / f(64))
    ang = np.concatenate([inv[:, None] * pos] * 4).astype(f)
    t[:, T_MOBA, 0], t[:, T_MOBA, 1] = tables(ang)

    mask = np.zeros((P, 3, P), f)
    mask[:, 0] = mask[:, 2] = np.where(c > r, f(NEG), f(0))
    eps = np.zeros((P, 4), f)
    eps[:, E_RMS], eps[:, E_LN], eps[:, E_GN], eps[:, E_SHIFT] = 1e-6, 1e-5, 64e-5, GUARD_LOG2 / 2 * math.log(2)
    return {
        "const_mats": m.reshape(P, -1), "const_rope": t.reshape(P, -1),
        "const_mask": mask.reshape(P, -1), "const_eps": eps, "const_iota": np.arange(P, dtype=f),
    }


class Steps:

    def __init__(self, k, name, steps):
        self.sem, self.sem_name, self.names, self.built = k.sem(name), name, steps.split(), 0
        self.n = len(self.names)
        k.steps.append(self)

    def credit(self, eng):
        eng.sem_inc(self.sem, self.n)

    def at(self, name, rnd=0):
        return self.sem, rnd * self.n + (self.n + self.names.index(name) + 1)

    def done(self, name):
        assert self.names[self.built % self.n] == name, (name, self.names[self.built % self.n])
        self.built += 1
        return self.sem, 1


class Kern:
    pass


def setup(k, nc, ctx, t, out):
    k.nc, k.t, k.out, k.steps = nc, t, out, []

    def sb(name, shape, dt=F32):
        return ctx.enter_context(nc.sbuf_tensor(name, shape, dt))

    k.sem = lambda name: ctx.enter_context(nc.semaphore(name))
    k.X = sb("X", [P, 4, D])
    k.XT = sb("XT", [P, KB, 2 * L])
    k.OT = sb("OT", [P, KB, 2 * L])
    k.WO = sb("WO", [P, KB, D])
    k.WH = sb("WH", [P, 4, D])
    k.WF = sb("WF", [P, 2, 3, D])
    k.mats = sb("mats", [P, N_MATS, P])
    k.rope = sb("rope", [P, 3, 2, L])
    k.mask = sb("mask", [P, 3, P])
    k.eps = sb("eps", [P, 4])
    k.vecs = sb("vecs", [P, 3, P])

    k.S = sb("scratch", [P, 16384])
    k.vrow = view(k, 13312, 3, P)
    k.small = sb("small", [P, 512])
    k.zero = sb("zero", [P, 640], BF16)
    k.PS = ctx.enter_context(nc.psum_tensor("PS", [P, 8, 512], F32))
    k.ada = nc.dram_tensor("ada_rows", (2, 2, 6 * D), F32, kind="Internal").ap()
    k.grow = nc.dram_tensor("gate_rows", (HEADS, 4, 2 * L), F32, kind="Internal").ap()
    k.frow = nc.dram_tensor("forget_rows", (HEADS, L), F32, kind="Internal").ap()

    k.d = {name: k.sem("dma_" + name) for name in (
        "consts vecs x ada_b ada_w0 ada_w1 ada_store ada_vecs head_w gate_w gate_in gate_store gate_rows "
        "out_w norm_rows lam_in lora_w lat_w forget_in forget_store forget_rows router_in "
        "out_store").split()}


def view(k, at, *shape):
    n = int(np.prod(shape))
    v = k.S[:, at:at + n]
    if len(shape) == 1:
        return v
    if len(shape) == 2:
        return v.rearrange("p (a b) -> p a b", a=shape[0])
    if len(shape) == 3:
        return v.rearrange("p (a b c) -> p a b c", a=shape[0], b=shape[1])
    return v.rearrange("p (a b c d) -> p a b c d", a=shape[0], b=shape[1], c=shape[2])


def mat(k, c):
    return k.mats[:, c, :]


def bcast(ap, n):
    return ap.unsqueeze(1).to_broadcast([ap.shape[0], n, ap.shape[-1]])


def feature_rows(ap):
    return ap.rearrange("(kb p) n -> p kb n", p=P)


def rsqrt(k, act, buf, src, scale, eps):
    act.activation(buf, src, ACT.Ln, scale=scale, bias=eps)
    act.drain()
    return act.activation(buf, buf, ACT.Exp, scale=-0.5)



V_DN_G, V_DA_G, V_QN, V_KVN, V_MUW = 120, 121, 122, 124, 125
V_MIX0, V_FFN0, V_MIX1, V_FFN1, V_C = 40, 48, 56, 64, 72
ROWS0, ROWS1 = 127, 88
N_VEC_LOADS = 20
N_ADA_VEC_LOADS = 8


def mod_col(k, layer, who, part, what, kb):
    c = ((layer * 2 + who) * 2 + part) * 16 + what * 8 + kb
    return k.vecs[:, 2, c:c + 1]


def vec_col(k, tile, c):
    return k.vecs[:, tile, c:c + 1]


def declare_pre(k):
    k.pre_pe = Steps(k, "pre_pe", "vecs")
    k.pre_act = Steps(k, "pre_act", "vecs silu")
    k.pre_dve = Steps(k, "pre_dve", "zeros")
    k.ada_pe = Steps(k, "ada_pe", "half0 half1")
    k.ada_dve = Steps(k, "ada_dve", "half0 half1")
    k.adv_pe = Steps(k, "adv_pe", "cols")
    k.adv_act = Steps(k, "adv_act", "cols")
    k.adv_dve = Steps(k, "adv_dve", "scales")
    k.ada_acc = k.S[0:2, 0:12 * D]
    k.cond = k.small[:, 496:512]


def pre_sync(k, sp):
    t, d = k.t, k.d
    sp.dma_start(k.mats[:, :, :].rearrange("p a b -> p (a b)"), t["const_mats"]).then_inc(d["consts"], 16)
    sp.dma_start(k.eps[:, :], t["const_eps"]).then_inc(d["consts"], 16)

    def rows(tile, at, ap, n):
        sp.dma_start(k.vrow[at:at + n, tile, :], ap.rearrange("(r c) -> r c", c=P)).then_inc(d["vecs"], 16)

    rows(1, V_C, t["c"][0], 8)
    rows(1, V_C + 8, t["c_ctx"], 8)
    rows(0, 0, t["dn_conv"][0].rearrange("a n -> (a n)"), 120)
    rows(0, V_DN_G, t["dn_norm_g"][0], 1)
    rows(0, V_DA_G, t["da_subln_g"][0], 1)
    rows(0, V_QN, t["mla_qnorm_0_2"], 2)
    rows(0, V_KVN, t["mla_kvnorm_0_2"], 1)
    rows(0, V_MUW, t["shift_mu_0_2"][1536:RW_COLS], 2)
    rows(1, 0, t["shift_mu_0_2"][0:1536], 12)
    for n, name in enumerate(("rw_w0_0_2", "rw_a0_0_2", "rw_kk_0_2", "rw_ka_0_2")):
        rows(1, 12 + 4 * n, t[name], 4)
    rows(1, 28, t["rw_rk_0_2"].rearrange("h d -> (h d)"), 4)
    rows(1, 32, t["rw_lnx_g_0_2"], 4)
    rows(1, 36, t["rw_lnx_b_0_2"], 4)
    for at, name in ((V_MIX0, "norm_mix_0_2"), (V_FFN0, "norm_ffn_0_2"), (V_MIX1, "norm_mix_1_2"),
                     (V_FFN1, "norm_ffn_1_2")):
        rows(1, at, t[name], 8)
    sp.dma_start(k.ada_acc, t["ada_b"].rearrange("l n -> (l n)").partition_broadcast(2)).then_inc(d["ada_b"], 16)
    for layer in range(DEPTH):
        with sp.Fori(0, 6) as j:
            for half in range(2):
                sp.wait_ge(*k.ada_pe.at(f"half{half}", j + (layer * 6 - 1)))
                sp.dma_start(k.WO[:, :, half * 512:(half + 1) * 512],
                             feature_rows(t["ada_w"][layer])[:, :, ds(j * D + half * 512, 512)]
                             ).then_inc(d[f"ada_w{half}"], 16)
    sp.dma_start(k.X[:, 0:2, :], t["x"][0].rearrange("(t p) n -> p t n", p=P)).then_inc(d["x"], 16)
    sp.dma_start(k.X[:, 2:4, :], t["ctx"][0].rearrange("(t p) n -> p t n", p=P)).then_inc(d["x"], 16)
    sp.dma_start(k.rope[:, :, :, :].rearrange("p a b c -> p (a b c)"), t["const_rope"]).then_inc(d["x"], 16)
    sp.dma_start(k.mask[:, :, :].rearrange("p a b -> p (a b)"), t["const_mask"]).then_inc(d["x"], 16)


def pre_gpsimd(k, pool):
    d = k.d
    for layer in range(DEPTH):
        pool.wait_ge(*k.ada_dve.at("half1", layer * 6 + 5))
        pool.dma_start(k.ada[layer], k.ada_acc[:, layer * 6 * D:(layer + 1) * 6 * D]).then_inc(d["ada_store"], 16)
    pool.wait_ge(d["ada_store"], 32)
    for layer in range(DEPTH):
        for who in range(2):
            for part in range(2):
                at = ((layer * 2 + who) * 2 + part) * 16
                src = k.ada[layer, who, part * 3 * D:part * 3 * D + 2 * D]
                pool.dma_start(k.vrow[at:at + 16, 2, :], src.rearrange("(r c) -> r c", c=P)
                               ).then_inc(d["ada_vecs"], 16)


def pre_tensor(k, pe):
    nc, d = k.nc, k.d
    pe.wait_ge(d["consts"], 32)
    pe.wait_ge(d["vecs"], 16 * N_VEC_LOADS)
    ident = mat(k, C_ID)
    nc.tensor.transpose(k.PS[:, 2, 0:ROWS0], k.vrow[0:ROWS0, 0, :], ident[0:ROWS0, 0:ROWS0])
    nc.tensor.transpose(k.PS[:, 3, 0:ROWS1], k.vrow[0:ROWS1, 1, :], ident[0:ROWS1, 0:ROWS1]
                        ).then_inc(*k.pre_pe.done("vecs"))
    pe.wait_ge(*k.pre_act.at("silu"))
    cond = k.cond.rearrange("p (w kb) -> p kb w", w=2)
    for layer in range(DEPTH):
        with pe.Fori(0, 6) as j:
            for half in range(2):
                pe.wait_ge(d[f"ada_w{half}"], j * 16 + (layer * 6 + 1) * 16)
                pe.wait_ge(*k.ada_dve.at(f"half{half}", j + (layer * 6 - 1)))
                for kb in range(KB):
                    mm = nc.tensor.matmul(k.PS[0:2, half, :], cond[:, kb, :],
                                          k.WO[:, kb, half * 512:(half + 1) * 512],
                                          start=kb == 0, stop=kb == KB - 1)
                mm.then_inc(*k.ada_pe.done(f"half{half}"))
    pe.wait_ge(d["ada_vecs"], 16 * N_ADA_VEC_LOADS)
    nc.tensor.transpose(k.PS[:, 2, 0:P], k.vrow[:, 2, :], ident).then_inc(*k.adv_pe.done("cols"))


def pre_scalar(k, act):
    act.wait_ge(*k.pre_pe.at("vecs"))
    act.activation(k.vecs[:, 0, 0:ROWS0], k.PS[:, 2, 0:ROWS0], ACT.Copy)
    act.activation(k.vecs[:, 1, 0:ROWS1], k.PS[:, 3, 0:ROWS1], ACT.Copy).then_inc(*k.pre_act.done("vecs"))
    act.activation(k.cond, k.PS[:, 3, V_C:V_C + 16], ACT.Silu).then_inc(*k.pre_act.done("silu"))
    act.wait_ge(*k.adv_pe.at("cols"))
    act.activation(k.vecs[:, 2, :], k.PS[:, 2, 0:P], ACT.Copy).then_inc(*k.adv_act.done("cols"))


def pre_vector(k, dve):
    nc, d = k.nc, k.d
    nc.vector.memset(k.zero[:, :], 0.0).then_inc(*k.pre_dve.done("zeros"))
    dve.wait_ge(d["ada_b"], 16)
    for layer in range(DEPTH):
        with dve.Fori(0, 6) as j:
            for half in range(2):
                dve.wait_ge(*k.ada_pe.at(f"half{half}", j + layer * 6))
                acc = k.ada_acc[:, ds(j * D + (layer * 6 * D + half * 512), 512)]
                nc.vector.tensor_tensor(acc, acc, k.PS[0:2, half, :], ALU.add
                                        ).then_inc(*k.ada_dve.done(f"half{half}"))
    dve.wait_ge(*k.adv_act.at("cols"))
    scales = k.vecs[:, 2, :].rearrange("p (a s kb) -> p a s kb", s=2, kb=8)[:, :, 1, :]
    nc.vector.tensor_scalar(scales, scales, 1.0, None, ALU.add).then_inc(*k.adv_dve.done("scales"))



def declare_xt(k):
    k.xt_pe = Steps(k, "xt_pe", " ".join(f"t{kb}" for kb in range(KB)))
    k.xt_act = Steps(k, "xt_act", " ".join(f"x{kb}" for kb in range(KB)))


def xt_tensor(k, pe, rnd, src, tiles):
    nc = k.nc
    for kb in range(KB):
        if kb >= 4:
            pe.wait_ge(*k.xt_act.at(f"x{kb - 4}", rnd))
        for n, tile in enumerate(tiles):
            mm = nc.tensor.transpose(k.PS[:, kb % 4, n * P:(n + 1) * P], src(tile, kb), mat(k, C_ID))
        mm.then_inc(*k.xt_pe.done(f"t{kb}"))


def xt_scalar(k, act, rnd, parts):
    for kb in range(KB):
        act.wait_ge(*k.xt_pe.at(f"t{kb}", rnd))
        for n, (to, scale, shift) in enumerate(parts):
            a = act.activation(k.XT[:, kb, to:to + L], k.PS[:, kb % 4, n * L:(n + 1) * L], ACT.Identity,
                               scale=scale(kb), bias=shift(kb) if shift else 0.0)
        a.then_inc(*k.xt_act.done(f"x{kb}"))



def declare_norms(k):
    k.out_pe = Steps(k, "out_pe", "y0 y1 y2 y3")
    k.ln_dve = Steps(k, "ln_dve", "var out")
    k.ln_act = Steps(k, "ln_act", "rstd")
    k.res_dve = Steps(k, "res_dve", "h out")
    k.res_act = Steps(k, "res_act", "rstd")


def out_tensor(k, pe, rnd, tiles, ready):
    nc = k.nc
    pe.wait_ge(k.d["out_w"], 16 * (rnd + 1))
    for w in ready:
        pe.wait_ge(*w)
    for tile in range(4):
        if tile in tiles:
            for half in range(2):
                for kb in range(KB):
                    mm = nc.tensor.matmul(k.PS[:, tile * 2 + half, :], k.OT[:, kb, tile * P:(tile + 1) * P],
                                          k.WO[:, kb, half * 512:(half + 1) * 512],
                                          start=kb == 0, stop=kb == KB - 1)
            mm.then_inc(*k.out_pe.done(f"y{tile}"))
        else:
            pe.drain().then_inc(*k.out_pe.done(f"y{tile}"))


def bank_rows(k, bank):
    return k.PS[:, bank:bank + 2, :].rearrange("p a b -> p (a b)")


def ln_vector(k, dve, rnd, tile, bank, gate):
    nc = k.nc
    r = view(k, 0, D)
    stats, mv, var = k.small[:, 400:412], k.small[:, 412:414], k.small[:, 413:414]
    nc.vector.tensor_tensor(r, bank_rows(k, bank), k.WH[:, gate, :], ALU.mult)
    dve.drain()
    nc.vector.scalar_tensor_tensor(r, k.X[:, tile, :], ALPHA, r, ALU.mult, ALU.add)
    dve.drain()
    for h in range(2):
        nc.vector.bn_stats(stats[:, 6 * h:6 * h + 6], r[:, h * 512:(h + 1) * 512])
    dve.drain()
    nc.vector.bn_aggr(mv, stats).then_inc(*k.ln_dve.done("var"))
    dve.wait_ge(*k.ln_act.at("rstd", rnd))
    dve.drain()
    nc.vector.tensor_scalar(r, r, mv[:, 0:1], k.small[:, 414:415], ALU.subtract, ALU.mult)
    dve.drain()
    nc.vector.tensor_tensor(r, r, k.WH[:, 1, :], ALU.mult)
    dve.drain()
    nc.vector.tensor_tensor(k.X[:, tile, :], r, k.WH[:, 2, :], ALU.add).then_inc(*k.ln_dve.done("out"))
    dve.drain()


def ln_scalar(k, act, rnd):
    act.wait_ge(*k.ln_dve.at("var", rnd))
    rsqrt(k, act, k.small[:, 414:415], k.small[:, 413:414], 1.0, k.eps[:, E_LN:E_LN + 1]
          ).then_inc(*k.ln_act.done("rstd"))


def res_vector(k, dve, rnd, tile, bank, gain=None):
    nc = k.nc
    if bank is None:
        dve.drain().then_inc(*k.res_dve.done("h"))
    else:
        nc.vector.tensor_tensor(k.X[:, tile, :], k.X[:, tile, :], bank_rows(k, bank), ALU.add
                                ).then_inc(*k.res_dve.done("h"))
    dve.wait_ge(*k.res_act.at("rstd", rnd))
    out = view(k, D * (1 + tile), D)
    if gain is None:
        nc.vector.tensor_scalar(out, k.X[:, tile, :], k.small[:, 416 + tile:417 + tile], None, ALU.mult
                                ).then_inc(*k.res_dve.done("out"))
    else:
        nc.vector.scalar_tensor_tensor(out, k.X[:, tile, :], k.small[:, 416 + tile:417 + tile], gain,
                                       ALU.mult, ALU.mult).then_inc(*k.res_dve.done("out"))


def res_scalar(k, act, rnd, tile):
    act.wait_ge(*k.res_dve.at("h", rnd))
    ms = k.small[:, 416 + tile:417 + tile]
    act.activation(view(k, 0, D), k.X[:, tile, :], ACT.Square, accum_out=ms)
    act.drain()
    rsqrt(k, act, ms, ms, 1.0 / D, k.eps[:, E_RMS:E_RMS + 1]).then_inc(*k.res_act.done("rstd"))
    act.drain()



ROUND = 2 * P
UPS, DOWNS = 2 * KB * P * 2, 2 * D


class Slot:

    def __init__(self, k, name, buf):
        self.gu = buf[:, 0:UPS].rearrange("p (w kb n) -> p w kb n", w=2, kb=KB)
        self.dn = buf[:, UPS:UPS + DOWNS].rearrange("p (f n) -> p f n", f=2)
        self.pe = Steps(k, name + "_pe", "up0 up1 down0 down1")
        self.act = Steps(k, name + "_act", "silu0 silu1")
        self.dve = Steps(k, name + "_dve", "h0 h1")
        self.gu_in, self.dn_in = k.sem(name + "_up_weights"), k.sem(name + "_down_weights")


TURN = (("up", 0, 0), ("up", 0, 1), ("down", 0, 0), ("up", 1, 0), ("down", 0, 1), ("up", 1, 1), ("down", 1, 0),
        ("down", 1, 1))
LAST = (("up", 0, 0), ("up", 0, 1), ("down", 0, 0), ("down", 0, 1))


def declare_ffn(k):
    bufs = (k.WF.rearrange("p a b c -> p (a b c)"), k.WO.rearrange("p a b -> p (a b)"))
    k.dense = [Slot(k, "ffn" + "ab"[s], bufs[s]) for s in range(2)]
    k.acc_pe = Steps(k, "acc_pe", "sum")
    k.sg = view(k, 4096, 2, L)
    k.hid = view(k, 4096 + 2 * L, 2, L)
    k.sgm, k.hidm = view(k, 5120, 2, P), view(k, 5376, 2, P)


def load_round(k, sp, slot, rnd, wg, wu, wd):
    sp.wait_ge(*slot.pe.at("up1", rnd - 1))
    for n, w in enumerate((wg, wu)):
        sp.dma_start(slot.gu[:, n, :, :], w).then_inc(slot.gu_in, 16)
    sp.wait_ge(*slot.pe.at("down1", rnd - 1))
    sp.dma_start(slot.dn, wd).then_inc(slot.dn_in, 16)


def ffn_sync(k, sp, wg, wu, wd, m, b_free):
    wg, wu = feature_rows(wg), feature_rows(wu)
    wd = wd.rearrange("(b p) n -> p b n", p=P)

    def load(s, rnd, at):
        cols, rows = ds(at * P, ROUND), ds(at, 2)
        load_round(k, sp, k.dense[s], rnd, wg[:, :, cols], wu[:, :, cols], wd[:, rows, :])

    with sp.Fori(0, TURNS) as j:
        load(0, j + m * (TURNS + 1), j * 4)
        sp.wait_ge(*b_free)
        load(1, j + m * TURNS, j * 4 + 2)
    load(0, TURNS + m * (TURNS + 1), TURNS * 4)


def zero_sum(k, start, banks):
    for bank in banks:
        mm = k.nc.tensor.matmul(k.PS[:, bank, :], k.zero[:, 0:P], k.zero[:, P:P + 512],
                                start=start, stop=not start)
    return mm


def turn_tensor(k, pe, slots, order, rnds, rhs, n, hid, acc):
    nc = k.nc
    for what, s, f in order:
        slot, rnd = slots[s], rnds[s]
        if what == "up":
            if f == 0:
                pe.wait_ge(slot.gu_in, (rnd + 1) * 32)
            for w in range(2):
                for kb in range(KB):
                    mm = nc.tensor.matmul(k.PS[:, 4 + f, w * n:(w + 1) * n], slot.gu[:, w, kb, f * P:(f + 1) * P],
                                          rhs(kb), start=kb == 0, stop=kb == KB - 1)
        else:
            if f == 0:
                pe.wait_ge(slot.dn_in, (rnd + 1) * 16)
            pe.wait_ge(*slot.dve.at(f"h{f}", rnd))
            for i, bank in enumerate(acc):
                tile, half = i // 2, i % 2
                mm = nc.tensor.matmul(k.PS[:, bank, :], hid[:, f, tile * P:(tile + 1) * P],
                                      slot.dn[:, f, half * 512:(half + 1) * 512], start=False, stop=False)
        mm.then_inc(*slot.pe.done(f"{what}{f}"))


def turn_scalar(k, act, slots, count, rnds, n, sg):
    for s in range(count):
        for f in range(2):
            act.wait_ge(*slots[s].pe.at(f"up{f}", rnds[s]))
            act.activation(sg[:, f, :], k.PS[:, 4 + f, 0:n], ACT.Silu).then_inc(*slots[s].act.done(f"silu{f}"))


def turn_vector(k, dve, slots, count, rnds, n, sg, hid, after_last):
    for s in range(count):
        for f in range(2):
            dve.wait_ge(*slots[s].act.at(f"silu{f}", rnds[s]))
            dve.wait_ge(*(slots[0].pe.at(f"down{f}", rnds[0]) if s else after_last(f)))
            k.nc.vector.tensor_tensor(hid[:, f, :], sg[:, f, :], k.PS[:, 4 + f, n:2 * n], ALU.mult
                                      ).then_inc(*slots[s].dve.done(f"h{f}"))


def dense_rounds(m, j):
    return j + m * (TURNS + 1), j + m * TURNS


def ffn_tensor(k, pe, col, m):
    rhs = lambda kb: k.XT[:, kb, col:col + L]
    zero_sum(k, True, range(4))
    with pe.Fori(0, TURNS) as j:
        turn_tensor(k, pe, k.dense, TURN, dense_rounds(m, j), rhs, L, k.hid, range(4))
    turn_tensor(k, pe, k.dense, LAST, dense_rounds(m, TURNS), rhs, L, k.hid, range(4))
    zero_sum(k, False, range(4)).then_inc(*k.acc_pe.done("sum"))


def ffn_scalar(k, act, m):
    with act.Fori(0, TURNS) as j:
        turn_scalar(k, act, k.dense, 2, dense_rounds(m, j), L, k.sg)
    turn_scalar(k, act, k.dense, 1, dense_rounds(m, TURNS), L, k.sg)


def ffn_vector(k, dve, m):
    last_b = lambda j: (lambda f: k.dense[1].pe.at(f"down{f}", j + (m * TURNS - 1)))
    with dve.Fori(0, TURNS) as j:
        turn_vector(k, dve, k.dense, 2, dense_rounds(m, j), L, k.sg, k.hid, last_b(j))
    turn_vector(k, dve, k.dense, 1, dense_rounds(m, TURNS), L, k.sg, k.hid, last_b(TURNS))



def inverse_steps(groups):
    return (" ".join(" ".join([f"ax{l}{g}" for g in range(groups)] + [f"xax{l}{g}" for g in range(groups)])
                     for l in range(LEVELS)),
            " ".join(" ".join([f"ax{l}{g}" for g in range(groups)] + [f"x{l}{g}" for g in range(groups)])
                     for l in range(LEVELS)))


def inverse_tensor(k, pe, rnd, groups, s_pe, s_dve, at, x, xt, p, banks_p, banks_x, banks_t):
    nc = k.nc
    for l in range(LEVELS):
        for g in range(groups):
            if l:
                pe.wait_ge(*s_dve.at(f"x{l - 1}{g}", rnd))
            for n in range(4):
                mm = nc.tensor.matmul(k.PS[:, banks_p[g], n * P:(n + 1) * P], at(g, n),
                                      x[:, g, n, :] if l else mat(k, C_ID), start=True, stop=True)
            mm.then_inc(*s_pe.done(f"ax{l}{g}"))
        for g in range(groups):
            pe.wait_ge(*s_dve.at(f"ax{l}{g}", rnd))
            for n in range(4):
                if l < LEVELS - 1:
                    nc.tensor.matmul(k.PS[:, banks_x[g], n * P:(n + 1) * P],
                                     xt[:, g, n, :] if l else mat(k, C_ID), p[:, g, n, :],
                                     start=True, stop=True)
                mm = nc.tensor.matmul(k.PS[:, banks_t[g], n * P:(n + 1) * P], p[:, g, n, :],
                                      xt[:, g, n, :] if l else mat(k, C_ID), start=True, stop=True)
            mm.then_inc(*s_pe.done(f"xax{l}{g}"))


def tiles_of(k, bank):
    return k.PS[:, bank, :].rearrange("p (n c) -> p n c", n=4)


def inverse_vector(k, dve, rnd, groups, s_pe, s_dve, x, xt, p, banks_p, banks_x, banks_t, reverse):
    nc = k.nc
    for l in range(LEVELS):
        for g in range(groups):
            dve.wait_ge(*s_pe.at(f"ax{l}{g}", rnd))
            lv = bcast(mat(k, C_LV + l + (LEVELS if reverse[g] else 0)), 4)
            nc.vector.tensor_tensor(p[:, g, :, :], tiles_of(k, banks_p[g]), lv, ALU.mult
                                    ).then_inc(*s_dve.done(f"ax{l}{g}"))
        for g in range(groups):
            dve.wait_ge(*s_pe.at(f"xax{l}{g}", rnd))
            if l < LEVELS - 1:
                nc.vector.tensor_tensor(x[:, g, :, :], x[:, g, :, :] if l else bcast(mat(k, C_ID), 4),
                                        tiles_of(k, banks_x[g]), ALU.subtract)
            nc.vector.tensor_tensor(xt[:, g, :, :], xt[:, g, :, :] if l else bcast(mat(k, C_ID), 4),
                                    tiles_of(k, banks_t[g]), ALU.subtract).then_inc(*s_dve.done(f"x{l}{g}"))



G_CUM, G_NBE, G_BETA, G_KDEC, G_TOT = range(5)


def declare_gates(k):
    k.gate_pe = Steps(k, "gate_pe", "ab sums rows")
    k.gate_act = Steps(k, "gate_act", "beta soft rows decays")
    k.gate_dve = Steps(k, "gate_dve", "nabs g diff nbe")
    k.gw = view(k, 15896, KB, 32)
    k.dtb, k.alog = view(k, 16152, 32)[:, 0:16], view(k, 16152, 32)[:, 16:32]
    k.gx = view(k, 16184, 4, 16)
    k.ge = view(k, 16248, 4, 16)
    k.gg = view(k, 16312, 4, 16)
    k.grows = k.S[0:8, 0:4 * 512]
    k.gall = k.small[:, 0:320].rearrange("p (q t c) -> p q t c", q=5, t=4)


def gates_gpsimd(k, pool):
    t, d = k.t, k.d
    pool.dma_start(k.gw, feature_rows(t["dn_w_in"][0])[:, :, 4 * D:4 * D + 32]).then_inc(d["gate_w"], 16)
    for to, name in ((k.dtb, "dn_dt_bias"), (k.alog, "dn_a_log")):
        pool.dma_start(to, t[name][0].rearrange("d h -> (d h)").partition_broadcast(P)).then_inc(d["gate_in"], 16)
    pool.wait_ge(*k.gate_act.at("rows"))
    pool.dma_start(k.grow.rearrange("h a n -> h (a n)"), k.grows).then_inc(d["gate_store"], 16)
    pool.wait_ge(d["gate_store"], 16)


def gates_tensor(k, pe):
    nc, ps = k.nc, k.PS
    pe.wait_ge(k.d["gate_w"], 16)
    pe.wait_ge(*k.xt_act.at("x7", 0))
    for tile in range(4):
        for kb in range(KB):
            mm = nc.tensor.matmul(ps[:, 4, tile * 32:tile * 32 + 32], k.XT[:, kb, tile * P:(tile + 1) * P],
                                  k.gw[:, kb, :], start=kb == 0, stop=kb == KB - 1)
    mm.then_inc(*k.gate_pe.done("ab"))
    pe.wait_ge(*k.gate_dve.at("g"))
    for tile in range(4):
        for d, tri in ((0, C_UP), (1, C_LO)):
            nc.tensor.matmul(ps[:, 5, tile * 16 + 8 * d:tile * 16 + 8 * d + 8], mat(k, tri),
                             k.gg[:, tile, 8 * d:8 * d + 8], start=True, stop=True)
        mm = nc.tensor.matmul(ps[:, 6, tile * 16:tile * 16 + 16], mat(k, C_ONES), k.gg[:, tile, :],
                              start=True, stop=True)
    mm.then_inc(*k.gate_pe.done("sums"))
    for tile in range(4):
        c = slice(tile * P, (tile + 1) * P)
        for d, tri in ((0, C_UP), (1, C_LO)):
            nc.tensor.matmul(ps[0:8, d, c], k.gg[:, tile, 8 * d:8 * d + 8], mat(k, tri), start=True, stop=True)
            mm = nc.tensor.matmul(ps[0:8, 2 + d, c], k.gall[:, G_BETA, tile, 8 * d:8 * d + 8], mat(k, C_ID),
                                  start=True, stop=True)
    mm.then_inc(*k.gate_pe.done("rows"))


def gates_scalar(k, act):
    ps = k.PS
    act.wait_ge(*k.gate_pe.at("ab"))
    ab = ps[:, 4, 0:128].rearrange("p (t c) -> p t c", t=4)
    act.activation(k.gall[:, G_BETA, :, :], ab[:, :, 16:32], ACT.Sigmoid).then_inc(*k.gate_act.done("beta"))
    act.wait_ge(*k.gate_dve.at("nabs"))
    act.wait_ge(k.d["gate_in"], 32)
    act.activation(k.alog, k.alog, ACT.Exp)
    act.activation(k.ge, k.ge, ACT.Exp)
    act.drain()
    act.activation(k.ge, k.ge, ACT.Ln, bias=1.0).then_inc(*k.gate_act.done("soft"))
    act.wait_ge(*k.gate_pe.at("rows"))
    act.activation(k.grows, ps[0:8, 0:4, :].rearrange("p a b -> p (a b)"), ACT.Copy
                   ).then_inc(*k.gate_act.done("rows"))
    act.wait_ge(*k.gate_dve.at("diff"))
    act.activation(k.gall[:, G_NBE, :, :], k.gall[:, G_CUM, :, :], ACT.Exp)
    act.activation(k.gall[:, G_KDEC, :, :], k.gall[:, G_KDEC, :, :], ACT.Exp)
    act.activation(k.gall[:, G_TOT, :, :], ps[:, 6, 0:64].rearrange("p (t c) -> p t c", t=4), ACT.Exp)
    act.drain().then_inc(*k.gate_act.done("decays"))


def gates_vector(k, dve):
    nc, ps = k.nc, k.PS
    dve.wait_ge(*k.gate_act.at("beta"))
    dve.wait_ge(k.d["gate_in"], 32)
    ab = ps[:, 4, 0:128].rearrange("p (t c) -> p t c", t=4)
    nc.vector.tensor_tensor(k.gx, ab[:, :, 0:16], bcast(k.dtb, 4), ALU.add)
    dve.drain()
    nc.vector.scalar_tensor_tensor(k.ge, k.gx, -1.0, k.gx, ALU.mult, ALU.min).then_inc(*k.gate_dve.done("nabs"))
    dve.wait_ge(*k.gate_act.at("soft"))
    nc.vector.scalar_tensor_tensor(k.gx, k.gx, 0.0, k.ge, ALU.max, ALU.add)
    dve.wait_ge(*k.gate_act.at("soft"))
    dve.drain()
    nc.vector.scalar_tensor_tensor(k.gg, k.gx, -1.0, bcast(k.alog, 4), ALU.mult, ALU.mult
                                   ).then_inc(*k.gate_dve.done("g"))
    dve.wait_ge(*k.gate_pe.at("sums"))
    nc.vector.tensor_copy(k.gall[:, G_CUM, :, :], ps[:, 5, 0:64].rearrange("p (t c) -> p t c", t=4))
    dve.drain()
    nc.vector.tensor_tensor(k.gall[:, G_KDEC, :, :], ps[:, 6, 0:64].rearrange("p (t c) -> p t c", t=4),
                            k.gall[:, G_CUM, :, :], ALU.subtract).then_inc(*k.gate_dve.done("diff"))
    dve.wait_ge(*k.gate_act.at("decays"))
    nc.vector.scalar_tensor_tensor(k.gall[:, G_NBE, :, :], k.gall[:, G_NBE, :, :], -1.0,
                                   k.gall[:, G_BETA, :, :], ALU.mult, ALU.mult).then_inc(*k.gate_dve.done("nbe"))
    dve.drain()



SCAN = ((2, 3, 0, 1), (3, 2, 1, 0))
DN_SCALE = P ** -0.5


def declare_gdn(k):
    ip, iv = inverse_steps(2)
    scan_pe = " ".join(" ".join(f"ks{t}{d}" for d in range(2) if t) + " " + " ".join(f"vn{t}{d}" for d in range(2))
                       + " " + " ".join(f"os{t}{d}" for d in range(2)) for t in range(4))
    scan_dve = " ".join(" ".join(f"r{t}{d}" for d in range(2) if t) + " " + " ".join(f"vn{t}{d}" for d in range(2))
                        + " " + " ".join(f"s{t}{d}" for d in range(2) if t < 3) for t in range(4))
    k.gdn_pe = Steps(k, "gdn_pe", f"pq pk pv pz ssq kk qk tk tv {ip} {scan_pe} oss")
    k.gdn_act = Steps(k, "gdn_act", "gam eg raw z silu norm ktok vb o0 onorm")
    k.gdn_dve = Steps(k, "gdn_dve", f"head gam conv sq unit at att qt {iv} {scan_dve} osq out")
    k.raw = view(k, 0, 3, 2, 260)
    k.cv = view(k, 1560, 4, 512)
    k.rows = view(k, 3608, 4, 512)
    k.gm = view(k, 5656, 2, 4, P)
    k.eg = view(k, 6680, 2, 512)
    k.at_ = view(k, 7704, 2, 4, P)
    k.att = view(k, 8728, 2, 4, P)
    k.pm = view(k, 9752, 2, 4, P)
    k.xi = view(k, 10776, 2, 4, P)
    k.xit = view(k, 11800, 2, 4, P)
    k.ktok = view(k, 12824, 4, P)
    k.vb = view(k, 13336, 2, 4, P)
    k.st = view(k, 14360, 2, P)
    k.rr = view(k, 14616, 2, P)
    k.vn = view(k, 14872, 2, P)
    k.vd = view(k, 15128, 2, P)
    k.os = view(k, 15384, 512)
    k.sq = view(k, 9752, 2, 512)
    k.rn = view(k, 10776, 2, 512)
    k.gh = k.small[:, 320:360].rearrange("p (q t d) -> p q t d", q=5, t=4)
    k.cw = k.small[:, 360:375].rearrange("p (a n) -> p a n", a=5)


def gdn_sync(k, sp):
    w = feature_rows(k.t["dn_w_in"][0])
    with sp.Fori(0, HEADS) as h:
        sp.wait_ge(*k.gdn_pe.at("pz", h - 1))
        for n in range(4):
            sp.dma_start(k.WH[:, n, :].rearrange("p (kb c) -> p kb c", kb=KB), w[:, :, ds(h * P + n * D, P)]
                         ).then_inc(k.d["head_w"], 16)


def gdn_gpsimd(k, pool):
    with pool.Fori(0, HEADS) as h:
        pool.wait_ge(*k.gdn_dve.at("at", h - 1))
        pool.wait_ge(*k.gdn_act.at("eg", h - 1))
        pool.dma_start(k.rows.rearrange("p a n -> p (a n)"),
                       k.grow.rearrange("h a n -> h (a n)")[ds(h, 1), :].rearrange("h n -> (h n)").partition_broadcast(P)
                       ).then_inc(k.d["gate_rows"], 16)


def gdn_tensor(k, pe):
    nc, ps, S, A, V = k.nc, k.PS, k.gdn_pe, k.gdn_act, k.gdn_dve
    q, kt = k.cv[:, 0, :], k.cv[:, 1, :]
    pe.wait_ge(*k.gate_act.at("rows"))
    with pe.Fori(0, HEADS) as h:
        pe.wait_ge(k.d["head_w"], h * 64 + 64)
        for n, name in enumerate(("pq", "pk", "pv", "pz")):
            w = k.WH[:, n, :].rearrange("p (kb c) -> p kb c", kb=KB)
            for kb in range(KB):
                mm = nc.tensor.matmul(ps[:, n, :], w[:, kb, :], k.XT[:, kb, :], start=kb == 0, stop=kb == KB - 1)
            mm.then_inc(*S.done(name))
        pe.wait_ge(*V.at("sq", h))
        for n in range(2):
            mm = nc.tensor.matmul(ps[:, n, :], mat(k, C_ONES), k.sq[:, n, :], start=True, stop=True)
        mm.then_inc(*S.done("ssq"))
        pe.wait_ge(*V.at("unit", h))
        for name, bank, rhs in (("kk", 0, kt), ("qk", 1, q)):
            for n in range(4):
                c = slice(n * P, (n + 1) * P)
                mm = nc.tensor.matmul(ps[:, bank, c], kt[:, c], rhs[:, c], start=True, stop=True)
            mm.then_inc(*S.done(name))
        for name, bank, src in (("tk", 2, kt), ("tv", 3, k.cv[:, 2, :])):
            for n in range(4):
                c = slice(n * P, (n + 1) * P)
                mm = nc.tensor.transpose(ps[:, bank, c], src[:, c], mat(k, C_ID))
            mm.then_inc(*S.done(name))
        pe.wait_ge(*V.at("at", h))
        pe.wait_ge(*V.at("att", h))
        inverse_tensor(k, pe, h, 2, S, V, lambda g, n: k.at_[:, g, n, :], k.xi, k.xit, k.pm, (4, 5), (6, 7), (0, 1))
        for t in range(4):
            for d in range(2):
                tile = SCAN[d][t]
                if t == 0:
                    pe.wait_ge(*A.at("vb", h))
                    pe.wait_ge(*V.at("qt", h))
                    continue
                pe.wait_ge(*V.at(f"s{t - 1}{d}", h))
                nc.tensor.matmul(ps[:, 2 + d, 0:P], kt[:, tile * P:(tile + 1) * P], k.st[:, d, :],
                                 start=True, stop=True).then_inc(*S.done(f"ks{t}{d}"))
            for d in range(2):
                tile = SCAN[d][t]
                if t:
                    pe.wait_ge(*V.at(f"r{t}{d}", h))
                pe.wait_ge(*V.at(f"x{LEVELS - 1}{d}", h))
                rhs = k.rr[:, d, :] if t else k.vb[:, d, tile, :]
                nc.tensor.matmul(ps[:, 2 + d, P:2 * P], k.xit[:, d, tile, :], rhs, start=True, stop=True
                                 ).then_inc(*S.done(f"vn{t}{d}"))
            for d in range(2):
                tile = SCAN[d][t]
                c = slice(tile * P, (tile + 1) * P)
                pe.wait_ge(*V.at(f"vn{t}{d}", h))
                if t:
                    nc.tensor.matmul(ps[:, 4 + d, c], k.st[:, d, :], k.eg[:, d, c], start=True, stop=False)
                nc.tensor.matmul(ps[:, 4 + d, c], k.vn[:, d, :], k.att[:, d, tile, :], start=t == 0, stop=True)
                nc.tensor.matmul(ps[:, 2 + d, 2 * P:3 * P], k.ktok[:, tile, :], k.vd[:, d, :],
                                 start=True, stop=True).then_inc(*S.done(f"os{t}{d}"))
        pe.wait_ge(*V.at("osq", h))
        nc.tensor.matmul(ps[:, 6, :], mat(k, C_ONES), k.pm[:, 0, :, :].rearrange("p a b -> p (a b)"),
                         start=True, stop=True).then_inc(*S.done("oss"))


def gdn_scalar(k, act):
    ps, S, T, V = k.PS, k.gdn_act, k.gdn_pe, k.gdn_dve
    with act.Fori(0, HEADS) as h:
        act.wait_ge(*V.at("out", h - 1))
        act.wait_ge(*V.at("gam", h))
        act.activation(k.gm[:, :, :, :].rearrange("p a b c -> p (a b c)"),
                       k.gm[:, :, :, :].rearrange("p a b c -> p (a b c)"), ACT.Exp).then_inc(*S.done("gam"))
        act.activation(k.eg[:, :, :], k.rows[:, 0:2, :], ACT.Exp).then_inc(*S.done("eg"))
        for n, name in enumerate(("pq", "pk", "pv")):
            act.wait_ge(*T.at(name, h))
            a = act.activation(k.raw[:, n, :, 2:258], ps[:, n, :].rearrange("p (s c) -> p s c", s=2), ACT.Copy)
        a.then_inc(*S.done("raw"))
        act.wait_ge(*T.at("pz", h))
        act.activation(k.cv[:, 3, :], ps[:, 3, :], ACT.Silu).then_inc(*S.done("z"))
        act.wait_ge(*V.at("conv", h))
        act.activation(k.cv[:, 0:3, :], k.cv[:, 0:3, :], ACT.Silu).then_inc(*S.done("silu"))
        act.wait_ge(*T.at("ssq", h))
        rsqrt(k, act, k.rn[:, :, :], ps[:, 0:2, :], 1.0, k.eps[:, E_RMS:E_RMS + 1]).then_inc(*S.done("norm"))
        act.wait_ge(*T.at("tk", h))
        act.activation(k.ktok[:, :, :], tiles_of(k, 2), ACT.Copy).then_inc(*S.done("ktok"))
        act.wait_ge(*T.at("tv", h))
        for d in range(2):
            for n in range(4):
                a = act.activation(k.vb[:, d, n, :], ps[:, 3, n * P:(n + 1) * P], ACT.Copy,
                                   scale=k.gh[:, G_BETA, n, d:d + 1])
        a.then_inc(*S.done("vb"))
        act.wait_ge(*T.at("os31", h))
        act.activation(k.os, ps[:, 4, :], ACT.Copy).then_inc(*S.done("o0"))
        act.wait_ge(*T.at("oss", h))
        rsqrt(k, act, k.rn[:, 0, :], ps[:, 6, :], 1.0 / P, k.eps[:, E_RMS:E_RMS + 1]).then_inc(*S.done("onorm"))


def gdn_vector(k, dve):
    nc, ps, S, T, A = k.nc, k.PS, k.gdn_dve, k.gdn_pe, k.gdn_act
    conv = k.vecs[:, 0, 0:120].rearrange("p (a n h) -> p a n h", a=5, n=3)
    gall = k.gall.rearrange("p q t (d h) -> p (q t d) h", d=2)
    dve.wait_ge(k.d["gate_store"], 16)
    nc.vector.memset(k.raw[:, :, :, 0:2], 0.0)
    nc.vector.memset(k.raw[:, :, :, 258:260], 0.0)
    dve.drain()
    with dve.Fori(0, HEADS) as h:
        nc.vector.tensor_copy(k.gh.rearrange("p q t d -> p (q t d)").unsqueeze(2), gall[:, :, ds(h, 1)])
        for a in range(5):
            nc.vector.tensor_copy(k.cw[:, a, :].unsqueeze(2), conv[:, a, :, ds(h, 1)])
        dve.drain().then_inc(*S.done("head"))
        dve.wait_ge(k.d["gate_rows"], h * 16 + 16)
        for d in range(2):
            for n in range(4):
                nc.vector.tensor_scalar(k.gm[:, d, n, :], k.rows[:, d, n * P:(n + 1) * P],
                                        k.gh[:, G_CUM, n, d:d + 1], 0.0, ALU.subtract, ALU.min)
        dve.drain().then_inc(*S.done("gam"))
        dve.wait_ge(*A.at("raw", h))
        for n in range(3):
            cv = k.cv[:, n, :].rearrange("p (s c) -> p s c", s=2)
            nc.vector.tensor_scalar(cv, k.raw[:, n, :, 0:L], k.cw[:, 0, n:n + 1], None, ALU.mult)
        for a in range(1, 5):
            dve.drain()
            for n in range(3):
                cv = k.cv[:, n, :].rearrange("p (s c) -> p s c", s=2)
                i = nc.vector.scalar_tensor_tensor(cv, k.raw[:, n, :, a:a + L], k.cw[:, a, n:n + 1], cv,
                                                   ALU.mult, ALU.add)
        i.then_inc(*S.done("conv"))
        dve.wait_ge(*A.at("silu", h))
        nc.vector.tensor_tensor(k.sq[:, :, :], k.cv[:, 0:2, :], k.cv[:, 0:2, :], ALU.mult).then_inc(*S.done("sq"))
        dve.wait_ge(*A.at("gam", h))
        for d, tri in ((0, C_UP), (1, C_LO)):
            nc.vector.tensor_tensor(k.gm[:, d, :, :], k.gm[:, d, :, :], bcast(mat(k, tri), 4), ALU.mult)
        dve.wait_ge(*A.at("norm", h))
        nc.vector.scalar_tensor_tensor(k.cv[:, 0, :], k.cv[:, 0, :], DN_SCALE, k.rn[:, 0, :], ALU.mult, ALU.mult)
        nc.vector.tensor_tensor(k.cv[:, 1, :], k.cv[:, 1, :], k.rn[:, 1, :], ALU.mult).then_inc(*S.done("unit"))
        dve.wait_ge(*T.at("kk", h))
        for d in range(2):
            nc.vector.tensor_tensor(k.at_[:, d, :, :], tiles_of(k, 0), k.gm[:, d, :, :], ALU.mult)
        dve.drain()
        i = nc.vector.tensor_tensor(k.at_.rearrange("p d n c -> p (d n c)"), k.at_.rearrange("p d n c -> p (d n c)"),
                                    k.rows[:, 2:4, :].rearrange("p d c -> p (d c)"), ALU.mult)
        i.then_inc(*S.done("at"))
        dve.wait_ge(*T.at("qk", h))
        for d in range(2):
            i = nc.vector.tensor_tensor(k.att[:, d, :, :], tiles_of(k, 1), k.gm[:, d, :, :], ALU.mult)
        i.then_inc(*S.done("att"))
        dve.wait_ge(*A.at("eg", h))
        for d in range(2):
            i = nc.vector.tensor_tensor(k.eg[:, d, :], k.eg[:, d, :], k.cv[:, 0, :], ALU.mult)
        i.then_inc(*S.done("qt"))
        inverse_vector(k, dve, h, 2, T, S, k.xi, k.xit, k.pm, (4, 5), (6, 7), (0, 1), (False, True))
        for t in range(4):
            for d in range(2):
                tile = SCAN[d][t]
                if t == 0:
                    continue
                dve.wait_ge(*T.at(f"ks{t}{d}", h))
                nc.vector.scalar_tensor_tensor(k.rr[:, d, :], ps[:, 2 + d, 0:P], k.gh[:, G_NBE, tile, d:d + 1],
                                               k.vb[:, d, tile, :], ALU.mult, ALU.add
                                               ).then_inc(*S.done(f"r{t}{d}"))
            for d in range(2):
                tile = SCAN[d][t]
                dve.wait_ge(*T.at(f"vn{t}{d}", h))
                nc.vector.tensor_copy(k.vn[:, d, :], ps[:, 2 + d, P:2 * P])
                nc.vector.tensor_scalar(k.vd[:, d, :], ps[:, 2 + d, P:2 * P], k.gh[:, G_KDEC, tile, d:d + 1],
                                        None, ALU.mult).then_inc(*S.done(f"vn{t}{d}"))
            for d in range(2 if t < 3 else 0):
                tile = SCAN[d][t]
                dve.wait_ge(*T.at(f"os{t}{d}", h))
                if t == 0:
                    i = nc.vector.tensor_copy(k.st[:, d, :], ps[:, 2 + d, 2 * P:3 * P])
                else:
                    i = nc.vector.scalar_tensor_tensor(k.st[:, d, :], k.st[:, d, :], k.gh[:, G_TOT, tile, d:d + 1],
                                                       ps[:, 2 + d, 2 * P:3 * P], ALU.mult, ALU.add)
                i.then_inc(*S.done(f"s{t}{d}"))
        dve.wait_ge(*A.at("o0", h))
        nc.vector.tensor_tensor(k.os, k.os, ps[:, 5, :], ALU.add)
        dve.drain()
        nc.vector.tensor_tensor(k.pm[:, 0, :, :].rearrange("p a b -> p (a b)"), k.os, k.os, ALU.mult
                                ).then_inc(*S.done("osq"))
        dve.wait_ge(*A.at("onorm", h))
        nc.vector.scalar_tensor_tensor(k.os, k.os, vec_col(k, 0, V_DN_G), k.rn[:, 0, :], ALU.mult, ALU.mult)
        dve.drain()
        nc.vector.tensor_tensor(k.OT[:, ds(h, 1), :].rearrange("p a n -> p (a n)"), k.os, k.cv[:, 3, :], ALU.mult
                                ).then_inc(*S.done("out"))



DA_SCALE = 64 ** -0.5


def declare_da(k):
    k.lam_dve = Steps(k, "lam_dve", "dots lam")
    k.lam_act = Steps(k, "lam_act", "exps")
    k.da_pe = Steps(k, "da_pe", "pq pk pv rot s00 s01 s10 s11 tr0 tr1 o oss")
    k.da_act = Steps(k, "da_act", "qk v p00 p01 p10 p11 pt0 pt1 o onorm")
    k.da_dve = Steps(k, "da_dve", "rope max rs a osq out")
    k.dq = view(k, 0, 256)
    k.dk = view(k, 256, 512)
    k.dv = view(k, 768, 4, P)
    k.dt1 = view(k, 1280, 512)
    k.dp = view(k, 1792, 2, 2, 512)
    k.da = view(k, 3840, 2, 512)
    k.dpt = view(k, 4864, 4, 256)
    k.do = view(k, 5888, 256)
    k.dsq = view(k, 6144, 256)
    k.drn = view(k, 6400, 256)
    k.lamr = view(k, 6656, 256)
    k.lamp = view(k, 6912, 2, 64)
    k.lam = k.small[:, 424:428]
    k.dag = k.small[:, 428:429]
    k.dmx, k.dnm, k.dsum, k.drs = (k.small[:, 432 + 4 * n:436 + 4 * n] for n in range(4))


def da_sync(k, sp):
    w = feature_rows(k.t["da_w_in"][0])
    with sp.Fori(0, HEADS) as h:
        sp.wait_ge(*k.da_pe.at("pv", h - 1))
        for n in range(3):
            sp.dma_start(k.WH[:, n, :].rearrange("p (kb c) -> p kb c", kb=KB), w[:, :, ds(h * P + n * D, P)]
                         ).then_inc(k.d["head_w"], 16)


def lam_gpsimd(k, pool):
    pool.dma_start(k.lamr, k.t["da_lambda"][0].rearrange("a n -> (a n)").partition_broadcast(P)
                   ).then_inc(k.d["lam_in"], 16)


def lam_vector(k, dve):
    nc = k.nc
    dve.wait_ge(k.d["lam_in"], 16)
    l = k.lamr.rearrange("p (a b n) -> p a b n", a=2, b=2)
    nc.vector.tensor_tensor(k.lamp, l[:, :, 0, :], l[:, :, 1, :], ALU.mult)
    dve.drain()
    nc.vector.tensor_reduce(k.lam[:, 0:2], k.lamp, AX, ALU.add).then_inc(*k.lam_dve.done("dots"))
    dve.wait_ge(*k.lam_act.at("exps"))
    nc.vector.tensor_tensor(k.lam[:, 2:3], k.lam[:, 0:1], k.lam[:, 1:2], ALU.subtract)
    dve.drain()
    nc.vector.tensor_scalar(k.lam[:, 3:4], k.lam[:, 2:3], LAMBDA_INIT, -1.0, ALU.add, ALU.mult)
    nc.vector.tensor_scalar(k.dag, vec_col(k, 0, V_DA_G), 1.0 - LAMBDA_INIT, None, ALU.mult
                            ).then_inc(*k.lam_dve.done("lam"))
    dve.drain()


def lam_scalar(k, act):
    act.wait_ge(*k.lam_dve.at("dots"))
    act.activation(k.lam[:, 0:2], k.lam[:, 0:2], ACT.Exp).then_inc(*k.lam_act.done("exps"))


def da_tensor(k, pe, loads):
    nc, ps, S, A, V = k.nc, k.PS, k.da_pe, k.da_act, k.da_dve
    w = [k.WH[:, n, :].rearrange("p (kb c) -> p kb c", kb=KB) for n in range(3)]
    with pe.Fori(0, HEADS) as h:
        pe.wait_ge(k.d["head_w"], h * 48 + (16 * loads + 48))
        pe.wait_ge(*V.at("out", h - 1))
        for kb in range(KB):
            mm = nc.tensor.matmul(ps[:, 0, 0:L], w[0][:, kb, :], k.XT[:, kb, 0:L], start=kb == 0, stop=kb == KB - 1)
        mm.then_inc(*S.done("pq"))
        for kb in range(KB):
            mm = nc.tensor.matmul(ps[:, 1, :], w[1][:, kb, :], k.XT[:, kb, :], start=kb == 0, stop=kb == KB - 1)
        mm.then_inc(*S.done("pk"))
        for n in range(4):
            for kb in range(KB):
                mm = nc.tensor.matmul(ps[:, 2, n * P:(n + 1) * P], k.XT[:, kb, n * P:(n + 1) * P], w[2][:, kb, :],
                                      start=kb == 0, stop=kb == KB - 1)
        mm.then_inc(*S.done("pv"))
        pe.wait_ge(*A.at("qk", h))
        nc.tensor.matmul(ps[:, 3, 0:L], mat(k, C_RDA), k.dq, start=True, stop=True)
        nc.tensor.matmul(ps[:, 3, L:2 * L], mat(k, C_RDA), k.dk[:, 0:L], start=True, stop=True
                         ).then_inc(*S.done("rot"))
        pe.wait_ge(*V.at("rope", h))
        for c in range(2):
            r = slice(64 * c, 64 * c + 64)
            for q in range(2):
                nc.tensor.matmul(ps[:, 4 + 2 * c + q, :], k.dq[r, q * P:(q + 1) * P], k.dk[r, :],
                                 start=True, stop=True).then_inc(*S.done(f"s{c}{q}"))
        pe.wait_ge(*V.at("a", h))
        pe.wait_ge(*A.at("v", h))
        for half in range(2):
            for n in range(2):
                for q in range(2):
                    at = (2 * half + n) * P
                    mm = nc.tensor.transpose(ps[:, half, n * L + q * P:n * L + (q + 1) * P],
                                             k.da[:, q, at:at + P], mat(k, C_ID))
            mm.then_inc(*S.done(f"tr{half}"))
        pe.wait_ge(*A.at("pt1", h))
        for n in range(4):
            mm = nc.tensor.matmul(ps[:, 2, 0:L], k.dv[:, n, :], k.dpt[:, n, :], start=n == 0, stop=n == 3)
        mm.then_inc(*S.done("o"))
        pe.wait_ge(*V.at("osq", h))
        nc.tensor.matmul(ps[:, 3, 0:L], mat(k, C_ONES), k.dsq, start=True, stop=True).then_inc(*S.done("oss"))


def da_scalar(k, act):
    ps, S, T, V = k.PS, k.da_act, k.da_pe, k.da_dve
    with act.Fori(0, HEADS) as h:
        act.wait_ge(*T.at("pq", h))
        act.activation(k.dq, ps[:, 0, 0:L], ACT.Copy)
        act.wait_ge(*T.at("pk", h))
        act.activation(k.dk, ps[:, 1, :], ACT.Copy)
        act.drain().then_inc(*S.done("qk"))
        act.wait_ge(*T.at("pv", h))
        act.activation(k.dv, tiles_of(k, 2), ACT.Copy).then_inc(*S.done("v"))
        act.wait_ge(*V.at("max", h))
        for c in range(2):
            for q in range(2):
                i = 2 * c + q
                act.activation(k.dp[:, c, q, :], ps[:, 4 + i, :], ACT.Exp, scale=DA_SCALE,
                               bias=k.dnm[:, i:i + 1], accum_out=k.dsum[:, i:i + 1])
                act.drain().then_inc(*S.done(f"p{c}{q}"))
        for half in range(2):
            act.wait_ge(*T.at(f"tr{half}", h))
            act.activation(k.dpt[:, 2 * half:2 * half + 2, :], ps[:, half, :].rearrange("p (n c) -> p n c", n=2),
                           ACT.Copy).then_inc(*S.done(f"pt{half}"))
        act.wait_ge(*T.at("o", h))
        act.activation(k.do, ps[:, 2, 0:L], ACT.Copy).then_inc(*S.done("o"))
        act.wait_ge(*T.at("oss", h))
        rsqrt(k, act, k.drn, ps[:, 3, 0:L], 1.0 / P, k.eps[:, E_RMS:E_RMS + 1]).then_inc(*S.done("onorm"))


def rope_vector(k, dve, x, rot, table, tmp):
    nc = k.nc
    n = x.shape[0]
    nc.vector.tensor_tensor(tmp, rot, k.rope[0:n, table, 1, :], ALU.mult)
    nc.vector.tensor_tensor(x, x, k.rope[0:n, table, 0, :], ALU.mult)
    dve.drain()
    return nc.vector.tensor_tensor(x, x, tmp, ALU.add)


def da_vector(k, dve):
    nc, ps, S, T, A = k.nc, k.PS, k.da_dve, k.da_pe, k.da_act
    with dve.Fori(0, HEADS) as h:
        dve.wait_ge(*T.at("rot", h))
        dve.wait_ge(*A.at("qk", h))
        rope_vector(k, dve, k.dq, ps[:, 3, 0:L], T_DA, k.dt1[:, 0:L])
        rope_vector(k, dve, k.dk[:, 0:L], ps[:, 3, L:2 * L], T_DA, k.dt1[:, L:2 * L])
        dve.drain().then_inc(*S.done("rope"))
        for c in range(2):
            for q in range(2):
                dve.wait_ge(*T.at(f"s{c}{q}", h))
                nc.vector.reduce_max(k.dmx[:, 2 * c + q:2 * c + q + 1], ps[:, 4 + 2 * c + q, :], AX)
        dve.drain()
        nc.vector.tensor_scalar(k.dnm, k.dmx, -DA_SCALE, None, ALU.mult).then_inc(*S.done("max"))
        dve.wait_ge(*A.at("p11", h))
        nc.vector.reciprocal(k.drs, k.dsum)
        dve.drain()
        nc.vector.tensor_scalar(k.drs[:, 2:4], k.drs[:, 2:4], k.lam[:, 3:4], None, ALU.mult).then_inc(*S.done("rs"))
        dve.drain()
        for q in range(2):
            nc.vector.tensor_scalar(k.da[:, q, :], k.dp[:, 0, q, :], k.drs[:, q:q + 1], None, ALU.mult)
        dve.drain()
        for q in range(2):
            i = nc.vector.scalar_tensor_tensor(k.da[:, q, :], k.dp[:, 1, q, :], k.drs[:, 2 + q:3 + q], k.da[:, q, :],
                                               ALU.mult, ALU.add)
        i.then_inc(*S.done("a"))
        dve.wait_ge(*A.at("o", h))
        nc.vector.tensor_tensor(k.dsq, k.do, k.do, ALU.mult).then_inc(*S.done("osq"))
        dve.wait_ge(*A.at("onorm", h))
        nc.vector.scalar_tensor_tensor(k.OT[:, ds(h, 1), 0:L].rearrange("p a n -> p (a n)"), k.do, k.dag, k.drn,
                                       ALU.mult, ALU.mult).then_inc(*S.done("out"))



def attn_steps():
    return ("s0 s1 tr0 tr1 o0 o1", "p0 p1 pt0 pt1 o", "m0 m1 w0 w1")


def declare_attn(k):
    k.aq = view(k, 8192, 2, 256)
    k.ak = view(k, 8704, 2, 256)
    k.av = view(k, 9216, 2, P)
    k.asc = view(k, 9472, 2, 384)
    k.apt = view(k, 10240, 2, 384)
    k.atm = view(k, 11008, 512)
    k.amx, k.asum = k.small[:, 448:452], k.small[:, 452:456]
    k.ars = k.small[:, 456:460]


QCOLS = (slice(0, P), slice(P, 3 * P))


def attn_tensor(k, pe, rnd, S, A, V, q, kk, v):
    nc, ps = k.nc, k.PS
    for hh in range(2):
        nc.tensor.matmul(ps[:, 4 + hh, QCOLS[0]], q(hh)[:, 0:P], kk(hh)[:, 0:P], start=True, stop=True)
        nc.tensor.matmul(ps[:, 4 + hh, QCOLS[1]], q(hh)[:, P:L], kk(hh)[:, 0:L], start=True, stop=True
                         ).then_inc(*S.done(f"s{hh}"))
    for hh in range(2):
        pe.wait_ge(*V.at(f"w{hh}", rnd))
        for n in range(3):
            mm = nc.tensor.transpose(ps[:, 6 + hh, n * P:(n + 1) * P], k.asc[:, hh, n * P:(n + 1) * P], mat(k, C_ID))
        mm.then_inc(*S.done(f"tr{hh}"))
    for hh in range(2):
        pe.wait_ge(*A.at(f"pt{hh}", rnd))
        o = ps[64 * hh:64 * hh + 64, 3, :]
        nc.tensor.matmul(o[:, 0:P], v(hh, 0), k.apt[:, hh, 0:P], start=True, stop=True)
        nc.tensor.matmul(o[:, P:L], v(hh, 0), k.apt[:, hh, P:2 * P], start=True, stop=False)
        nc.tensor.matmul(o[:, P:L], v(hh, 1), k.apt[:, hh, 2 * P:3 * P], start=False, stop=True
                         ).then_inc(*S.done(f"o{hh}"))


def attn_scalar(k, act, rnd, S, T, V, block):
    ps = k.PS
    for hh in range(2):
        act.wait_ge(*V.at(f"m{hh}", rnd))
        for q in range(2):
            i = 2 * hh + q
            act.activation(k.asc[:, hh, QCOLS[q]], k.asc[:, hh, QCOLS[q]], ACT.Exp, bias=k.amx[:, i:i + 1],
                           accum_out=k.asum[:, i:i + 1])
        act.drain().then_inc(*S.done(f"p{hh}"))
    for hh in range(2):
        act.wait_ge(*T.at(f"tr{hh}", rnd))
        act.activation(k.apt[:, hh, :], ps[:, 6 + hh, 0:384], ACT.Copy).then_inc(*S.done(f"pt{hh}"))
    act.wait_ge(*T.at("o0", rnd))
    act.wait_ge(*T.at("o1", rnd))
    act.activation(block, ps[:, 3, 0:L], ACT.Copy).then_inc(*S.done("o"))


def attn_vector(k, dve, rnd, S, T, A, scale, decay=None):
    nc, ps = k.nc, k.PS
    mask = k.mask.rearrange("p a b -> p (a b)")
    for hh in range(2):
        dve.wait_ge(*T.at(f"s{hh}", rnd))
        nc.vector.scalar_tensor_tensor(k.asc[:, hh, :], ps[:, 4 + hh, 0:384], scale, mask, ALU.mult, ALU.add)
        if decay:
            col, row = decay(hh)
            dve.drain()
            for q in range(2):
                sc = k.asc[:, hh, QCOLS[q]]
                nc.vector.scalar_tensor_tensor(sc, sc, col(q), row[:, 0:(q + 1) * P], ALU.add, ALU.subtract)
        dve.drain()
        for q in range(2):
            i = 2 * hh + q
            nc.vector.reduce_max(k.amx[:, i:i + 1], k.asc[:, hh, QCOLS[q]], AX)
        dve.drain()
        nc.vector.tensor_scalar(k.amx[:, 2 * hh:2 * hh + 2], k.amx[:, 2 * hh:2 * hh + 2], -1.0, None, ALU.mult
                                ).then_inc(*S.done(f"m{hh}"))
    for hh in range(2):
        dve.wait_ge(*A.at(f"p{hh}", rnd))
        nc.vector.reciprocal(k.ars[:, 2 * hh:2 * hh + 2], k.asum[:, 2 * hh:2 * hh + 2])
        dve.drain()
        for q in range(2):
            sc, i = k.asc[:, hh, QCOLS[q]], 2 * hh + q
            nc.vector.tensor_scalar(sc, sc, k.ars[:, i:i + 1], None, ALU.mult)
        dve.drain().then_inc(*S.done(f"w{hh}"))



RW_DECAY = -math.exp(-0.5)


def declare_rw(k):
    k.rwl_pe = Steps(k, "rwl_pe", "p")
    k.rwl_act = Steps(k, "rwl_act", "raw funcs")
    k.rwl_dve = Steps(k, "rwl_dve", "mix")
    ip, iv = inverse_steps(1)
    k.rw_pe = Steps(k, "rw_pe", f"rk vw ag ssk bo m0 m1 tr {ip} rn00 rn01 u00 u01 z rn10 rn11 u10 u11 y mean var")
    k.rw_act = Steps(k, "rw_act", "raw w a g knorm ws tok y gnorm")
    k.rw_dve = Steps(k, "rw_dve", f"head mix ksq kmax cum bo til ab {iv} rn00 rn01 u00 u01 z rn10 rn11 u10 u11 "
                                  "ysq out")
    k.raw3 = view(k, 0, 3, 257)
    k.rkv = view(k, 800, 3, 256)
    k.lw = view(k, 1568, 2, 256)
    k.l2 = view(k, 2080, 2, P)
    k.ld, k.ra, k.kk, k.k2, k.rb, k.cum = (view(k, 2336 + 256 * n, 256) for n in range(6))
    k.wt, k.wi, k.wp, k.rt, k.kt, k.bt, k.kap, k.rsq, k.rtm = (view(k, 3872 + 256 * n, 256) for n in range(9))
    k.ab = view(k, 6176, 2, 4, P)
    k.rbk = view(k, 7200, 2, 4, P)
    k.rxi, k.rxit, k.rp = (view(k, 8224 + 512 * n, 1, 4, P) for n in range(3))
    k.tok = view(k, 9760, 3, 2, P)
    k.rrn, k.ru = view(k, 10528, 2, 64), view(k, 10656, 2, 64)
    k.z = view(k, 10784, 64)
    k.y, k.rg, k.bon = (view(k, 10848 + 256 * n, 256) for n in range(3))
    k.lraw = view(k, 11616, 2, 257)
    k.lorw = view(k, 12288, KB, 256)
    k.rv = k.small[:, 376:386]
    k.oka, k.nmid, k.fz = k.small[:, 386:387], k.small[:, 388:390], k.small[:, 390:391]


R_MU, R_W0, R_A0, R_KK, R_KA, R_RK, R_G, R_B = 0, 3, 4, 5, 6, 7, 8, 9


def rwl_gpsimd(k, pool, ready):
    for w in ready:
        pool.wait_ge(*w)
    pool.dma_start(k.lorw, feature_rows(k.t["w_in_0_2"])[:, :, 1536:RW_COLS]).then_inc(k.d["lat_w"], 16)


def rwl_tensor(k, pe):
    nc = k.nc
    pe.wait_ge(k.d["lat_w"], 16)
    for n in range(2):
        for kb in range(KB):
            mm = nc.tensor.matmul(k.PS[:, n, 0:L], k.lorw[:, kb, n * P:(n + 1) * P], k.XT[:, kb, 0:L],
                                  start=kb == 0, stop=kb == KB - 1)
    mm.then_inc(*k.rwl_pe.done("p"))


def rwl_scalar(k, act):
    act.wait_ge(*k.rwl_pe.at("p"))
    act.activation(k.lraw[:, :, 1:257], k.PS[:, 0:2, 0:L], ACT.Copy).then_inc(*k.rwl_act.done("raw"))
    act.wait_ge(*k.rwl_dve.at("mix"))
    act.activation(k.lw[0:64, 0, :], k.lw[0:64, 0, :], ACT.Tanh)
    act.activation(k.lw[:, 1, :], k.lw[:, 1, :], ACT.Sigmoid)
    act.drain().then_inc(*k.rwl_act.done("funcs"))


def rwl_vector(k, dve):
    nc = k.nc
    nc.vector.memset(k.lraw[:, :, 0:1], 0.0)
    nc.vector.memset(k.raw3[:, :, 0:1], 0.0)
    dve.wait_ge(*k.rwl_act.at("raw"))
    dve.drain()
    nc.vector.tensor_tensor(k.lw, k.lraw[:, :, 0:L], k.lraw[:, :, 1:257], ALU.subtract)
    dve.drain()
    for n in range(2):
        nc.vector.scalar_tensor_tensor(k.lw[:, n, :], k.lw[:, n, :], vec_col(k, 0, V_MUW + n),
                                       k.lraw[:, n, 1:257], ALU.mult, ALU.add)
    dve.drain().then_inc(*k.rwl_dve.done("mix"))



def rw_sync(k, sp):
    t = k.t
    w = feature_rows(t["w_in_0_2"])
    with sp.Fori(0, PAIRS) as p:
        sp.wait_ge(*k.rw_pe.at("ag", p - 1))
        for n in range(3):
            sp.dma_start(k.WH[:, n, :].rearrange("p (kb c) -> p kb c", kb=KB), w[:, :, ds(p * P + n * 512, P)]
                         ).then_inc(k.d["head_w"], 16)
        for to, name in ((k.l2[0:64, 0, :], "rw_w2_0_2"), (k.l2[64:128, 0, :], "rw_a2_0_2"),
                         (k.l2[:, 1, :], "rw_g2_0_2")):
            sp.dma_start(to, t[name][:, ds(p * P, P)]).then_inc(k.d["lora_w"], 16)


def rw_tensor(k, pe, loads):
    nc, ps, S, A, V = k.nc, k.PS, k.rw_pe, k.rw_act, k.rw_dve
    w = [k.WH[:, n, :].rearrange("p (kb c) -> p kb c", kb=KB) for n in range(3)]
    rows = [slice(0, 64), slice(64, 128)]
    tcol = [slice(0, P), slice(P, 2 * P)]

    def unit(buf, hh, m, tile):
        return buf[:, hh, 2 * m + tile, :]

    pe.wait_ge(*k.rwl_act.at("funcs"))
    with pe.Fori(0, PAIRS) as p:
        pe.wait_ge(k.d["head_w"], p * 48 + (16 * loads + 48))
        pe.wait_ge(k.d["lora_w"], p * 48 + 48)
        pe.wait_ge(*V.at("out", p - 1))
        for n, bank, c in ((0, 0, 0), (1, 0, L), (2, 1, 0)):
            for kb in range(KB):
                mm = nc.tensor.matmul(ps[:, bank, c:c + L], w[n][:, kb, :], k.XT[:, kb, 0:L],
                                      start=kb == 0, stop=kb == KB - 1)
            if n == 1:
                mm.then_inc(*S.done("rk"))
        nc.tensor.matmul(ps[:, 1, L:2 * L], k.l2[0:64, 0, :], k.lw[0:64, 0, :], start=True, stop=True
                         ).then_inc(*S.done("vw"))
        nc.tensor.matmul(ps[:, 2, 0:L], k.l2[64:128, 0, :], k.lw[64:128, 0, :], start=True, stop=True)
        nc.tensor.matmul(ps[:, 2, L:2 * L], k.l2[:, 1, :], k.lw[:, 1, :], start=True, stop=True
                         ).then_inc(*S.done("ag"))
        pe.wait_ge(*V.at("ksq", p))
        nc.tensor.matmul(ps[:, 3, 0:L], mat(k, C_ONES64), k.rsq, start=True, stop=True).then_inc(*S.done("ssk"))
        pe.wait_ge(*V.at("bo", p))
        nc.tensor.matmul(ps[:, 3, L:2 * L], mat(k, C_ONES64), k.bon, start=True, stop=True).then_inc(*S.done("bo"))
        pe.wait_ge(*V.at("til", p))
        for hh in range(2):
            r = rows[hh]
            for rhs, bank in ((k.kap, 4 + 2 * hh), (k.rt, 5 + 2 * hh)):
                for m, lhs in ((0, k.bt), (1, k.kt)):
                    for tile in range(2):
                        c = (2 * m + tile) * P
                        mm = nc.tensor.matmul(ps[:, bank, c:c + P], lhs[r, tcol[tile]], rhs[r, tcol[tile]],
                                              start=True, stop=True)
            mm.then_inc(*S.done(f"m{hh}"))
        for n, src in enumerate((k.rkv[:, 2, :], k.bt, k.kt)):
            for tile in range(2):
                c = (2 * n + tile) % 4 * P
                mm = nc.tensor.transpose(ps[:, n // 2, c:c + P], src[:, tcol[tile]], mat(k, C_ID))
        mm.then_inc(*S.done("tr"))
        pe.wait_ge(*V.at("ab", p))
        inverse_tensor(k, pe, p, 1, S, V, lambda g, n: unit(k.ab, n // 2, 0, n % 2), k.rxi, k.rxit, k.rp,
                       (4,), (5,), (6,))
        pe.wait_ge(*A.at("tok", p))
        for tile in range(2):
            for hh in range(2):
                r = rows[hh]
                if tile:
                    pe.wait_ge(*V.at("z", p))
                    nc.tensor.matmul(ps[:, hh, 0:64], k.kap[r, tcol[tile]], k.z[r, :], start=True, stop=False)
                nc.tensor.matmul(ps[:, hh, 0:64], unit(k.ab, hh, 1, tile), k.tok[:, 0, tile, r],
                                 start=tile == 0, stop=True).then_inc(*S.done(f"rn{tile}{hh}"))
            for hh in range(2):
                pe.wait_ge(*V.at(f"rn{tile}{hh}", p))
                pe.wait_ge(*V.at(f"x{LEVELS - 1}0", p))
                nc.tensor.matmul(ps[:, hh, 64:128], k.rxit[:, 0, 2 * hh + tile, :], k.rrn[:, hh, :],
                                 start=True, stop=True).then_inc(*S.done(f"u{tile}{hh}"))
            for hh in range(2):
                r = rows[hh]
                pe.wait_ge(*V.at(f"u{tile}{hh}", p))
                nc.tensor.matmul(ps[r, 2, tcol[tile]], k.ru[:, hh, :], unit(k.rbk, hh, 0, tile),
                                 start=True, stop=False)
                if tile:
                    nc.tensor.matmul(ps[r, 2, tcol[tile]], k.z[r, :], k.rt[r, tcol[tile]], start=False, stop=False)
                mm = nc.tensor.matmul(ps[r, 2, tcol[tile]], k.tok[:, 0, tile, r], unit(k.rbk, hh, 1, tile),
                                      start=False, stop=True)
                if tile == 0:
                    nc.tensor.matmul(ps[r, 7, 0:64], k.tok[:, 1, tile, r], k.ru[:, hh, :], start=True, stop=False)
                    mm = nc.tensor.matmul(ps[r, 7, 0:64], k.tok[:, 2, tile, r], k.tok[:, 0, tile, r],
                                          start=False, stop=True)
            mm.then_inc(*S.done("y" if tile else "z"))
        pe.wait_ge(*A.at("y", p))
        nc.tensor.matmul(ps[:, 0, 0:L], mat(k, C_ONES64), k.y, start=True, stop=True).then_inc(*S.done("mean"))
        pe.wait_ge(*V.at("ysq", p))
        nc.tensor.matmul(ps[:, 1, 0:L], mat(k, C_ONES64), k.rsq, start=True, stop=True).then_inc(*S.done("var"))


def rw_scalar(k, act):
    ps, S, T, V = k.PS, k.rw_act, k.rw_pe, k.rw_dve
    with act.Fori(0, PAIRS) as p:
        act.wait_ge(*T.at("rk", p))
        act.activation(k.raw3[:, 0:2, 1:257], ps[:, 0, :].rearrange("p (n c) -> p n c", n=2), ACT.Copy)
        act.wait_ge(*T.at("vw", p))
        act.activation(k.raw3[:, 2, 1:257], ps[:, 1, 0:L], ACT.Copy)
        act.drain().then_inc(*S.done("raw"))
        act.wait_ge(*V.at("head", p))
        act.activation(k.ld, ps[:, 1, L:2 * L], ACT.Sigmoid, bias=k.rv[:, R_W0:R_W0 + 1]).then_inc(*S.done("w"))
        act.wait_ge(*T.at("ag", p))
        act.activation(k.ra, ps[:, 2, 0:L], ACT.Sigmoid, bias=k.rv[:, R_A0:R_A0 + 1]).then_inc(*S.done("a"))
        act.activation(k.rg, ps[:, 2, L:2 * L], ACT.Copy).then_inc(*S.done("g"))
        act.wait_ge(*V.at("kmax", p))
        act.activation(k.rtm, k.rtm, ACT.Ln, scale=float(2 ** GUARD_LOG2))
        act.drain()
        act.activation(k.rtm, k.rtm, ACT.Exp, scale=-0.5, bias=k.eps[:, E_SHIFT:E_SHIFT + 1]
                       ).then_inc(*S.done("knorm"))
        act.wait_ge(*V.at("cum", p))
        for tile in range(2):
            c = slice(tile * P, (tile + 1) * P)
            mid = k.cum[:, tile * P + 63:tile * P + 64]
            act.activation(k.wt[:, c], k.cum[:, c], ACT.Exp, bias=k.nmid[:, tile:tile + 1])
            act.activation(k.wi[:, c], k.cum[:, c], ACT.Exp, scale=-1.0, bias=mid)
            act.activation(k.wp[:, c], k.wp[:, c], ACT.Exp, bias=k.nmid[:, tile:tile + 1])
        act.activation(k.fz, k.fz, ACT.Exp)
        act.drain().then_inc(*S.done("ws"))
        act.wait_ge(*T.at("tr", p))
        act.activation(k.tok[:, 0:2, :, :].rearrange("p a b c -> p (a b c)"), ps[:, 0, :], ACT.Copy)
        act.activation(k.tok[:, 2, :, :].rearrange("p b c -> p (b c)"), ps[:, 1, 0:L], ACT.Copy)
        act.drain().then_inc(*S.done("tok"))
        act.wait_ge(*T.at("y", p))
        act.activation(k.y, ps[:, 2, 0:L], ACT.Copy).then_inc(*S.done("y"))
        act.wait_ge(*T.at("var", p))
        rsqrt(k, act, k.rtm, ps[:, 1, 0:L], 1.0 / 64, k.eps[:, E_GN:E_GN + 1]).then_inc(*S.done("gnorm"))


def rw_vector(k, dve):
    nc, ps, S, T, A = k.nc, k.PS, k.rw_dve, k.rw_pe, k.rw_act
    tt, ts, stt = nc.vector.tensor_tensor, nc.vector.tensor_scalar, nc.vector.scalar_tensor_tensor
    vecs = k.vecs[:, 1, 0:40].rearrange("p (a n) -> p a n", n=4)
    rv = lambda c: k.rv[:, c:c + 1]
    r, kk_, v = (k.rkv[:, n, :] for n in range(3))
    with dve.Fori(0, PAIRS) as p:
        nc.vector.tensor_copy(k.rv.unsqueeze(2), vecs[:, :, ds(p, 1)])
        dve.drain()
        ts(k.oka, rv(R_KA), -1.0, 1.0, ALU.mult, ALU.add)
        dve.drain().then_inc(*S.done("head"))
        dve.wait_ge(*A.at("raw", p))
        tt(k.rkv, k.raw3[:, :, 0:L], k.raw3[:, :, 1:257], ALU.subtract)
        dve.drain()
        for n in range(3):
            stt(k.rkv[:, n, :], k.rkv[:, n, :], rv(R_MU + n), k.raw3[:, n, 1:257], ALU.mult, ALU.add)
        dve.drain().then_inc(*S.done("mix"))
        ts(k.kk, kk_, rv(R_KK), None, ALU.mult)
        dve.drain()
        tt(k.rsq, k.kk, k.kk, ALU.mult).then_inc(*S.done("ksq"))
        dve.wait_ge(*T.at("ssk", p))
        ts(k.rtm, ps[:, 3, 0:L], 1e-24, None, ALU.max).then_inc(*S.done("kmax"))
        dve.wait_ge(*A.at("a", p))
        ts(k.ld, k.ld, RW_DECAY, None, ALU.mult)
        ts(k.k2, k.ra, rv(R_KA), k.oka, ALU.mult, ALU.add)
        dve.drain()
        for tile in range(2):
            c = slice(tile * P, (tile + 1) * P)
            nc.vector.tensor_tensor_scan(k.cum[:, c], mat(k, C_ONES), k.ld[:, c], 0.0, ALU.mult, ALU.add)
        tt(k.k2, k.k2, kk_, ALU.mult)
        dve.drain()
        tt(k.wp, k.cum, k.ld, ALU.subtract)
        for tile in range(2):
            ts(k.nmid[:, tile:tile + 1], k.cum[:, tile * P + 63:tile * P + 64], -1.0, None, ALU.mult)
        ts(k.fz, k.cum[:, 127:128], k.cum[:, 63:64], k.cum[:, P + 63:P + 64], ALU.subtract, ALU.add)
        dve.drain().then_inc(*S.done("cum"))
        stt(k.bon, r, rv(R_RK), k.k2, ALU.mult, ALU.mult).then_inc(*S.done("bo"))
        dve.wait_ge(*A.at("knorm", p))
        tt(k.kk, k.kk, k.rtm, ALU.mult)
        dve.drain()
        tt(k.rb, k.kk, k.ra, ALU.mult)
        dve.drain()
        dve.wait_ge(*A.at("ws", p))
        tt(k.rt, r, k.wt, ALU.mult)
        tt(k.kap, k.kk, k.wp, ALU.mult)
        tt(k.bt, k.rb, k.wi, ALU.mult)
        tt(k.kt, k.k2, k.wi, ALU.mult)
        dve.drain().then_inc(*S.done("til"))
        dve.wait_ge(*T.at("bo", p))
        tt(k.bon, v, ps[:, 3, L:2 * L], ALU.mult)
        for hh in range(2):
            dve.wait_ge(*T.at(f"m{hh}", p))
            tt(k.ab[:, hh, :, :], tiles_of(k, 4 + 2 * hh), bcast(mat(k, C_SUP), 4), ALU.mult)
            i = tt(k.rbk[:, hh, :, :], tiles_of(k, 5 + 2 * hh), bcast(mat(k, C_UP), 4), ALU.mult)
        i.then_inc(*S.done("ab"))
        inverse_vector(k, dve, p, 1, T, S, k.rxi, k.rxit, k.rp, (4,), (5,), (6,), (False,))
        for tile in range(2):
            for hh in range(2):
                dve.wait_ge(*T.at(f"rn{tile}{hh}", p))
                ts(k.rrn[:, hh, :], ps[:, hh, 0:64], -1.0, None, ALU.mult).then_inc(*S.done(f"rn{tile}{hh}"))
            for hh in range(2):
                dve.wait_ge(*T.at(f"u{tile}{hh}", p))
                nc.vector.tensor_copy(k.ru[:, hh, :], ps[:, hh, 64:128]).then_inc(*S.done(f"u{tile}{hh}"))
            if tile == 0:
                dve.wait_ge(*T.at("z", p))
                ts(k.z, ps[:, 7, 0:64], k.fz, None, ALU.mult).then_inc(*S.done("z"))
        dve.wait_ge(*T.at("mean", p))
        stt(k.y, ps[:, 0, 0:L], -1.0 / 64, k.y, ALU.mult, ALU.add)
        dve.drain()
        tt(k.rsq, k.y, k.y, ALU.mult).then_inc(*S.done("ysq"))
        dve.wait_ge(*A.at("gnorm", p))
        tt(k.y, k.y, k.rtm, ALU.mult)
        dve.drain()
        ts(k.y, k.y, rv(R_G), rv(R_B), ALU.mult, ALU.add)
        dve.drain()
        tt(k.y, k.y, k.bon, ALU.add)
        dve.drain()
        tt(k.OT[:, ds(p, 1), 0:L].rearrange("p a n -> p (a n)"), k.y, k.rg, ALU.mult).then_inc(*S.done("out"))



QN = 2
MLA_SCALE = MLA_QK ** -0.5


def declare_mla(k):
    k.lat_pe = Steps(k, "lat_pe", "p ss rot")
    k.lat_act = Steps(k, "lat_act", "copy norm")
    k.lat_dve = Steps(k, "lat_dve", "sq out")
    a_pe, a_act, a_dve = attn_steps()
    k.mla_pe = Steps(k, "mla_pe", f"p rot {a_pe}")
    k.mla_act = Steps(k, "mla_act", f"copy {a_act}")
    k.mla_dve = Steps(k, "mla_dve", f"rope {a_dve}")
    k.latw = view(k, 12288, KB, 416)
    k.ql = view(k, 0, 3, 256)
    k.qsq = view(k, 768, 3, 256)
    k.qrn = view(k, 1536, 2, 256)
    k.wq = view(k, 2048, QN, 192)
    k.wkv = view(k, 2432, 256)
    k.kpe, k.kpt = view(k, 2688, 256), view(k, 2944, 256)


def lat_gpsimd(k, pool, ready):
    for w in ready:
        pool.wait_ge(*w)
    pool.dma_start(k.latw, feature_rows(k.t["w_in_0_2"])[:, :, RW_COLS:RW_COLS + 416]).then_inc(k.d["lat_w"], 16)


def lat_tensor(k, pe):
    nc, ps = k.nc, k.PS
    pe.wait_ge(k.d["lat_w"], 32)
    for out, c, n in ((ps[:, 0, 0:L], 0, P), (ps[:, 0, L:2 * L], P, P), (ps[:, 1, 0:L], 2 * P, P),
                      (ps[64:96, 1, L:2 * L], 3 * P, 32)):
        for kb in range(KB):
            mm = nc.tensor.matmul(out, k.latw[:, kb, c:c + n], k.XT[:, kb, 0:L], start=kb == 0, stop=kb == KB - 1)
    mm.then_inc(*k.lat_pe.done("p"))
    pe.wait_ge(*k.lat_dve.at("sq"))
    for n in range(QN):
        nc.tensor.matmul(ps[:, 2, 0:L], mat(k, C_ONES), k.qsq[:, n, :], start=n == 0, stop=n == QN - 1)
    nc.tensor.matmul(ps[:, 2, L:2 * L], mat(k, C_ONES), k.qsq[:, 2, :], start=True, stop=True
                     ).then_inc(*k.lat_pe.done("ss"))
    nc.tensor.matmul(ps[64:96, 3, 0:L], k.mats[64:96, C_RMLA, 64:96], k.kpe[64:96, :], start=True, stop=True
                     ).then_inc(*k.lat_pe.done("rot"))


def lat_scalar(k, act):
    ps = k.PS
    act.wait_ge(*k.lat_pe.at("p"))
    act.activation(k.ql[:, 0:2, :].rearrange("p a b -> p (a b)"), ps[:, 0, :], ACT.Copy)
    act.activation(k.ql[:, 2, :], ps[:, 1, 0:L], ACT.Copy)
    act.activation(k.kpe[64:96, :], ps[64:96, 1, L:2 * L], ACT.Copy)
    act.drain().then_inc(*k.lat_act.done("copy"))
    act.wait_ge(*k.lat_pe.at("ss"))
    rsqrt(k, act, k.qrn[:, 0, :], ps[:, 2, 0:L], 1.0 / (QN * P), k.eps[:, E_RMS:E_RMS + 1])
    rsqrt(k, act, k.qrn[:, 1, :], ps[:, 2, L:2 * L], 1.0 / P, k.eps[:, E_RMS:E_RMS + 1])
    act.drain().then_inc(*k.lat_act.done("norm"))


def lat_vector(k, dve):
    nc, ps = k.nc, k.PS
    dve.wait_ge(*k.lat_act.at("copy"))
    nc.vector.tensor_tensor(k.qsq, k.ql, k.ql, ALU.mult).then_inc(*k.lat_dve.done("sq"))
    dve.wait_ge(*k.lat_pe.at("rot"))
    s = slice(64, 96)
    nc.vector.tensor_tensor(k.kpt[s, :], ps[s, 3, 0:L], k.rope[s, T_MLA, 1, :], ALU.mult)
    nc.vector.tensor_tensor(k.kpe[s, :], k.kpe[s, :], k.rope[s, T_MLA, 0, :], ALU.mult)
    dve.drain()
    for hh in range(2):
        nc.vector.tensor_tensor(k.ak[s, hh, :], k.kpe[s, :], k.kpt[s, :], ALU.add)
    dve.wait_ge(*k.lat_act.at("norm"))
    for n, (g, rn) in enumerate(((V_QN, 0), (V_QN + 1, 0), (V_KVN, 1))):
        nc.vector.scalar_tensor_tensor(k.ql[:, n, :], k.ql[:, n, :], vec_col(k, 0, g), k.qrn[:, rn, :],
                                       ALU.mult, ALU.mult)
    dve.drain().then_inc(*k.lat_dve.done("out"))



def mla_sync(k, sp, ready):
    t = k.t
    for w in ready:
        sp.wait_ge(*w)
    with sp.Fori(0, PAIRS) as p:
        sp.wait_ge(*k.mla_pe.at("p", p - 1))
        sp.dma_start(k.wq, t["mla_wuq_0_2"].rearrange("(a p) n -> p a n", p=P)[:, :, ds(p * 192, 192)]
                     ).then_inc(k.d["lora_w"], 16)
        sp.dma_start(k.wkv, t["mla_wukv_0_2"][:, ds(p * 256, 256)]).then_inc(k.d["lora_w"], 16)


def mla_tensor(k, pe, loads):
    nc, ps, S, A, V = k.nc, k.PS, k.mla_pe, k.mla_act, k.mla_dve
    pe.wait_ge(*k.lat_dve.at("out"))
    with pe.Fori(0, PAIRS) as p:
        pe.wait_ge(k.d["lora_w"], p * 32 + (16 * loads + 32))
        pe.wait_ge(*V.at("w1", p - 1))
        for hh in range(2):
            for n in range(QN):
                nc.tensor.matmul(ps[0:96, 0, hh * L:(hh + 1) * L], k.wq[:, n, hh * 96:(hh + 1) * 96], k.ql[:, n, :],
                                 start=n == 0, stop=n == QN - 1)
            nc.tensor.matmul(ps[0:64, 1, hh * L:(hh + 1) * L], k.wkv[:, hh * P:hh * P + 64], k.ql[:, 2, :],
                             start=True, stop=True)
        for tile in range(2):
            for hh in range(2):
                c = (2 * tile + hh) * 64
                mm = nc.tensor.matmul(ps[:, 2, c:c + 64], k.ql[:, 2, tile * P:(tile + 1) * P],
                                      k.wkv[:, hh * P + 64:hh * P + 128], start=True, stop=True)
        mm.then_inc(*S.done("p"))
        pe.wait_ge(*A.at("copy", p))
        nc.tensor.matmul(ps[0:96, 3, :], k.mats[0:96, C_RMLA, 0:96], k.aq[0:96, :, :].rearrange("p a b -> p (a b)"),
                         start=True, stop=True).then_inc(*S.done("rot"))
        pe.wait_ge(*V.at("rope", p))
        attn_tensor(k, pe, p, S, A, V, lambda hh: k.aq[0:96, hh, :], lambda hh: k.ak[0:96, hh, :],
                    lambda hh, tile: k.av[:, tile, 64 * hh:64 * hh + 64])


def mla_scalar(k, act):
    ps, S, T, V = k.PS, k.mla_act, k.mla_pe, k.mla_dve
    with act.Fori(0, PAIRS) as p:
        act.wait_ge(*T.at("p", p))
        act.activation(k.aq[0:96, :, :].rearrange("p a b -> p (a b)"), ps[0:96, 0, :], ACT.Copy)
        act.activation(k.ak[0:64, :, :].rearrange("p a b -> p (a b)"), ps[0:64, 1, :], ACT.Copy)
        act.activation(k.av.rearrange("p a b -> p (a b)"), ps[:, 2, 0:L], ACT.Copy)
        act.drain().then_inc(*S.done("copy"))
        attn_scalar(k, act, p, S, T, V, k.OT[:, ds(p + 4, 1), 0:L].rearrange("p a n -> p (a n)"))


def mla_vector(k, dve):
    nc, ps, S, T, A = k.nc, k.PS, k.mla_dve, k.mla_pe, k.mla_act
    with dve.Fori(0, PAIRS) as p:
        dve.wait_ge(*T.at("rot", p))
        cos, sin = (bcast(k.rope[0:96, T_MLA, n, :], 2) for n in range(2))
        q, tmp = k.aq[0:96, :, :], k.atm[0:96, :].rearrange("p (a b) -> p a b", a=2)
        nc.vector.tensor_tensor(tmp, ps[0:96, 3, :].rearrange("p (a b) -> p a b", a=2), sin, ALU.mult)
        nc.vector.tensor_tensor(q, q, cos, ALU.mult)
        dve.drain()
        nc.vector.tensor_tensor(q, q, tmp, ALU.add).then_inc(*S.done("rope"))
        attn_vector(k, dve, p, S, T, A, MLA_SCALE)



SCALE64 = 64 ** -0.5
FOX_F, MOBA_0 = 1536, 1544


def declare_fox(k):
    k.fg_pe = Steps(k, "fg_pe", "f d")
    k.fg_act = Steps(k, "fg_act", "soft rows")
    k.fg_dve = Steps(k, "fg_dve", "nabs g col")
    a_pe, a_act, a_dve = attn_steps()
    k.fox_pe = Steps(k, "fox_pe", f"qk v {a_pe}")
    k.fox_act = Steps(k, "fox_act", f"copy {a_act}")
    k.fox_dve = Steps(k, "fox_dve", f"head {a_dve}")
    k.moba_pe = Steps(k, "moba_pe", f"qk v rot {a_pe}")
    k.moba_act = Steps(k, "moba_act", f"copy {a_act}")
    k.moba_dve = Steps(k, "moba_dve", f"rope {a_dve}")
    k.fw = view(k, 12288, KB, 8)
    k.fbf = view(k, 12352, 8)
    k.fx, k.fe, k.fgg = view(k, 12360, 2, 8), view(k, 12376, 2, 8), view(k, 12392, 2, 8)
    k.fcol = k.small[:, 460:476].rearrange("p (t h) -> p t h", t=2)
    k.fcp = k.small[:, 476:480].rearrange("p (t h) -> p t h", t=2)
    k.frw = k.S[0:8, 12416:12672]
    k.fr = view(k, 12672, 2, 256)


def fg_gpsimd(k, pool, ready):
    t, d = k.t, k.d
    for w in ready:
        pool.wait_ge(*w)
    pool.dma_start(k.fw, feature_rows(t["w_in_1_2"])[:, :, FOX_F:FOX_F + 8]).then_inc(d["forget_in"], 16)
    pool.dma_start(k.fbf, t["fox_bf_1_2"].partition_broadcast(P)).then_inc(d["forget_in"], 16)
    pool.wait_ge(*k.fg_act.at("rows"))
    pool.dma_start(k.frow, k.frw).then_inc(d["forget_store"], 16)
    pool.wait_ge(d["forget_store"], 16)
    with pool.Fori(0, PAIRS) as p:
        pool.wait_ge(*k.fox_dve.at("m1", p - 1))
        pool.dma_start(k.fr.rearrange("p a n -> p (a n)"),
                       k.frow.rearrange("(p a) n -> p (a n)", a=2)[ds(p, 1), :].rearrange("h n -> (h n)").partition_broadcast(P)
                       ).then_inc(d["forget_rows"], 16)


def fg_tensor(k, pe):
    nc, ps = k.nc, k.PS
    pe.wait_ge(k.d["forget_in"], 32)
    for tile in range(2):
        for kb in range(KB):
            mm = nc.tensor.matmul(ps[:, 4, tile * 8:tile * 8 + 8], k.XT[:, kb, tile * P:(tile + 1) * P], k.fw[:, kb, :],
                                  start=kb == 0, stop=kb == KB - 1)
    mm.then_inc(*k.fg_pe.done("f"))
    pe.wait_ge(*k.fg_dve.at("g"))
    nc.tensor.matmul(ps[:, 5, 0:8], mat(k, C_UP), k.fgg[:, 0, :], start=True, stop=True)
    nc.tensor.matmul(ps[:, 5, 8:16], mat(k, C_UP), k.fgg[:, 1, :], start=True, stop=False)
    nc.tensor.matmul(ps[:, 5, 8:16], mat(k, C_ONES), k.fgg[:, 0, :], start=False, stop=True)
    nc.tensor.matmul(ps[0:8, 6, 0:P], k.fgg[:, 0, :], mat(k, C_UP), start=True, stop=True)
    nc.tensor.matmul(ps[0:8, 6, P:L], k.fgg[:, 1, :], mat(k, C_UP), start=True, stop=False)
    nc.tensor.matmul(ps[0:8, 6, P:L], k.fgg[:, 0, :], mat(k, C_ONES), start=False, stop=True
                     ).then_inc(*k.fg_pe.done("d"))


def fg_scalar(k, act):
    act.wait_ge(*k.fg_dve.at("nabs"))
    act.activation(k.fe, k.fe, ACT.Exp)
    act.drain()
    act.activation(k.fe, k.fe, ACT.Ln, bias=1.0).then_inc(*k.fg_act.done("soft"))
    act.wait_ge(*k.fg_pe.at("d"))
    act.activation(k.frw, k.PS[0:8, 6, 0:L], ACT.Copy).then_inc(*k.fg_act.done("rows"))


def fg_vector(k, dve):
    nc, ps = k.nc, k.PS
    dve.wait_ge(k.d["forget_in"], 32)
    dve.wait_ge(*k.fg_pe.at("f"))
    nc.vector.tensor_tensor(k.fx, ps[:, 4, 0:16].rearrange("p (t h) -> p t h", t=2), bcast(k.fbf, 2), ALU.add)
    dve.drain()
    nc.vector.scalar_tensor_tensor(k.fe, k.fx, -1.0, k.fx, ALU.mult, ALU.min).then_inc(*k.fg_dve.done("nabs"))
    dve.wait_ge(*k.fg_act.at("soft"))
    nc.vector.scalar_tensor_tensor(k.fgg, k.fx, 0.0, k.fe, ALU.min, ALU.subtract).then_inc(*k.fg_dve.done("g"))
    dve.wait_ge(*k.fg_pe.at("d"))
    nc.vector.tensor_copy(k.fcol, ps[:, 5, 0:16].rearrange("p (t h) -> p t h", t=2)).then_inc(*k.fg_dve.done("col"))
    dve.drain()


def pair_sync(k, sp, steps, last, col, base_cols=512):
    w = feature_rows(k.t["w_in_1_2"])
    with sp.Fori(0, PAIRS) as p:
        sp.wait_ge(*steps.at(last, p - 1))
        for n in range(3):
            sp.dma_start(k.WH[:, n, :].rearrange("p (kb c) -> p kb c", kb=KB),
                         w[:, :, ds(p * P + (col + n * base_cols), P)]).then_inc(k.d["head_w"], 16)


def pair_project(k, pe, S):
    nc, ps = k.nc, k.PS
    w = [k.WH[:, n, :].rearrange("p (kb c) -> p kb c", kb=KB) for n in range(3)]
    for n in range(2):
        for kb in range(KB):
            mm = nc.tensor.matmul(ps[:, 0, n * L:(n + 1) * L], w[n][:, kb, :], k.XT[:, kb, 0:L],
                                  start=kb == 0, stop=kb == KB - 1)
    mm.then_inc(*S.done("qk"))
    for tile in range(2):
        for kb in range(KB):
            mm = nc.tensor.matmul(ps[:, 1, tile * P:(tile + 1) * P], k.XT[:, kb, tile * P:(tile + 1) * P],
                                  w[2][:, kb, :], start=kb == 0, stop=kb == KB - 1)
    mm.then_inc(*S.done("v"))


def pair_copy(k, act, p, S, T):
    act.wait_ge(*T.at("qk", p))
    act.activation(k.aq.rearrange("p a b -> p (a b)"), k.PS[:, 0, :], ACT.Copy)
    act.wait_ge(*T.at("v", p))
    act.activation(k.av.rearrange("p a b -> p (a b)"), k.PS[:, 1, 0:L], ACT.Copy)
    act.drain().then_inc(*S.done("copy"))


def pair_attention(k, pe, p, S, A, V):
    attn_tensor(k, pe, p, S, A, V, lambda hh: k.aq[64 * hh:64 * hh + 64, 0, :],
                lambda hh: k.aq[64 * hh:64 * hh + 64, 1, :], lambda hh, tile: k.av[:, tile, 64 * hh:64 * hh + 64])


def fox_tensor(k, pe, loads):
    S, A, V = k.fox_pe, k.fox_act, k.fox_dve
    pe.wait_ge(*k.fg_dve.at("col"))
    pe.wait_ge(*k.fg_act.at("rows"))
    with pe.Fori(0, PAIRS) as p:
        pe.wait_ge(k.d["head_w"], p * 48 + (16 * loads + 48))
        pair_project(k, pe, S)
        pe.wait_ge(*A.at("copy", p))
        pair_attention(k, pe, p, S, A, V)


def fox_scalar(k, act):
    S, T, V = k.fox_act, k.fox_pe, k.fox_dve
    with act.Fori(0, PAIRS) as p:
        pair_copy(k, act, p, S, T)
        attn_scalar(k, act, p, S, T, V, k.OT[:, ds(p, 1), 0:L].rearrange("p a n -> p (a n)"))


def fox_vector(k, dve):
    nc, S, T, A = k.nc, k.fox_dve, k.fox_pe, k.fox_act
    with dve.Fori(0, PAIRS) as p:
        for tile in range(2):
            i = nc.vector.tensor_copy(k.fcp[:, tile, :].unsqueeze(1),
                                      k.fcol[:, tile, :].rearrange("p (a b) -> p a b", b=2)[:, ds(p, 1), :])
        dve.drain().then_inc(*S.done("head"))
        dve.wait_ge(k.d["forget_rows"], p * 16 + 16)
        attn_vector(k, dve, p, S, T, A, SCALE64,
                    lambda hh: (lambda q: k.fcp[:, q, hh:hh + 1], k.fr[:, hh, :]))


def moba_tensor(k, pe, loads):
    nc, S, A, V = k.nc, k.moba_pe, k.moba_act, k.moba_dve
    with pe.Fori(0, PAIRS) as p:
        pe.wait_ge(k.d["head_w"], p * 48 + (16 * loads + 48))
        pair_project(k, pe, S)
        pe.wait_ge(*A.at("copy", p))
        nc.tensor.matmul(k.PS[:, 2, :], mat(k, C_RMOBA), k.aq.rearrange("p a b -> p (a b)"), start=True, stop=True
                         ).then_inc(*S.done("rot"))
        pe.wait_ge(*V.at("rope", p))
        pair_attention(k, pe, p, S, A, V)


def moba_scalar(k, act):
    S, T, V = k.moba_act, k.moba_pe, k.moba_dve
    with act.Fori(0, PAIRS) as p:
        pair_copy(k, act, p, S, T)
        attn_scalar(k, act, p, S, T, V, k.OT[:, ds(p + 4, 1), 0:L].rearrange("p a n -> p (a n)"))


def moba_vector(k, dve):
    nc, ps, S, T, A = k.nc, k.PS, k.moba_dve, k.moba_pe, k.moba_act
    with dve.Fori(0, PAIRS) as p:
        dve.wait_ge(*T.at("rot", p))
        cos, sin = (bcast(k.rope[:, T_MOBA, n, :], 2) for n in range(2))
        tmp = k.atm.rearrange("p (a b) -> p a b", a=2)
        nc.vector.tensor_tensor(tmp, ps[:, 2, :].rearrange("p (a b) -> p a b", a=2), sin, ALU.mult)
        nc.vector.tensor_tensor(k.aq, k.aq, cos, ALU.mult)
        dve.drain()
        nc.vector.tensor_tensor(k.aq, k.aq, tmp, ALU.add).then_inc(*S.done("rope"))
        attn_vector(k, dve, p, S, T, A, SCALE64)



SLOTS = P
SWEEPS = L // SLOTS
E_TURNS = D_EXPERT // 512
NE = EXPERTS + 1


class Sweep:

    def __init__(self, k, name, slots):
        self.slots = slots
        both = lambda s: " ".join(f"{w}{u}" for u in range(2) for w in s.split())
        self.pe = Steps(k, name + "_pe", both("acc ga tr sc0 sc1"))
        self.act = Steps(k, name + "_act", both("ga tr"))
        self.dve = Steps(k, name + "_dve", both("g y x0 x1"))
        self.pre_pe = Steps(k, name + "p_pe", "ga tr")
        self.pre_act = Steps(k, name + "p_act", "ga tr")
        self.pre_dve = Steps(k, name + "p_dve", "g")


def declare_moe(k):
    k.rt_pe = Steps(k, "rt_pe", "logits places")
    k.rt_act = Steps(k, "rt_act", "gates")
    k.rt_dve = Steps(k, "rt_dve", "top chosen places")
    bufs = (k.WF.rearrange("p a b c -> p (a b c)"), k.WO.rearrange("p a b -> p (a b)"))
    over = [Slot(k, "over" + "ab"[s], bufs[s]) for s in range(2)]
    k.sweeps = [Sweep(k, "moe", k.dense), Sweep(k, "more", over)]
    k.rw_ = view(k, 6144, KB, 8)
    k.lg = view(k, 6216, 2, 8)
    k.top = view(k, 6232, 2, 8)
    k.tix = view(k, 6248, 2, 8)
    k.tif = view(k, 6264, 2, 8)
    k.gt = view(k, 6280, 2, 2)
    k.eq, k.eq2 = view(k, 6284, 2, 8), view(k, 6300, 2, 8)
    k.chosen = view(k, 6316, 2, 8)
    k.route = view(k, 6332, 2, 2, NE)
    k.chosen_route = view(k, 6368, 2, 2)
    k.most, k.flag = view(k, 6372, 1), view(k, 6373, 1)
    k.counts = view(k, 6376, 8)
    k.ge_ = view(k, 6400, 2, 2, SLOTS)
    k.gated = view(k, 6912, 2, 2, SLOTS)
    k.gatedt = view(k, 7424, 2, L)
    k.ye = view(k, 7936, 2, D)
    k.xte = view(k, 9984, 2, KB, SLOTS)
    k.xg = view(k, 3072, 2, D)
    k.slot_iota = view(k, 12032, P)


def router_gpsimd(k, pool, ready):
    for w in ready:
        pool.wait_ge(*w)
    pool.dma_start(k.rw_, feature_rows(k.t["router_1_2"])).then_inc(k.d["router_in"], 16)
    pool.dma_start(k.slot_iota, k.t["const_iota"].partition_broadcast(P)).then_inc(k.d["router_in"], 16)


def router_tensor(k, pe):
    nc, ps = k.nc, k.PS
    pe.wait_ge(k.d["router_in"], 32)
    for tile in range(2):
        for kb in range(KB):
            mm = nc.tensor.matmul(ps[:, 7, tile * 8:tile * 8 + 8], k.XT[:, kb, tile * P:(tile + 1) * P],
                                  k.rw_[:, kb, :], start=kb == 0, stop=kb == KB - 1)
    mm.then_inc(*k.rt_pe.done("logits"))
    pe.wait_ge(*k.rt_dve.at("chosen"))
    nc.tensor.matmul(ps[:, 6, 0:8], mat(k, C_SUP), k.chosen[:, 0, :], start=True, stop=True)
    nc.tensor.matmul(ps[:, 6, 8:16], mat(k, C_SUP), k.chosen[:, 1, :], start=True, stop=False)
    nc.tensor.matmul(ps[:, 6, 8:16], mat(k, C_ONES), k.chosen[:, 0, :], start=False, stop=True)
    nc.tensor.matmul(ps[:, 6, 16:24], mat(k, C_ONES), k.chosen[:, 0, :], start=True, stop=False)
    nc.tensor.matmul(ps[:, 6, 16:24], mat(k, C_ONES), k.chosen[:, 1, :], start=False, stop=True
                     ).then_inc(*k.rt_pe.done("places"))


def router_scalar(k, act):
    act.wait_ge(*k.rt_dve.at("top"))
    act.activation(k.gt[:, :, 1:2], k.gt[:, :, 1:2], ACT.Exp).then_inc(*k.rt_act.done("gates"))


def router_vector(k, dve):
    nc = k.nc
    tt, ts, stt = nc.vector.tensor_tensor, nc.vector.tensor_scalar, nc.vector.scalar_tensor_tensor
    dve.wait_ge(k.d["router_in"], 32)
    for tile in range(2):
        tt(k.xg[:, tile, :], view(k, D * (1 + tile), D), k.WH[:, 1, :], ALU.mult)
    dve.wait_ge(*k.rt_pe.at("logits"))
    nc.vector.tensor_copy(k.lg, k.PS[:, 7, 0:16].rearrange("p (t e) -> p t e", t=2))
    dve.drain()
    for tile in range(2):
        nc.vector.max(k.top[:, tile, :], k.lg[:, tile, :])
    dve.drain()
    for tile in range(2):
        nc.vector.max_index(k.tix[:, tile, :].bitcast(U32), k.top[:, tile, :], k.lg[:, tile, :])
    tt(k.gt[:, :, 1:2], k.top[:, :, 1:2], k.top[:, :, 0:1], ALU.subtract)
    dve.drain()
    nc.vector.tensor_copy(k.tif, k.tix.bitcast(U32)).then_inc(*k.rt_dve.done("top"))
    dve.drain()
    for tile in range(2):
        ts(k.eq[:, tile, :], k.slot_iota[:, 0:EXPERTS], k.tif[:, tile, 0:1], None, ALU.is_equal)
        ts(k.eq2[:, tile, :], k.slot_iota[:, 0:EXPERTS], k.tif[:, tile, 1:2], None, ALU.is_equal)
    dve.drain()
    tt(k.chosen, k.eq, k.eq2, ALU.add).then_inc(*k.rt_dve.done("chosen"))
    dve.wait_ge(*k.rt_act.at("gates"))
    ts(k.gt[:, :, 0:1], k.gt[:, :, 1:2], 1.0, None, ALU.add)
    dve.drain()
    nc.vector.reciprocal(k.gt[:, :, 0:1], k.gt[:, :, 0:1])
    dve.drain()
    tt(k.gt[:, :, 1:2], k.gt[:, :, 1:2], k.gt[:, :, 0:1], ALU.mult)
    nc.vector.memset(k.route[:, 0, :, EXPERTS:NE], -1.0)
    nc.vector.memset(k.route[:, 1, :, EXPERTS:NE], 0.0)
    dve.drain()
    for tile in range(2):
        ts(k.eq[:, tile, :], k.eq[:, tile, :], k.gt[:, tile, 0:1], None, ALU.mult)
        ts(k.eq2[:, tile, :], k.eq2[:, tile, :], k.gt[:, tile, 1:2], None, ALU.mult)
    dve.drain()
    tt(k.route[:, 1, :, 0:EXPERTS], k.eq, k.eq2, ALU.add)
    dve.wait_ge(*k.rt_pe.at("places"))
    stt(k.lg, k.PS[:, 6, 0:16].rearrange("p (t e) -> p t e", t=2), 1.0, k.chosen, ALU.add, ALU.mult)
    nc.vector.tensor_copy(k.counts, k.PS[:, 6, 16:24])
    dve.drain()
    ts(k.route[:, 0, :, 0:EXPERTS], k.lg, -1.0, None, ALU.add)
    nc.vector.reduce_max(k.most, k.counts, AX)
    dve.drain()
    nc.vector.tensor_copy(k.flag.bitcast(I32), k.most)
    dve.drain().then_inc(*k.rt_dve.done("places"))


def moe_sync(k, sp, sweep, base):
    t = k.t
    wg, wu = (t[name].rearrange("e (kb p) n -> p e kb n", p=P) for name in ("moe_wg_1_2", "moe_wu_1_2"))
    wd = t["moe_wd_1_2"].rearrange("e (b p) n -> p (e b) n", p=P)
    with sp.Fori(0, EXPERTS) as e:
        with sp.Fori(0, E_TURNS) as j:
            for s in range(2):
                cols = ds(j * 512 + s * ROUND, ROUND)
                gu = [w[:, ds(e, 1), :, cols].rearrange("p e kb n -> p (e kb) n") for w in (wg, wu)]
                load_round(k, sp, sweep.slots[s], e * E_TURNS + j + base[s], *gu,
                           wd[:, ds(e * (4 * E_TURNS) + j * 4 + 2 * s, 2), :])


def gather_tensor(k, pe, u, steps, names, g_ready, act):
    nc, ps = k.nc, k.PS
    pe.wait_ge(*g_ready)
    for kb in range(KB):
        c = (kb % 4) * SLOTS
        for tile in range(2):
            mm = nc.tensor.matmul(ps[:, 6 + kb // 4, c:c + SLOTS], k.xg[:, tile, kb * P:(kb + 1) * P],
                                  k.ge_[:, u, tile, :], start=tile == 0, stop=tile == 1)
    mm.then_inc(*steps.done(names[0]))
    pe.wait_ge(*act)
    for tile in range(2):
        mm = nc.tensor.transpose(ps[:, 6, tile * P:(tile + 1) * P], k.gated[:, u, tile, :], mat(k, C_ID))
    mm.then_inc(*steps.done(names[1]))


def moe_tensor(k, pe, sweep, base):
    nc, ps, S, A, V = k.nc, k.PS, sweep.pe, sweep.act, sweep.dve
    gather_tensor(k, pe, 0, sweep.pre_pe, ("ga", "tr"), sweep.pre_dve.at("g"), sweep.pre_act.at("ga"))
    pe.wait_ge(*sweep.pre_act.at("tr"))
    with pe.Fori(0, EXPERTS // 2) as i:
        for u in range(2):
            acc = (2 * u, 2 * u + 1)
            zero_sum(k, True, acc)
            with pe.Fori(0, E_TURNS) as j:
                rnd = i * (2 * E_TURNS) + j + u * E_TURNS
                turn_tensor(k, pe, sweep.slots, TURN, [rnd + b for b in base],
                            lambda kb: k.xte[:, u, kb, :], SLOTS, k.hidm, acc)
            zero_sum(k, False, acc).then_inc(*S.done(f"acc{u}"))
            gather_tensor(k, pe, 1 - u, S, (f"ga{u}", f"tr{u}"), V.at(f"g{u}", i), A.at(f"ga{u}", i))
            pe.wait_ge(*V.at(f"y{u}", i))
            for tile in range(2):
                if tile:
                    pe.wait_ge(*V.at(f"x0{u}", i))
                else:
                    pe.wait_ge(*A.at(f"tr{u}", i))
                for half in range(2):
                    mm = nc.tensor.matmul(ps[:, 6 + half, :], k.gatedt[:, u, tile * P:(tile + 1) * P],
                                          k.ye[:, u, half * 512:(half + 1) * 512], start=True, stop=True)
                mm.then_inc(*S.done(f"sc{tile}{u}"))
            pe.wait_ge(*V.at(f"x1{u}", i))


def gather_scalar(k, act, u, steps, names, pe_ga, pe_tr):
    act.wait_ge(*pe_ga)
    for b in range(2):
        a = act.activation(k.xte[:, u, 4 * b:4 * b + 4, :], tiles_of(k, 6 + b), ACT.Copy)
    a.then_inc(*steps.done(names[0]))
    act.wait_ge(*pe_tr)
    act.activation(k.gatedt[:, u, :], k.PS[:, 6, 0:L], ACT.Copy).then_inc(*steps.done(names[1]))


def moe_scalar(k, act, sweep, base):
    gather_scalar(k, act, 0, sweep.pre_act, ("ga", "tr"), sweep.pre_pe.at("ga"), sweep.pre_pe.at("tr"))
    with act.Fori(0, EXPERTS // 2) as i:
        for u in range(2):
            with act.Fori(0, E_TURNS) as j:
                rnd = i * (2 * E_TURNS) + j + u * E_TURNS
                turn_scalar(k, act, sweep.slots, 2, [rnd + b for b in base], SLOTS, k.sgm)
            gather_scalar(k, act, 1 - u, sweep.act, (f"ga{u}", f"tr{u}"), sweep.pe.at(f"ga{u}", i),
                          sweep.pe.at(f"tr{u}", i))


def choice_vector(k, dve, u, src, first):
    nc = k.nc
    nc.vector.tensor_copy(k.chosen_route.rearrange("p a b -> p (a b)").unsqueeze(2), src)
    dve.drain()
    if first:
        nc.vector.tensor_scalar(k.chosen_route[:, 0, :], k.chosen_route[:, 0, :], -float(first), None, ALU.add)
        dve.drain()
    for tile in range(2):
        pos, gate = k.chosen_route[:, 0, tile:tile + 1], k.chosen_route[:, 1, tile:tile + 1]
        nc.vector.tensor_scalar(k.ge_[:, u, tile, :], k.slot_iota, pos, None, ALU.is_equal)
        nc.vector.tensor_scalar(k.gated[:, u, tile, :], k.slot_iota, pos, gate, ALU.is_equal, ALU.mult)
    return dve.drain()


def moe_vector(k, dve, sweep, base, first):
    nc, S, T = k.nc, sweep.dve, sweep.pe
    route = k.route.rearrange("p a t e -> p (a t) e")
    choice_vector(k, dve, 0, route[:, :, 0:1], first).then_inc(*sweep.pre_dve.done("g"))
    with dve.Fori(0, EXPERTS // 2) as i:
        for u in range(2):
            choice_vector(k, dve, 1 - u, route[:, :, ds(i * 2 + (u + 1), 1)], first).then_inc(*S.done(f"g{u}"))
            with dve.Fori(0, E_TURNS) as j:
                rnd = i * (2 * E_TURNS) + j + u * E_TURNS
                turn_vector(k, dve, sweep.slots, 2, [rnd + b for b in base], SLOTS, k.sgm, k.hidm,
                            lambda f: sweep.slots[1].pe.at(f"down{f}", rnd + (base[1] - 1)))
            dve.wait_ge(*T.at(f"acc{u}", i))
            nc.vector.tensor_copy(k.ye[:, u, :], bank_rows(k, 2 * u)).then_inc(*S.done(f"y{u}"))
            for tile in range(2):
                dve.wait_ge(*T.at(f"sc{tile}{u}", i))
                nc.vector.tensor_tensor(k.X[:, tile, :], k.X[:, tile, :], bank_rows(k, 6), ALU.add
                                        ).then_inc(*S.done(f"x{tile}{u}"))


def with_more(k, eng):
    return eng.If(eng.value_load(k.flag[0:1, :].bitcast(I32), min_val=0, max_val=L) > SLOTS)



DECLARE = (declare_pre, declare_xt, declare_norms, declare_ffn, declare_gates, declare_gdn, declare_da,
           declare_attn, declare_rw, declare_mla, declare_fox, declare_moe)
MOE_BASE = (4 * (TURNS + 1), 4 * TURNS)
DA_LOADS, RW_LOADS, FOX_LOADS, MOBA_LOADS = 32, 56, 68, 80


def out_w_sync(k, sp, w, free):
    sp.wait_ge(*free)
    sp.dma_start(k.WO[:, :, :], feature_rows(w)).then_inc(k.d["out_w"], 16)


def sync_program(k, sp):
    t = k.t

    def dense(m, wg, wu, wd, out_rnd):
        ffn_sync(k, sp, wg, wu, wd, m, k.out_pe.at("y3", out_rnd))

    def after_dense(m):
        return k.dense[1].pe.at("down1", m * TURNS + TURNS - 1)

    def first_block(layer):
        return t["ffn_w_gate"][layer], t["ffn_w_up"][layer], t["ffn_w_down"][layer]

    pre_sync(k, sp)
    out_w_sync(k, sp, t["dn_w_out"][0], k.ada_pe.at("half1", 11))
    gdn_sync(k, sp)
    dense(0, *first_block(0), 0)
    dense(1, *first_block(0), 0)
    out_w_sync(k, sp, t["da_w_out"][0], after_dense(1))
    sp.wait_ge(*k.ln_dve.at("out", 7))
    da_sync(k, sp)
    dense(2, *first_block(1), 1)
    out_w_sync(k, sp, t["w_out_0_2"], after_dense(2))
    sp.wait_ge(*k.ln_dve.at("out", 11))
    sp.wait_ge(*k.xt_pe.at("t7", 4))
    rw_sync(k, sp)
    mla_sync(k, sp, [k.rw_dve.at("out", PAIRS - 1), k.rw_pe.at("var", PAIRS - 1)])
    dense(3, t["ffn_wg_0_2"], t["ffn_wu_0_2"], t["ffn_wd_0_2"], 2)
    out_w_sync(k, sp, t["w_out_1_2"], after_dense(3))
    pair_sync(k, sp, k.fox_pe, "v", 0)
    sp.wait_ge(*k.fox_pe.at("v", PAIRS - 1))
    pair_sync(k, sp, k.moba_pe, "v", MOBA_0)
    sp.wait_ge(*k.out_pe.at("y3", 3))
    moe_sync(k, sp, k.sweeps[0], MOE_BASE)
    sp.wait_ge(*k.rt_dve.at("places"))
    with with_more(k, sp):
        sp.wait_ge(*k.sweeps[0].pe.at("acc1", EXPERTS // 2 - 1))
        moe_sync(k, sp, k.sweeps[1], (0, 0))
    sp.wait_ge(*k.res_dve.at("out", 9))
    sp.dma_start(k.out[0].rearrange("(t p) n -> p t n", p=P), view(k, D, 2, D)).then_inc(k.d["out_store"], 16)
    sp.wait_ge(k.d["out_store"], 16)


def gpsimd_program(k, pool):
    t = k.t

    def norm_rows(waits, layer, part, ctx):
        for w in waits:
            pool.wait_ge(*w)
        g = (2 + 3 * part) * D
        gain, bias = (("ln1_g", "ln1_b"), ("ln2_g", "ln2_b"))[part]
        rows = [k.ada[layer, 0, g:g + D], t[gain][layer], t[bias][layer]]
        for n, ap in enumerate(rows + ([k.ada[layer, 1, g:g + D]] if ctx else [])):
            pool.dma_start(k.WH[:, n, :], ap.partition_broadcast(P)).then_inc(k.d["norm_rows"], 16)

    pre_gpsimd(k, pool)
    gates_gpsimd(k, pool)
    gdn_gpsimd(k, pool)
    norm_rows([k.gdn_pe.at("pz", HEADS - 1)], 0, 0, True)
    norm_rows([k.ln_dve.at("out", 3)], 0, 1, True)
    lam_gpsimd(k, pool)
    norm_rows([k.da_pe.at("pv", HEADS - 1)], 1, 0, False)
    norm_rows([k.ln_dve.at("out", 9)], 1, 1, False)
    rwl_gpsimd(k, pool, [k.ln_dve.at("out", 11)])
    lat_gpsimd(k, pool, [k.rwl_pe.at("p")])
    fg_gpsimd(k, pool, [k.res_dve.at("out", 5)])
    pool.wait_ge(*k.moba_pe.at("v", PAIRS - 1))
    for n, name in enumerate(("final_norm_2", "norm_ffn_1_2")):
        pool.dma_start(k.WH[:, n, :], t[name].partition_broadcast(P)).then_inc(k.d["norm_rows"], 16)
    router_gpsimd(k, pool, [k.res_dve.at("out", 7)])


def from_x(k):
    return lambda tile, kb: k.X[:, tile, kb * P:(kb + 1) * P]


def from_scratch(k):
    return lambda tile, kb: view(k, D * (1 + tile) + kb * P, P)


def tensor_program(k, pe):
    def transposes(rnd, src, tiles, *ready):
        for w in ready:
            pe.wait_ge(*w)
        xt_tensor(k, pe, rnd, src, tiles)

    def ready(rnd):
        pe.wait_ge(*k.xt_act.at("x7", rnd))

    pre_tensor(k, pe)
    pe.wait_ge(k.d["x"], 64)
    transposes(0, from_x(k), range(4), k.adv_act.at("cols"))
    gates_tensor(k, pe)
    gdn_tensor(k, pe)
    out_tensor(k, pe, 0, range(4), [k.gdn_dve.at("out", HEADS - 1)])
    transposes(1, from_x(k), range(4), k.ln_dve.at("out", 3))
    ready(1)
    ffn_tensor(k, pe, 0, 0)
    pe.wait_ge(*k.ln_dve.at("out", 5))
    ffn_tensor(k, pe, L, 1)
    transposes(2, from_x(k), range(4), k.ln_dve.at("out", 7))
    ready(2)
    da_tensor(k, pe, DA_LOADS)
    out_tensor(k, pe, 1, range(2), [k.da_dve.at("out", HEADS - 1)])
    transposes(3, from_x(k), range(2), k.ln_dve.at("out", 9))
    ready(3)
    ffn_tensor(k, pe, 0, 2)
    transposes(4, from_scratch(k), range(2), k.res_dve.at("out", 1))
    ready(4)
    rwl_tensor(k, pe)
    rw_tensor(k, pe, RW_LOADS)
    pe.wait_ge(*k.rw_dve.at("out", PAIRS - 1))
    lat_tensor(k, pe)
    mla_tensor(k, pe, 12)
    out_tensor(k, pe, 2, range(2), [k.mla_act.at("o", PAIRS - 1)])
    transposes(5, from_scratch(k), range(2), k.res_dve.at("out", 3))
    ready(5)
    ffn_tensor(k, pe, 0, 3)
    transposes(6, from_scratch(k), range(2), k.res_dve.at("out", 5))
    ready(6)
    fg_tensor(k, pe)
    fox_tensor(k, pe, FOX_LOADS)
    moba_tensor(k, pe, MOBA_LOADS)
    out_tensor(k, pe, 3, range(2), [k.moba_act.at("o", PAIRS - 1)])
    transposes(7, from_scratch(k), range(2), k.res_dve.at("out", 7))
    ready(7)
    router_tensor(k, pe)
    pe.wait_ge(*k.rt_dve.at("places"))
    moe_tensor(k, pe, k.sweeps[0], MOE_BASE)
    with with_more(k, pe):
        moe_tensor(k, pe, k.sweeps[1], (0, 0))


def scalar_program(k, act):
    def modulated(rnd, layer, part, who):
        xt_scalar(k, act, rnd, [(w * L, lambda kb, w=w: mod_col(k, layer, w, part, 1, kb),
                                 lambda kb, w=w: mod_col(k, layer, w, part, 0, kb)) for w in who])

    def gained(rnd, col):
        xt_scalar(k, act, rnd, [(0, lambda kb: vec_col(k, 1, col + kb), None)])

    pre_scalar(k, act)
    act.wait_ge(*k.adv_dve.at("scales"))
    modulated(0, 0, 0, (0, 1))
    gates_scalar(k, act)
    gdn_scalar(k, act)
    for rnd in range(4):
        ln_scalar(k, act, rnd)
    modulated(1, 0, 1, (0, 1))
    for who in range(2):
        ffn_scalar(k, act, who)
        for rnd in (4 + 2 * who, 5 + 2 * who):
            ln_scalar(k, act, rnd)
    modulated(2, 1, 0, (0, 1))
    lam_scalar(k, act)
    da_scalar(k, act)
    for rnd in (8, 9):
        ln_scalar(k, act, rnd)
    modulated(3, 1, 1, (0,))
    ffn_scalar(k, act, 2)
    for rnd in (10, 11):
        ln_scalar(k, act, rnd)
    for tile in range(2):
        res_scalar(k, act, tile, tile)
    gained(4, V_MIX0)
    rwl_scalar(k, act)
    rw_scalar(k, act)
    act.wait_ge(*k.rw_dve.at("out", PAIRS - 1))
    lat_scalar(k, act)
    mla_scalar(k, act)
    for tile in range(2):
        res_scalar(k, act, 2 + tile, tile)
    gained(5, V_FFN0)
    ffn_scalar(k, act, 3)
    for tile in range(2):
        res_scalar(k, act, 4 + tile, tile)
    gained(6, V_MIX1)
    fg_scalar(k, act)
    fox_scalar(k, act)
    moba_scalar(k, act)
    for tile in range(2):
        res_scalar(k, act, 6 + tile, tile)
    gained(7, V_FFN1)
    router_scalar(k, act)
    moe_scalar(k, act, k.sweeps[0], MOE_BASE)
    act.wait_ge(*k.rt_dve.at("places"))
    with with_more(k, act):
        moe_scalar(k, act, k.sweeps[1], (0, 0))
    for tile in range(2):
        res_scalar(k, act, 8 + tile, tile)


def vector_program(k, dve):
    pre_vector(k, dve)
    gates_vector(k, dve)
    gdn_vector(k, dve)
    dve.wait_ge(k.d["norm_rows"], 64)
    for tile in range(4):
        dve.wait_ge(*k.out_pe.at(f"y{tile}", 0))
        ln_vector(k, dve, tile, tile, 2 * tile, 3 if tile >= 2 else 0)
    for who in range(2):
        ffn_vector(k, dve, who)
        dve.wait_ge(k.d["norm_rows"], 128)
        dve.wait_ge(*k.acc_pe.at("sum", who))
        for tile in range(2):
            ln_vector(k, dve, 4 + 2 * who + tile, 2 * who + tile, 2 * tile, 3 * who)
    lam_vector(k, dve)
    da_vector(k, dve)
    dve.wait_ge(k.d["norm_rows"], 176)
    for tile in range(2):
        dve.wait_ge(*k.out_pe.at(f"y{tile}", 1))
        ln_vector(k, dve, 8 + tile, tile, 2 * tile, 0)
    ffn_vector(k, dve, 2)
    dve.wait_ge(k.d["norm_rows"], 224)
    dve.wait_ge(*k.acc_pe.at("sum", 2))
    for tile in range(2):
        ln_vector(k, dve, 10 + tile, tile, 2 * tile, 0)
    for tile in range(2):
        res_vector(k, dve, tile, tile, None)
    dve.wait_ge(*k.xt_pe.at("t7", 4))
    rwl_vector(k, dve)
    rw_vector(k, dve)
    lat_vector(k, dve)
    mla_vector(k, dve)
    for tile in range(2):
        dve.wait_ge(*k.out_pe.at(f"y{tile}", 2))
        res_vector(k, dve, 2 + tile, tile, 2 * tile)
    ffn_vector(k, dve, 3)
    dve.wait_ge(*k.acc_pe.at("sum", 3))
    for tile in range(2):
        res_vector(k, dve, 4 + tile, tile, 2 * tile)
    fg_vector(k, dve)
    fox_vector(k, dve)
    moba_vector(k, dve)
    for tile in range(2):
        dve.wait_ge(*k.out_pe.at(f"y{tile}", 3))
        res_vector(k, dve, 6 + tile, tile, 2 * tile)
    dve.wait_ge(k.d["norm_rows"], 256)
    dve.drain()
    router_vector(k, dve)
    moe_vector(k, dve, k.sweeps[0], MOE_BASE, 0)
    with with_more(k, dve):
        moe_vector(k, dve, k.sweeps[1], (0, 0), SLOTS)
    dve.drain()
    for tile in range(2):
        res_vector(k, dve, 8 + tile, tile, None, k.WH[:, 0, :])



def program(nc, t, out):
    with ExitStack() as ctx:
        k = Kern()
        setup(k, nc, ctx, t, out)
        for declare in DECLARE:
            declare(k)
        credits = {name: [s for s in k.steps if s.sem_name.endswith(name)] for name in ("_pe", "_act", "_dve")}
        block = ctx.enter_context(nc.Block())

        @block.sync
        def _(sp):
            sync_program(k, sp)

        @block.gpsimd
        def _(pool):
            gpsimd_program(k, pool)

        @block.scalar
        def _(act):
            for s in credits["_act"]:
                s.credit(act)
            scalar_program(k, act)

        @block.vector
        def _(dve):
            for s in credits["_dve"]:
                s.credit(dve)
            vector_program(k, dve)

        @block.tensor
        def _(pe):
            for s in credits["_pe"]:
                s.credit(pe)
            tensor_program(k, pe)



def kernel(**inputs):
    import concourse.bacc as bacc
    from concourse.bass_utils import run_bass_kernel_spmd

    nc = bacc.Bacc("TRN2", target_bir_lowering=False, num_devices=1)
    arrays = {name: np.ascontiguousarray(a) for name, a in inputs.items()}
    arrays.update(constants())
    t = {name: nc.dram_tensor("in_" + name, a.shape, mybir.dt.from_np(a.dtype), kind="ExternalInput").ap()
         for name, a in arrays.items()}
    out = nc.dram_tensor("out", (1, L, D), F32, kind="ExternalOutput").ap()
    program(nc, t, out)
    r = run_bass_kernel_spmd(nc, [{"in_" + name: a for name, a in arrays.items()}], core_ids=[0])
    return r.results[0]["out"]
```
